# Optimizing a Trainium2 kernel written in Bass

```python
import jax, jax.numpy as jnp
from jax import lax
import numpy as np

D_MODEL = 1024
BATCH = 1
SEQ = 256
DEPTH = 2

N_EVEN = (DEPTH + 1) // 2
N_ODD = DEPTH // 2
DEEPNORM_ALPHA = (2 * DEPTH) ** 0.25
DEEPNORM_BETA = (8 * DEPTH) ** -0.25
LN_EPS = 1e-5
RMS_EPS = 1e-6

SWA_HEADS = 8
SWA_KV_HEADS = 2
SWA_HEAD_DIM = 64
SWA_WINDOW = 128
SWA_BLOCK = 128
ROPE_DIM = SWA_HEAD_DIM // 4
ROPE_THETA = 500000.0

DN_HEADS = 4
DN_HEAD_DIM = 128
DN_CONV = 4
DN_CHUNK = 64
DN_QKV = 3 * DN_HEADS * DN_HEAD_DIM

EVEN_SPLITS = (SWA_HEADS * SWA_HEAD_DIM, SWA_KV_HEADS * SWA_HEAD_DIM, SWA_KV_HEADS * SWA_HEAD_DIM,
               DN_HEADS * DN_HEAD_DIM, DN_HEADS * DN_HEAD_DIM, DN_HEADS * DN_HEAD_DIM,
               DN_HEADS * DN_HEAD_DIM, DN_HEADS, DN_HEADS)
EVEN_PROJ = sum(EVEN_SPLITS)
MIX_WIDTH = SWA_HEADS * SWA_HEAD_DIM + DN_HEADS * DN_HEAD_DIM

SSM_D_INNER = 2 * D_MODEL
SSM_HEAD_DIM = 64
SSM_HEADS = SSM_D_INNER // SSM_HEAD_DIM
SSM_GROUPS = 4
SSM_STATE = 128
SSM_CONV = 4
SSM_CHUNK = 128
SSM_CONV_DIM = SSM_D_INNER + 2 * SSM_GROUPS * SSM_STATE
SSM_PROJ = SSM_D_INNER + SSM_CONV_DIM + SSM_HEADS

FFN_DIM = 2816
N_EXPERTS = 8
TOP_K = 2
EXPERT_DIM = 3584

kernel_name = "hybrid_swa_deltanet_mamba2_moe_deepnorm"

def layer_norm(x, g, b):
    xf = x.astype(jnp.float32)
    mu = jnp.mean(xf, axis=-1, keepdims=True)
    var = jnp.mean(jnp.square(xf - mu), axis=-1, keepdims=True)
    return ((xf - mu) * lax.rsqrt(var + LN_EPS) * g + b).astype(x.dtype)

def rms_norm(x, w):
    xf = x.astype(jnp.float32)
    return xf * lax.rsqrt(jnp.mean(jnp.square(xf), axis=-1, keepdims=True) + RMS_EPS) * w

def l2_normalize(x):
    xf = x.astype(jnp.float32)
    return xf * lax.rsqrt(jnp.sum(jnp.square(xf), axis=-1, keepdims=True) + RMS_EPS)

def split_last(a, sizes):
    return jnp.split(a, np.cumsum(sizes)[:-1].tolist(), axis=-1)

def causal_depthwise_conv(x, w):
    K, C = w.shape
    return lax.conv_general_dilated(x, w[:, None, :].astype(x.dtype), window_strides=(1,),
                                    padding=[(K - 1, 0)], dimension_numbers=("NWC", "WIO", "NWC"),
                                    feature_group_count=C)

def partial_rope(x, pos):
    half = ROPE_DIM // 2
    inv_freq = jnp.power(ROPE_THETA, -jnp.arange(half, dtype=jnp.float32) / half)
    ang = pos.astype(jnp.float32)[:, None] * inv_freq[None, :]
    cos = jnp.cos(ang)[None, :, None, :]
    sin = jnp.sin(ang)[None, :, None, :]
    xf = x.astype(jnp.float32)
    x1, x2, rest = xf[..., :half], xf[..., half:ROPE_DIM], xf[..., ROPE_DIM:]
    return jnp.concatenate([x1 * cos - x2 * sin, x2 * cos + x1 * sin, rest], axis=-1).astype(x.dtype)

def sliding_window_sink_attention(q, k, v, sinks):
    Bsz, T, Hq, D = q.shape
    Hkv = k.shape[2]
    G = Hq // Hkv
    Q = SWA_BLOCK
    N = T // Q
    qb = q.reshape(Bsz, N, Q, Hkv, G, D)
    kb = k.reshape(Bsz, N, Q, Hkv, D)
    vb = v.reshape(Bsz, N, Q, Hkv, D)
    prev = lambda a: jnp.concatenate([jnp.zeros_like(a[:, :1]), a[:, :-1]], axis=1)
    kw = jnp.concatenate([prev(kb), kb], axis=2)
    vw = jnp.concatenate([prev(vb), vb], axis=2)
    s = jnp.einsum("bnqhgd,bnkhd->bnhgqk", qb, kw, preferred_element_type=jnp.float32) * (D ** -0.5)
    qi = jnp.arange(Q)[:, None] + Q
    kj = jnp.arange(2 * Q)[None, :]
    band = (kj <= qi) & (qi - kj < SWA_WINDOW)
    has_prev = (jnp.arange(N) > 0)[:, None, None] | (kj >= Q)[None]
    valid = band[None] & has_prev
    s = jnp.where(valid[None, :, None, None], s, -jnp.inf)
    sink = sinks.astype(jnp.float32).reshape(Hkv, G)[None, None, :, :, None, None]
    s_all = jnp.concatenate([s, jnp.broadcast_to(sink, s.shape[:-1] + (1,))], axis=-1)
    p = jax.nn.softmax(s_all, axis=-1)[..., :-1]
    o = jnp.einsum("bnhgqk,bnkhd->bnqhgd", p.astype(v.dtype), vw)
    return o.reshape(Bsz, T, Hq * D)

def gated_delta_rule(q, k, v, g, beta):
    Bsz, T, H, Dk = q.shape
    Dv = v.shape[-1]
    C = DN_CHUNK
    N = T // C
    f32 = jnp.float32

    def chunks(a):
        a = a.astype(f32).reshape((Bsz, N, C, H) + a.shape[3:])
        return jnp.moveaxis(a, 3, 1)

    q = chunks(q) * (Dk ** -0.5)
    k, v, g, beta = chunks(k), chunks(v), chunks(g), chunks(beta)
    gc = jnp.cumsum(g, axis=-1)
    causal = jnp.tril(jnp.ones((C, C), bool))
    strict = jnp.tril(jnp.ones((C, C), bool), -1)
    decay = jnp.exp(jnp.where(causal, gc[..., :, None] - gc[..., None, :], -jnp.inf))
    kb = k * beta[..., None]
    a_lower = jnp.where(strict, jnp.einsum("bhncd,bhnsd->bhncs", kb, k) * decay, 0.0)
    rhs = jnp.concatenate([v * beta[..., None], kb * jnp.exp(gc)[..., None]], axis=-1)
    sol = lax.linalg.triangular_solve(a_lower + jnp.eye(C, dtype=f32), rhs, left_side=True,
                                      lower=True, unit_diagonal=True)
    u, w = sol[..., :Dv], sol[..., Dv:]
    attn = jnp.einsum("bhncd,bhnsd->bhncs", q, k) * decay
    q_dec = q * jnp.exp(gc)[..., None]
    k_dec = k * jnp.exp(gc[..., -1:] - gc)[..., None]
    g_last = jnp.exp(gc[..., -1])

    def step(S, inp):
        qd, kd, uc, wc, ac, gl = inp
        v_new = uc - jnp.einsum("bhck,bhkv->bhcv", wc, S)
        o = jnp.einsum("bhck,bhkv->bhcv", qd, S) + jnp.einsum("bhcs,bhsv->bhcv", ac, v_new)
        S = S * gl[..., None, None] + jnp.einsum("bhck,bhcv->bhkv", kd, v_new)
        return S, o

    lead = lambda a: jnp.moveaxis(a, 2, 0)
    S0 = jnp.zeros((Bsz, H, Dk, Dv), f32)
    _, o = lax.scan(step, S0, (lead(q_dec), lead(k_dec), lead(u), lead(w), lead(attn), lead(g_last)))
    return jnp.transpose(o, (1, 0, 3, 2, 4)).reshape(Bsz, T, H, Dv)

def ssd_chunked(x, dt, a, bmat, cmat):
    Bsz, T, H, P = x.shape
    G, Ns = bmat.shape[2], bmat.shape[3]
    R = H // G
    L = SSM_CHUNK
    Nc = T // L
    f32 = jnp.float32
    xdt = (x.astype(f32) * dt[..., None]).reshape(Bsz, Nc, L, G, R, P)
    dA = (dt * a).reshape(Bsz, Nc, L, G, R).transpose(0, 1, 3, 4, 2)
    acs = jnp.cumsum(dA, axis=-1)
    bc = bmat.astype(f32).reshape(Bsz, Nc, L, G, Ns)
    cc = cmat.astype(f32).reshape(Bsz, Nc, L, G, Ns)
    causal = jnp.tril(jnp.ones((L, L), bool))
    seg = jnp.exp(jnp.where(causal, acs[..., :, None] - acs[..., None, :], -jnp.inf))
    cb = jnp.einsum("bclgn,bcsgn->bcgls", cc, bc)
    y_diag = jnp.einsum("bcgrls,bcsgrp->bclgrp", cb[:, :, :, None] * seg, xdt)
    decay_states = jnp.exp(acs[..., -1:] - acs)
    states = jnp.einsum("bclgn,bcgrl,bclgrp->bcgrpn", bc, decay_states, xdt)
    chunk_decay = jnp.exp(acs[..., -1])

    def step(h, inp):
        st, dec = inp
        return h * dec[..., None, None] + st, h

    h0 = jnp.zeros((Bsz, G, R, P, Ns), f32)
    _, h_in = lax.scan(step, h0, (jnp.moveaxis(states, 1, 0), jnp.moveaxis(chunk_decay, 1, 0)))
    h_in = jnp.moveaxis(h_in, 0, 1)
    y_off = jnp.einsum("bclgn,bcgrpn,bcgrl->bclgrp", cc, h_in, jnp.exp(acs))
    return (y_diag + y_off).reshape(Bsz, T, H, P)

def attn_deltanet_mixer(x, pos, w_in, sinks, conv_w, a_log, dt_bias, norm_w, w_out):
    Bsz, T, _ = x.shape
    f32 = jnp.float32
    aq, ak, av, bq, bk, bv, bgate, bbeta, ba = split_last(x @ w_in, EVEN_SPLITS)
    q = partial_rope(aq.reshape(Bsz, T, SWA_HEADS, SWA_HEAD_DIM), pos)
    k = partial_rope(ak.reshape(Bsz, T, SWA_KV_HEADS, SWA_HEAD_DIM), pos)
    v = av.reshape(Bsz, T, SWA_KV_HEADS, SWA_HEAD_DIM)
    out_a = sliding_window_sink_attention(q, k, v, sinks)
    qkv = jax.nn.silu(causal_depthwise_conv(jnp.concatenate([bq, bk, bv], axis=-1), conv_w))
    dq, dk, dv = jnp.split(qkv, 3, axis=-1)
    shp = (Bsz, T, DN_HEADS, DN_HEAD_DIM)
    beta = jax.nn.sigmoid(bbeta.astype(f32))
    g = -jnp.exp(a_log.astype(f32)) * jax.nn.softplus(ba.astype(f32) + dt_bias)
    o = gated_delta_rule(l2_normalize(dq.reshape(shp)), l2_normalize(dk.reshape(shp)), dv.reshape(shp), g, beta)
    o = rms_norm(o, norm_w) * jax.nn.silu(bgate.reshape(shp).astype(f32))
    out_b = o.reshape(Bsz, T, DN_HEADS * DN_HEAD_DIM).astype(x.dtype)
    return jnp.concatenate([out_a, out_b], axis=-1) @ w_out

def mamba2_mixer(x, w_in, conv_w, conv_b, dt_bias, a_log, d_skip, norm_w, w_out):
    Bsz, T, _ = x.shape
    f32 = jnp.float32
    z, xbc, dt = split_last(x @ w_in, (SSM_D_INNER, SSM_CONV_DIM, SSM_HEADS))
    xbc = jax.nn.silu(causal_depthwise_conv(xbc, conv_w) + conv_b)
    xs, bmat, cmat = split_last(xbc, (SSM_D_INNER, SSM_GROUPS * SSM_STATE, SSM_GROUPS * SSM_STATE))
    xs = xs.reshape(Bsz, T, SSM_HEADS, SSM_HEAD_DIM)
    dt = jax.nn.softplus(dt.astype(f32) + dt_bias)
    y = ssd_chunked(xs, dt, -jnp.exp(a_log.astype(f32)),
                    bmat.reshape(Bsz, T, SSM_GROUPS, SSM_STATE), cmat.reshape(Bsz, T, SSM_GROUPS, SSM_STATE))
    y = y + d_skip.astype(f32)[:, None] * xs.astype(f32)
    y = y.reshape(Bsz, T, SSM_D_INNER) * jax.nn.silu(z.astype(f32))
    y = rms_norm(y.reshape(Bsz, T, SSM_GROUPS, -1), norm_w.reshape(SSM_GROUPS, -1)).reshape(Bsz, T, SSM_D_INNER)
    return y.astype(x.dtype) @ w_out

def swiglu(x, w_gate, w_up, w_down):
    return (jax.nn.silu(x @ w_gate) * (x @ w_up)) @ w_down

def moe_swiglu(x, w_router, b_router, w_gate, w_up, w_down):
    Bsz, T, D = x.shape
    xt = x.reshape(-1, D)
    logits = (xt @ w_router).astype(jnp.float32) + b_router.astype(jnp.float32)
    top_val, top_idx = lax.top_k(logits, TOP_K)
    gates = jax.nn.softmax(top_val, axis=-1)
    combine = jnp.sum(jax.nn.one_hot(top_idx, N_EXPERTS, dtype=jnp.float32) * gates[..., None], axis=1)
    out = jnp.zeros(xt.shape, jnp.float32)
    for e in range(N_EXPERTS):
        out = out + combine[:, e:e + 1] * swiglu(xt, w_gate[e], w_up[e], w_down[e]).astype(jnp.float32)
    return out.reshape(Bsz, T, D).astype(x.dtype)

def setup_inputs(seed: int = 0) -> dict:
    key = jax.random.key(seed)
    ks = jax.random.split(key, 32)
    f32 = jnp.float32
    nrm = lambda i, shape, scale: jax.random.normal(ks[i], shape, f32) * scale

    def dt_bias_init(i, shape):
        dt = jnp.exp(jax.random.uniform(ks[i], shape, f32, np.log(1e-3), np.log(1e-1)))
        return dt + jnp.log(-jnp.expm1(-dt))

    def a_log_init(i, shape):
        return jnp.log(jax.random.uniform(ks[i], shape, f32, 1.0, 16.0))

    b = DEEPNORM_BETA
    return {
        "x": nrm(0, (BATCH, SEQ, D_MODEL), 1.0),
        "ln_g": 1.0 + nrm(1, (DEPTH, 2, D_MODEL), 0.02),
        "ln_b": nrm(2, (DEPTH, 2, D_MODEL), 0.02),
        "even_w_in": nrm(3, (N_EVEN, D_MODEL, EVEN_PROJ), D_MODEL ** -0.5),
        "swa_sinks": nrm(4, (N_EVEN, SWA_HEADS), 1.0),
        "dn_conv_w": nrm(5, (N_EVEN, DN_CONV, DN_QKV), DN_CONV ** -0.5),
        "dn_a_log": a_log_init(6, (N_EVEN, DN_HEADS)),
        "dn_dt_bias": dt_bias_init(7, (N_EVEN, DN_HEADS)),
        "dn_norm_w": 1.0 + nrm(8, (N_EVEN, DN_HEAD_DIM), 0.02),
        "even_w_out": nrm(9, (N_EVEN, MIX_WIDTH, D_MODEL), b * MIX_WIDTH ** -0.5),
        "ssm_w_in": nrm(10, (N_ODD, D_MODEL, SSM_PROJ), D_MODEL ** -0.5),
        "ssm_conv_w": nrm(11, (N_ODD, SSM_CONV, SSM_CONV_DIM), SSM_CONV ** -0.5),
        "ssm_conv_b": nrm(12, (N_ODD, SSM_CONV_DIM), 0.02),
        "ssm_dt_bias": dt_bias_init(13, (N_ODD, SSM_HEADS)),
        "ssm_a_log": a_log_init(14, (N_ODD, SSM_HEADS)),
        "ssm_d": 1.0 + nrm(15, (N_ODD, SSM_HEADS), 0.02),
        "ssm_norm_w": 1.0 + nrm(16, (N_ODD, SSM_D_INNER), 0.02),
        "ssm_w_out": nrm(17, (N_ODD, SSM_D_INNER, D_MODEL), b * SSM_D_INNER ** -0.5),
        "ffn_w_gate": nrm(18, (N_EVEN, D_MODEL, FFN_DIM), D_MODEL ** -0.5),
        "ffn_w_up": nrm(19, (N_EVEN, D_MODEL, FFN_DIM), D_MODEL ** -0.5),
        "ffn_w_down": nrm(20, (N_EVEN, FFN_DIM, D_MODEL), b * FFN_DIM ** -0.5),
        "moe_w_router": nrm(21, (N_ODD, D_MODEL, N_EXPERTS), D_MODEL ** -0.5),
        "moe_b_router": nrm(22, (N_ODD, N_EXPERTS), 0.01),
        "moe_w_gate": nrm(23, (N_ODD, N_EXPERTS, D_MODEL, EXPERT_DIM), D_MODEL ** -0.5),
        "moe_w_up": nrm(24, (N_ODD, N_EXPERTS, D_MODEL, EXPERT_DIM), D_MODEL ** -0.5),
        "moe_w_down": nrm(25, (N_ODD, N_EXPERTS, EXPERT_DIM, D_MODEL), b * EXPERT_DIM ** -0.5),
    }

def reference(x, ln_g, ln_b, even_w_in, swa_sinks, dn_conv_w, dn_a_log, dn_dt_bias, dn_norm_w,
              even_w_out, ssm_w_in, ssm_conv_w, ssm_conv_b, ssm_dt_bias, ssm_a_log, ssm_d,
              ssm_norm_w, ssm_w_out, ffn_w_gate, ffn_w_up, ffn_w_down, moe_w_router, moe_b_router,
              moe_w_gate, moe_w_up, moe_w_down):
    pos = jnp.arange(x.shape[1], dtype=jnp.int32)
    for i in range(DEPTH):
        j = i // 2
        if i % 2 == 0:
            mix = attn_deltanet_mixer(x, pos, even_w_in[j], swa_sinks[j], dn_conv_w[j], dn_a_log[j],
                                      dn_dt_bias[j], dn_norm_w[j], even_w_out[j])
        else:
            mix = mamba2_mixer(x, ssm_w_in[j], ssm_conv_w[j], ssm_conv_b[j], ssm_dt_bias[j],
                               ssm_a_log[j], ssm_d[j], ssm_norm_w[j], ssm_w_out[j])
        x = layer_norm(DEEPNORM_ALPHA * x + mix, ln_g[i, 0], ln_b[i, 0])
        if i % 2 == 0:
            ffn = swiglu(x, ffn_w_gate[j], ffn_w_up[j], ffn_w_down[j])
        else:
            ffn = moe_swiglu(x, moe_w_router[j], moe_b_router[j], moe_w_gate[j], moe_w_up[j], moe_w_down[j])
        x = layer_norm(DEEPNORM_ALPHA * x + ffn, ln_g[i, 1], ln_b[i, 1])
    return x


_drawn_inputs = setup_inputs


def setup_inputs(seed=0):
    import zlib

    import numpy as np

    out = dict(_drawn_inputs(seed))
    spreads = {}
    factors = {'swa_sinks': 8.0,
     'dn_norm_w': 5.644,
     'ssm_conv_b': 4.17,
     'ssm_d': 7.348,
     'ssm_norm_w': 5.119,
     'moe_b_router': 3.463}
    for name, (base, spread) in spreads.items():
        noise = np.random.default_rng([zlib.crc32(name.encode()), seed]).standard_normal(out[name].shape)
        drawn = base * np.exp(spread * noise) if base else spread * noise
        out[name] = __import__('jax').numpy.asarray(drawn.astype(out[name].dtype))
    for name, factor in factors.items():
        out[name] = (out[name] * factor).astype(out[name].dtype)
    return out
```

```python
from contextlib import ExitStack

import numpy as np

import concourse.bass as bass
from concourse import mybir

ALU = mybir.AluOpType
ACT = mybir.ActivationFunctionType
F32 = mybir.dt.float32
BF16 = mybir.dt.bfloat16
F32R = mybir.dt.float32r
I32 = mybir.dt.int32
U32 = mybir.dt.uint32
AX = mybir.AxisListType.X

P = 128
SEQ = 256
TT = SEQ // P
D = 1024
KD = D // P
DEPTH = 2
ALPHA = (2 * DEPTH) ** 0.25
LN_EPS, RMS_EPS = 1e-5, 1e-6
AH, AKV, AD = 8, 2, 64
ROPE = AD // 4
HALF = ROPE // 2
THETA = 500000.0
DH, DD = 4, 128
CONV = 4
NDN = 3 * DH
LEVELS = 7
Q0, K0 = 0, AH * AD
B0 = K0 + 2 * AKV * AD
G0 = B0 + NDN * P
BA0 = G0 + DH * DD
SI = 2048
SH, SD, SG, SN = 32, 64, 4, 128
NX = SI // P
NXBC = NX + 2 * SG
F = 2816
FW = 256
FSTEPS = F // FW
E = 8
EF = 3584
EW = 512
ESTEPS = EF // EW
NEG = -1e30

FIRST = 1

SLOT = 4096
RING = 4
PIECE = 2048
RAW = 7
CUT = 3
PPU = 2
PPE = 3 * ESTEPS * PPU
assert PPE % RAW == 0 and PPE % CUT == 0
ORDER = [(0, 0), (0, 1)]
for _j in range(1, ESTEPS):
    ORDER += [(_j, 0), (_j, 1), (_j - 1, 2)]
ORDER += [(ESTEPS - 1, 2)]


def last_piece(step, what):
    return PPU * ORDER.index((step, what)) + PPU - 1



C_ID, C_TRI, C_TRIS = 0, P, 2 * P
C_LVL = 3 * P
C_AM = C_LVL + LEVELS * P
C_COS = C_AM + 2 * P
C_SIN = C_COS + TT * HALF
C_IOTA = C_SIN + TT * HALF
C_I8 = C_IOTA + P
C_W = C_I8 + E


def shape_constants():
    c = np.zeros((P, C_W), np.float32)
    r = np.arange(P)
    c[:, C_ID:C_ID + P] = np.eye(P)
    c[:, C_TRI:C_TRI + P] = r[:, None] <= r[None, :]
    c[:, C_TRIS:C_TRIS + P] = r[:, None] < r[None, :]
    for lv in range(LEVELS):
        b = 1 << lv
        same = (r[:, None] // (2 * b)) == (r[None, :] // (2 * b))
        c[:, C_LVL + lv * P:C_LVL + (lv + 1) * P] = same & ((r[None, :] // b) % 2 == 1) & ((r[:, None] // b) % 2 == 0)
    c[:, C_AM:C_AM + P] = np.where(r[None, :] > r[:, None], 0, NEG)
    c[:, C_AM + P:C_AM + 2 * P] = np.where(r[None, :] <= r[:, None], 0, NEG)
    inv = THETA ** (-np.arange(HALF, dtype=np.float64) / HALF)
    for t in range(TT):
        ang = (r[:, None] + t * P) * inv[None, :]
        c[:, C_COS + t * HALF:C_COS + (t + 1) * HALF] = np.cos(ang)
        c[:, C_SIN + t * HALF:C_SIN + (t + 1) * HALF] = np.sin(ang)
    c[:, C_IOTA:C_IOTA + P] = r[None, :]
    c[:, C_I8:C_I8 + E] = np.arange(E)[None, :]
    return c


def shape_constants_b(dtype):
    r = np.arange(P)
    return np.concatenate([np.eye(P), np.where(r[:, None] <= r[None, :], 0, NEG)], axis=1).astype(dtype)


def build(nc, dram, out, limit=99):
    with ExitStack() as ctx:
        def sb(name, shape, dt=F32):
            return ctx.enter_context(nc.sbuf_tensor(name, [P] + shape, dt))

        sems = {}

        def sem(name):
            if name not in sems:
                sems[name] = ctx.enter_context(nc.semaphore(name))
            return sems[name]

        ps = ctx.enter_context(nc.psum_tensor("ps", [P, 8, 512], F32))

        const = sb("const", [C_W])
        identb = sb("identb", [P], BF16)
        maskb = sb("maskb", [P], BF16)
        zerob = sb("zerob", [512], BF16)
        ones = sb("ones", [P])
        x_tok = sb("x_tok", [TT, D])
        xT = sb("xT", [KD, SEQ])
        ln_gb = sb("ln_gb", [2, D])
        prow_a = sb("prow_a", [P])
        prow_b = sb("prow_b", [P])
        pcol = sb("pcol", [2 * P])
        w_ba = sb("w_ba", [KD, 2 * DH])
        w_dt = sb("w_dt", [KD, SH])
        w_rt = sb("w_rt", [KD, E])
        sinks = sb("sinks", [AH])
        dn_al = sb("dn_al", [DH])
        dn_dtb = sb("dn_dtb", [DH])
        dn_nw = sb("dn_nw", [DD])
        ssm_al = sb("ssm_al", [SH])
        ssm_dtb = sb("ssm_dtb", [SH])
        ssm_db = sb("ssm_db", [SH])
        dcol = sb("dcol", [NX])
        brt = sb("brt", [E])
        stats = sb("stats", [TT, 2, 6])
        mv = sb("mv", [TT, 2])
        rstd = sb("rstd", [TT])
        nhalf = sb("nhalf", [TT])
        eps_rms = sb("eps_rms", [1])
        with ExitStack() as early:
            ring = early.enter_context(nc.sbuf_tensor("ring", [P, RING * SLOT], F32))
            arena = early.enter_context(nc.sbuf_tensor("arena", [P, 27200], F32))
        raw = sb("raw", [RAW, PIECE])
        w_hi = sb("w_hi", [CUT, PIECE], F32R)
        w_lo = sb("w_lo", [CUT, PIECE], F32R)
        xg_hi = sb("xg_hi", [KD, P], F32R)
        xg_lo = sb("xg_lo", [KD, P], F32R)
        ehT_hi = sb("ehT_hi", [2, 4, P], F32R)
        ehT_lo = sb("ehT_lo", [2, 4, P], F32R)
        esg = sb("esg", [2, EW])
        eh = sb("eh", [2, EW])
        sel_rows = sb("sel_rows", [TT, P])
        sel_gate = sb("sel_gate", [TT, P])
        G = sb("G", [TT, P])
        oe = sb("oe", [D])
        yacc = sb("yacc", [TT, D])
        lg = sb("lg", [TT, E])
        top8 = sb("top8", [TT, 8])
        idx8 = sb("idx8", [TT, 8])
        idxf = sb("idxf", [TT, 2])
        oh1 = sb("oh1", [TT, E])
        oh2 = sb("oh2", [TT, E])
        dm = sb("dm", [TT, 1])
        g1 = sb("g1", [TT, 1])
        g2 = sb("g2", [TT, 1])
        comb = sb("comb", [TT, E])
        sel = sb("sel", [TT, E])
        rank = sb("rank", [TT, E])
        rank2 = sb("rank2", [TT, E])
        cnt = sb("cnt", [1])
        over = sb("over", [1])

        ident = const[:, C_ID:C_ID + P]
        tri = const[:, C_TRI:C_TRI + P]
        tris = const[:, C_TRIS:C_TRIS + P]
        iota = const[:, C_IOTA:C_IOTA + P]
        iota8 = const[:, C_I8:C_I8 + E]

        def ssm_tap(k, j):
            return pcol[:, k * NXBC + j:k * NXBC + j + 1]

        def dn_tap(k, j):
            return pcol[:, P + k * NDN + j:P + k * NDN + j + 1]

        def ssm_nw(j):
            return pcol[:, P + CONV * NDN + j:P + CONV * NDN + j + 1]

        def ssm_cb(j):
            return pcol[:, P + CONV * NDN + NX + j:P + CONV * NDN + NX + j + 1]

        top = [0]

        def take(*shape, at=None):
            n = int(np.prod(shape))
            if at is not None:
                top[0] = at
            a = arena[:, top[0]:top[0] + n]
            top[0] += n
            assert top[0] <= 27200, top[0]
            if len(shape) == 2:
                a = a.rearrange("p (a b) -> p a b", b=shape[1])
            if len(shape) == 3:
                a = a.rearrange("p (a b c) -> p a b c", b=shape[1], c=shape[2])
            return a

        dnT = take(NDN, SEQ, at=0)
        qkv = take(TT, 768)
        gate = take(TT, DH * DD)
        mixT = take(KD, SEQ)
        rt = take(4, TT * 10 * HALF)
        ba = take(TT, 2 * DH)
        beta = take(TT, DH)
        gdn = take(TT, DH)
        zdn = take(TT, DH)
        adn = take(TT, DH)
        e2dn = take(TT, DH)
        ebdn = take(TT, DH)
        eadn = take(DH)
        mx = take(2, AH)
        nmx = take(2, AH)
        sdx = take(2, AH)
        den = take(2, AH)
        rden = take(2, AH)
        ngc = take(TT, DH)
        ddk = take(DH)
        dke = take(DH)
        egc1 = take(DH)
        bege = take(DH)
        oss = take(TT * DH)
        orn = take(TT * DH)
        base_dn = top[0]
        qT = take(4, SEQ)
        kT = take(SEQ)
        s = take(AH, 384)
        pT = take(3 * AH, P)
        sq = take(2048, at=base_dn)
        rn = take(2048)
        decT = take(8, P)
        attnT = take(8, P)
        AT = take(8, P)
        LT = take(8, P)
        X = take(8, P)
        XT = take(8, P)
        Pm = take(8, P)
        vb = take(8, P)
        kdec = take(4, P)
        kbe = take(4, P)
        u = take(8, P, at=base_dn)
        wT = take(4, P)
        S1 = take(4, P)
        vnew = take(4, P)
        o = take(8, P, at=base_dn + 4096 + 3072)
        osq = take(8, P)

        sg = take(2, 512, at=0)
        hT = take(2, 2, SEQ)

        xbcT = take(NXBC, SEQ, at=0)
        zT = take(NX, SEQ)
        xdt = take(TT, SI)
        xdec = take(SI)
        Btok = take(SG * SN)
        state = take(SI)
        seg = take(2, 8, P)
        MT = take(2, 8, P)
        cb = take(8, P)
        er = take(2, 512)
        yo = take(2, 512)
        ysq = MT.rearrange("p a b c -> p a (b c)")
        yrn = seg[:, 0].rearrange("p a b -> p (a b)").rearrange("p (g t) -> p g t", g=SG)
        sz = take(TT, SH)
        sdt = take(TT, SH)
        saz = take(TT, SH)
        se2 = take(TT, SH)
        dA = take(TT, SH)
        sea = take(SH)
        nacs = take(TT, SH)
        sdd = take(SH)
        sdec = take(SH)

        def bc(ap, n):
            return ap.unsqueeze(2).to_broadcast([P, ap.shape[1], n])

        def over_heads(ap, n):
            return ap.unsqueeze(1).to_broadcast([P, n, ap.shape[1]])

        def slot(i):
            return ring[:, i * SLOT:(i + 1) * SLOT]

        w_in0, w_out0 = dram["even_w_in"][0], dram["even_w_out"][0]
        w_in1, w_out1 = dram["ssm_w_in"][0], dram["ssm_w_out"][0]

        def cols(w, a, n):
            return w.rearrange("(k p) n -> p k n", p=P)[:, :, a:a + n]

        def rows(w, a, n):
            return w.rearrange("(k p) n -> p k n", p=P)[:, a:a + n, :]

        units0 = [(cols(w_in0, B0 + 512 * i, 512), 512) for i in range(3)]
        units0 += [(cols(w_in0, G0, 512), 512), (cols(w_in0, Q0, 512), 512), (cols(w_in0, K0, 256), 256)]
        units0 += [(rows(w_out0, 4 * i, 4), D) for i in range(2)]
        NU0 = len(units0)
        NUF = 2 * FSTEPS
        units1 = [(cols(w_in1, SI + 512 * i, 512), 512) for i in range(6)]
        units1 += [(cols(w_in1, 512 * i, 512), 512) for i in range(4)]
        units1 += [(rows(w_out1, 4 * i, 4), D) for i in range(4)]
        NU1 = len(units1)
        BASE1 = NU0 + NUF
        assert NU0 % RING == 0
        loaded = [sem(f"slot{i}_loaded") for i in range(RING)]
        raw_loaded = [sem(f"raw{i}_loaded") for i in range(RAW)]
        lo_made = sem("lo_made")
        piece_used = sem("piece_used")

        block = ctx.enter_context(nc.Block())

        @block.sync
        def _(sp):
            sp.dma_start(x_tok[:, :, :], dram["x"][0].rearrange("(t p) d -> p t d", p=P)).then_inc(sem("x_loaded"), 16)
            sp.dma_start(const[:, :], dram["shape_consts"]).then_inc(sem("x_loaded"), 16)

            def fill(dst, src, s_):
                k = src.shape[1] // 2
                sp.dma_start(dst[:, 0:k, :], src[:, 0:k, :]).then_inc(s_, 16)
                sp.dma_start(dst[:, k:2 * k, :], src[:, k:2 * k, :]).then_inc(s_, 16)

            done0 = [("dn_proj", 2), ("dn_proj", 4), ("dn_proj", 6), ("gate_proj", 2), ("q_proj", 2), ("kv_proj", 2),
                     ("out_proj", 1), ("out_proj", 2)]
            done1 = [("xbc_proj", 2 * i + 2) for i in range(6)] + [("z_proj", 2 * i + 2) for i in range(4)]
            done1 += [("out_proj", 2 + i + 1) for i in range(4)]
            done_ffn = [("ffn_down", FSTEPS - 1 + FIRST), ("ffn_gu", FSTEPS + FIRST), ("ffn_down", FSTEPS + FIRST),
                        ("ffn_down", FSTEPS + 1 + FIRST)]

            def unit(n, src, width, before):
                if before:
                    sp.wait_ge(sem(before[0]), before[1])
                k = src.shape[1]
                dst = slot(n % RING)[:, 0:k * width].rearrange("p (k n) -> p k n", k=k)
                fill(dst, src, loaded[n % RING])

            for n, (src, width) in enumerate(units0):
                unit(n, src, width, done0[n - RING] if n >= RING else None)
            if limit < 2:
                return
            wg, wu, wd = dram["ffn_w_gate"][0], dram["ffn_w_up"][0], dram["ffn_w_down"][0]
            gu_dst = [slot(i)[:, :].rearrange("p (w k n) -> p w k n", w=2, k=KD) for i in range(RING)]
            d_dst = [slot(i)[:, 0:2 * D].rearrange("p (k n) -> p k n", k=2) for i in range(RING)]

            def ffn_gu(i, step):
                for w_, src in enumerate((wg, wu)):
                    sp.dma_start(gu_dst[i][:, w_], src.rearrange("(k p) n -> p k n", p=P)[:, :, bass.ds(step * FW, FW)]
                                 ).then_inc(loaded[i], 16)

            def ffn_d(i, step):
                src = wd.rearrange("(s k p) n -> s p k n", k=2, p=P)[step]
                sp.dma_start(d_dst[i][:, 0:1], src[:, 0:1]).then_inc(loaded[i], 16)
                sp.dma_start(d_dst[i][:, 1:2], src[:, 1:2]).then_inc(loaded[i], 16)

            sp.wait_ge(sem("q_proj"), 2)
            ffn_gu(0, 0)
            sp.wait_ge(sem("kv_proj"), 2)
            sp.wait_ge(sem("out_proj"), 2)
            with sp.Fori(0, FSTEPS // 2) as i:
                sp.wait_ge(sem("ffn_gu"), 2 * i + FIRST)
                ffn_gu(1, 2 * i + 1)
                sp.wait_ge(sem("ffn_down"), 2 * i + FIRST)
                ffn_d(2, 2 * i)
                sp.wait_ge(sem("ffn_gu"), 2 * i + 1 + FIRST)
                ffn_gu(3, 2 * i + 2)
                sp.wait_ge(sem("ffn_down"), 2 * i + 1 + FIRST)
                ffn_d(0, 2 * i + 1)
            sp.wait_ge(sem("ffn_gu"), FSTEPS - 1 + FIRST)
            ffn_d(1, FSTEPS - 1)
            if limit < 3:
                return
            for n, (src, width) in enumerate(units1):
                unit(BASE1 + n, src, width, done1[n - RING] if n >= RING else done_ffn[n])
            if limit < 5:
                return

            eg, eu, ed = dram["moe_w_gate"][0], dram["moe_w_up"][0], dram["moe_w_down"][0]
            for i in range(RING):
                sp.wait_ge(sem("out_proj"), 2 + i + 1)
                sp.sem_inc(lo_made, min(2, RAW - 2 * i))

            def expert_loads(e, it):
                for n in range(PPE):
                    (j, what), half = ORDER[n // PPU], n % PPU
                    sp.wait_ge(lo_made, PPE * it + (n + 1))
                    i = n % RAW
                    if what < 2:
                        src = (eg, eu)[what][e].rearrange("(k p) n -> p k n", p=P)[:, 4 * half:4 * half + 4, EW * j:EW * (j + 1)]
                    else:
                        src = ed[e].rearrange("(k p) n -> p k n", p=P)[:, 4 * j + 2 * half:4 * j + 2 * half + 2, :]
                    sp.dma_start(raw[:, i, :].rearrange("p (k n) -> p k n", k=src.shape[1]), src).then_inc(raw_loaded[i], 16)

            with sp.Fori(0, E) as e:
                expert_loads(e, e)
            sp.wait_ge(sem("overflow_known"), 1)
            more = sp.value_load(over[0:1, 0:1].bitcast(I32), min_val=0, max_val=SEQ)
            with sp.If(more > 0):
                with sp.Fori(0, E) as e:
                    expert_loads(e, e + E)

        @block.gpsimd
        def _(pool):
            pool.memset(ones[:, :], 1.0).then_inc(sem("pool_set"), 1)
            pool.memset(zerob[:, :], 0.0).then_inc(sem("pool_set"), 1)
            pool.memset(nhalf[:, :], -0.5).then_inc(sem("pool_set"), 1)
            pool.wait_ge(sem("pool_set"), 3)
            for n in range(2 * DEPTH):
                if n >= limit:
                    break
                pool.wait_ge(sem("ln_var"), n + 1)
                pool.tensor_tensor(rstd[:, :], mv[:, :, 1], nhalf[:, :], ALU.pow).then_inc(sem("ln_rstd"), 1)

        @block.scalar
        def _(act):
            def small(dst, src):
                act.dma_start(dst, src).then_inc(sem("params_loaded"), 16)

            def row(name, *idx):
                a = dram[name]
                for i in idx:
                    a = a[i]
                return a.partition_broadcast(P)

            small(prow_b[0:CONV * NDN, :], dram["dn_conv_w"][0].rearrange("k (j p) -> (k j) p", p=P))
            small(prow_b[CONV * NDN:CONV * NDN + NX, :], dram["ssm_norm_w"][0].rearrange("(j p) -> j p", p=P))
            small(prow_b[CONV * NDN + NX:CONV * NDN + NX + NXBC, :], dram["ssm_conv_b"][0].rearrange("(j p) -> j p", p=P))
            small(prow_a[0:CONV * NXBC, :], dram["ssm_conv_w"][0].rearrange("k (j p) -> (k j) p", p=P))
            small(w_ba[:, :, :], cols(w_in0, BA0, 2 * DH))
            small(identb[:, :], dram["shape_consts_b"][:, 0:P])
            small(maskb[:, :], dram["shape_consts_b"][:, P:2 * P])
            small(sinks[:, :], row("swa_sinks", 0))
            small(dn_al[:, :], row("dn_a_log", 0))
            small(dn_dtb[:, :], row("dn_dt_bias", 0))
            small(dn_nw[:, :], row("dn_norm_w", 0))
            small(w_dt[:, :, :], cols(w_in1, SI + NXBC * P, SH))
            small(ssm_al[:, :], row("ssm_a_log", 0))
            small(ssm_dtb[:, :], row("ssm_dt_bias", 0))
            small(ssm_db[:, :], row("ssm_d", 0))
            small(w_rt[:, :, :], cols(dram["moe_w_router"][0], 0, E))
            small(brt[:, :], row("moe_b_router", 0))

            def load_ln(n):
                if n:
                    act.wait_ge(sem("ln_done"), n)
                act.dma_start(ln_gb[:, 0], dram["ln_g"][n // 2][n % 2].partition_broadcast(P)).then_inc(sem("ln_loaded"), 16)
                act.dma_start(ln_gb[:, 1], dram["ln_b"][n // 2][n % 2].partition_broadcast(P)).then_inc(sem("ln_loaded"), 16)

            def turn_copies(n):
                for q in range(2):
                    act.wait_ge(sem("x_turned"), 4 * n + 3 + q)
                    act.copy(xT[:, 4 * q:4 * q + 4, P:2 * P], ps[:, 2 + q, :].rearrange("p (k t) -> p k t", k=4)
                             ).then_inc(sem("xT_copied"), 1)

            act_step = [0]

            def link(ins):
                act_step[0] += 1
                ins.then_inc(sem("act_step"), 1)
                act.wait_ge(sem("act_step"), act_step[0])

            load_ln(0)
            turn_copies(0)
            for q in range(NDN // 2):
                act.wait_ge(sem("dn_conv"), q + 1)
                act.activation(dnT[:, 2 * q:2 * q + 2, :], dnT[:, 2 * q:2 * q + 2, :], ACT.Silu).then_inc(sem("dn_silu"), 1)
            for t in range(TT):
                act.wait_ge(sem("gate_proj"), t + 1)
                act.activation(gate[:, t, :], ps[:, 4 + t, :], ACT.Silu).then_inc(sem("gate_silu"), 1)
            act.wait_ge(sem("att_max"), 1)
            for n in range(2):
                for h in range(AH):
                    seg_ = s[:, h, 0:256] if n == 1 else s[:, h, 256:384]
                    act.activation(seg_, seg_, ACT.Exp, bias=nmx[:, n, h:h + 1], accum_out=den[:, n, h:h + 1]
                                   ).then_inc(sem("att_exp"), 1)
            act.activation(sdx[:, :, :], sdx[:, :, :], ACT.Exp).then_inc(sem("att_exp"), 1)
            for b in (1, 3, 5):
                act.wait_ge(sem("p_turned"), b + 1)
                act.copy(pT[:, 4 * b:4 * b + 4, :], ps[:, b, :].rearrange("p (k t) -> p k t", k=4)).then_inc(sem("pT_copied_act"), 1)
            for b in range(2):
                act.wait_ge(sem("att_out"), b + 1)
                act.copy(mixT[:, 2 * b:2 * b + 2, :], ps[:, 6 + b, :].rearrange("p (k t) -> p k t", k=2)).then_inc(sem("mix_att"), 1)
            act.wait_ge(sem("dn_z"), 1)
            act.activation(adn[:, :, :], adn[:, :, :], ACT.Exp, scale=-1.0).then_inc(sem("dn_e1"), 1)
            act.activation(ebdn[:, :, :], ba[:, :, 0:DH], ACT.Exp, scale=-1.0).then_inc(sem("dn_eb"), 1)
            act.wait_ge(sem("params_loaded"), 16 * 17)
            act.activation(eadn[:, :], dn_al[:, :], ACT.Exp).then_inc(sem("dn_eb"), 1)
            act.wait_ge(sem("dn_e1"), 1)
            act.activation(e2dn[:, :, :], adn[:, :, :], ACT.Ln, bias=1.0).then_inc(sem("dn_e2"), 1)
            for b in range(4):
                act.wait_ge(sem("dn_ss"), b + 1)
                link(act.activation(rn[:, 512 * b:512 * b + 512], ps[:, b, :], ACT.Ln, bias=eps_rms[:, 0:1]))
                act.activation(rn[:, 512 * b:512 * b + 512], rn[:, 512 * b:512 * b + 512], ACT.Exp, scale=-0.5).then_inc(sem("dn_rn"), 1)
            act.wait_ge(sem("dn_cols"), 1)
            act.activation(dke[:, :], ddk[:, :], ACT.Exp).then_inc(sem("dn_dke"), 1)
            act.activation(egc1[:, :], ngc[:, 1, :], ACT.Exp, scale=-1.0).then_inc(sem("dn_dke"), 1)
            for t in range(TT):
                act.wait_ge(sem("dn_gcrow"), t + 1)
                for h in range(DH):
                    act.activation(decT[:, t * DH + h, :], ps[:, t, h * P:(h + 1) * P], ACT.Exp, bias=ngc[:, t, h:h + 1]
                                   ).then_inc(sem("dn_dec"), 1)
            for lv in range(LEVELS):
                if lv:
                    for t in range(TT):
                        act.wait_ge(sem("inv_P"), 2 * lv + t + 1)
                        act.copy(Pm[:, t * DH:(t + 1) * DH, :], ps[:, t, :].rearrange("p (h c) -> p h c", h=DH)).then_inc(sem("inv_P_copied"), 1)
            act.wait_ge(sem("dn_w"), 1)
            act.copy(wT[:, :, :], ps[:, 2, :].rearrange("p (h c) -> p h c", h=DH)).then_inc(sem("dn_w_copied"), 1)
            act.wait_ge(sem("dn_S"), 1)
            act.copy(S1[:, :, :], ps[:, 4, :].rearrange("p (h c) -> p h c", h=DH)).then_inc(sem("dn_S_copied"), 1)
            act.wait_ge(sem("dn_oss"), 1)
            link(act.activation(orn[:, :], oss[:, :], ACT.Ln, bias=eps_rms[:, 0:1], scale=1.0 / DD))
            act.activation(orn[:, :], orn[:, :], ACT.Exp, scale=-0.5).then_inc(sem("dn_orn"), 1)
            act.wait_ge(sem("o_turned"), 2)
            act.copy(mixT[:, 4:8, P:2 * P], ps[:, 1, :].rearrange("p (h c) -> p h c", h=DH)).then_inc(sem("mix_dn"), 1)
            load_ln(1)
            turn_copies(1)
            if limit < 2:
                act.wait_ge(sem("ln_loaded"), 64)
                return
            def ffn_silu(b, step_plus_1, h_free):
                act.wait_ge(sem("ffn_gu"), step_plus_1 + FIRST)
                if h_free is not None:
                    act.wait_ge(sem("ffn_h"), h_free + FIRST)
                act.activation(sg[:, b, :], ps[:, 2 * b, :], ACT.Silu).then_inc(sem("ffn_silu"), 1)

            ffn_silu(0, 1, None)
            with act.Fori(0, FSTEPS // 2) as i:
                ffn_silu(1, 2 * i + 2, 2 * i)
                ffn_silu(0, 2 * i + 3, 2 * i + 1)
            load_ln(2)
            turn_copies(2)
            if limit < 3:
                act.wait_ge(sem("ln_loaded"), 96)
                return
            for q in range(NXBC // 2):
                act.wait_ge(sem("ssm_conv"), q + 1)
                for j in (2 * q, 2 * q + 1):
                    act.activation(xbcT[:, j, :], xbcT[:, j, :], ACT.Silu, bias=ssm_cb(j)).then_inc(sem("ssm_silu"), 1)
            for q in range(NX // 2):
                act.wait_ge(sem("z_proj"), q + 1)
                act.activation(zT[:, 2 * q:2 * q + 2, :], ps[:, 4 + q % 4, :].rearrange("p (k t) -> p k t", k=2), ACT.Silu
                               ).then_inc(sem("z_silu"), 1)
            act.wait_ge(sem("ssm_z"), 1)
            link(act.activation(saz[:, :, :], saz[:, :, :], ACT.Exp, scale=-1.0))
            act.activation(se2[:, :, :], saz[:, :, :], ACT.Ln, bias=1.0).then_inc(sem("ssm_sp"), 1)
            act.activation(sea[:, :], ssm_al[:, :], ACT.Exp).then_inc(sem("ssm_sp"), 1)
            act.wait_ge(sem("B_turned"), 1)
            act.copy(Btok[:, :], ps[:, 0, :]).then_inc(sem("B_copied"), 1)
            act.wait_ge(sem("ssm_cols"), 1)
            act.activation(sdec[:, :], sdd[:, :], ACT.Exp).then_inc(sem("ssm_dec"), 1)
            for t in range(TT):
                act.wait_ge(sem("cb_made"), t + 1)
                act.copy(cb[:, 4 * t:4 * t + 4, :], ps[:, 2 + t, :].rearrange("p (g c) -> p g c", g=SG)).then_inc(sem("cb_copied"), 1)
            for g in range(SG):
                act.wait_ge(sem("state_made"), g + 1)
                act.copy(state[:, 512 * g:512 * g + 512], ps[:, 4 + g, :]).then_inc(sem("state_copied"), 1)
            for i in range(TT * SG):
                t, g = i // SG, i % SG
                act.wait_ge(sem("acs_rows"), i + 1)
                if i >= 2:
                    act.wait_ge(sem("MT_made"), i - 1)
                for r in range(8):
                    h = 8 * g + r
                    act.activation(seg[:, i % 2, r, :], ps[:, 2 * (i % 2) + r // 4, (r % 4) * P:(r % 4 + 1) * P], ACT.Exp,
                                   bias=nacs[:, t, h:h + 1]).then_inc(sem("seg_made"), 1)
            for q in range(4):
                act.wait_ge(sem("yoff_made"), q + 1)
                if q >= 2:
                    act.wait_ge(sem("yoff_added"), q - 1)
                act.activation(er[:, q % 2, :], ps[:, 1 + 2 * (q % 2), :], ACT.Exp).then_inc(sem("er_made"), 1)
            for g in range(SG):
                act.wait_ge(sem("y_ss"), g + 1)
                link(act.activation(yrn[:, g, :], ps[:, 4 + g, 0:SEQ], ACT.Ln, bias=eps_rms[:, 0:1], scale=1.0 / (SI // SG)))
                act.activation(yrn[:, g, :], yrn[:, g, :], ACT.Exp, scale=-0.5).then_inc(sem("y_rn"), 1)
            load_ln(3)
            turn_copies(3)
            if limit < 5:
                act.wait_ge(sem("ln_loaded"), 128)
                return
            act.wait_ge(sem("rt_dm"), 1)
            act.activation(g1[:, :, :], dm[:, :, :], ACT.Exp).then_inc(sem("rt_e"), 1)

            def expert_act(it):
                def cut_high(n):
                    i = n % RAW
                    act.wait_ge(raw_loaded[i], 16 * (PPE // RAW) * it + 16 * (n // RAW + 1))
                    act.wait_ge(piece_used, PPE * it + (n + 1))
                    act.copy(w_hi[:, n % CUT, :], raw[:, i, :]).then_inc(sem("hi_made"), 1)

                def silu(j):
                    act.wait_ge(piece_used, PPE * it + (CUT + last_piece(j, 1) + 1))
                    if j >= 2:
                        act.wait_ge(sem("e_h"), ESTEPS * it + (j - 1) + FIRST)
                    else:
                        act.wait_ge(sem("e_h"), ESTEPS * it + FIRST)
                    act.activation(esg[:, j % 2, :], ps[:, 2 * (j % 2), :], ACT.Silu).then_inc(sem("e_silu"), 1)

                def turned(j):
                    act.wait_ge(sem("eh_turned"), ESTEPS * it + (j + 1))
                    act.copy(ehT_hi[:, j % 2], ps[:, 4, :].rearrange("p (k t) -> p k t", k=4)).then_inc(sem("ehT_hi_made"), 1)

                after = {}
                for j in range(ESTEPS):
                    after.setdefault(min(last_piece(j, 1) + 2, PPE - 1), []).append((silu, j))
                for j in range(ESTEPS - 1):
                    after.setdefault(min(last_piece(j + 1, 0) + 2, PPE - 1), []).append((turned, j))
                after.setdefault(PPE - 1, []).append((turned, ESTEPS - 1))
                for n in range(CUT):
                    cut_high(n)
                for q in range(2):
                    act.wait_ge(sem("xg_made"), 2 * it + q + 1 + FIRST)
                    act.copy(xg_hi[:, 4 * q:4 * q + 4, :], ps[:, 2 + q, :].rearrange("p (k t) -> p k t", k=4)
                             ).then_inc(sem("xg_hi_made"), 1)
                for n in range(CUT, PPE):
                    cut_high(n)
                    for do, j in after.get(n, ()):
                        do(j)
                act.wait_ge(piece_used, PPE * it + (CUT + PPE))
                act.copy(oe[:, 512:1024], ps[:, 6, :]).then_inc(sem("oe_copied_act"), 1)

            with act.Fori(0, E) as e:
                expert_act(e)
            act.wait_ge(sem("overflow_known"), 1)
            more = act.value_load(over[0:1, 0:1].bitcast(I32), min_val=0, max_val=SEQ)
            with act.If(more > 0):
                with act.Fori(0, E) as e:
                    expert_act(e + E)
            for t in range(TT):
                act.wait_ge(sem("out_ready"), t + 1)
                act.dma_start(out[0, t * P:(t + 1) * P, :], x_tok[:, t, :]).then_inc(sem("out_stored"), 16)
            act.wait_ge(sem("out_stored"), 16 * TT)

        @block.vector
        def _(dve):
            step = [0]

            def link(ins):
                step[0] += 1
                ins.then_inc(sem("dve_step"), 1)
                dve.wait_ge(sem("dve_step"), step[0])

            TTO, TS, STT = dve.tensor_tensor, dve.tensor_scalar, dve.scalar_tensor_tensor

            def four(ap):
                return ap.rearrange("p (k t) -> p k t", k=4)

            def turn_copies(n):
                for q in range(2):
                    dve.wait_ge(sem("x_turned"), 4 * n + 1 + q)
                    dve.tensor_copy(xT[:, 4 * q:4 * q + 4, 0:P], four(ps[:, q, :])).then_inc(sem("xT_copied"), 1)

            def layer_norm(n, acc_sem, acc_count, sub=None):
                dve.wait_ge(acc_sem, acc_count)
                dve.wait_ge(sem("ln_loaded"), 32 * (n + 1))
                if sub is None:
                    for t in range(TT):
                        link(STT(x_tok[:, t, :].rearrange("p (b n) -> p b n", b=2), x_tok[:, t, :].rearrange("p (b n) -> p b n", b=2),
                                 ALPHA, ps[:, 4 + 2 * t:6 + 2 * t, :], ALU.mult, ALU.add))
                for t in range(TT):
                    for b in range(2):
                        link(dve.bn_stats(stats[:, t, b, :], x_tok[:, t, 512 * b:512 * b + 512]))
                for t in range(TT):
                    link(dve.bn_aggr(mv[:, t, :], stats[:, t, :, :].rearrange("p b s -> p (b s)")))
                TS(mv[:, :, 1], mv[:, :, 1], LN_EPS, None, ALU.add).then_inc(sem("ln_var"), 1)
                for t in range(TT):
                    link(STT(x_tok[:, t, :], x_tok[:, t, :], mv[:, t, 0:1], ln_gb[:, 0, :], ALU.subtract, ALU.mult))
                dve.wait_ge(sem("ln_rstd"), n + 1)
                for t in range(TT):
                    ins = STT(x_tok[:, t, :], x_tok[:, t, :], rstd[:, t:t + 1], ln_gb[:, 1, :], ALU.mult, ALU.add)
                    if n == 2 * DEPTH - 1:
                        ins.then_inc(sem("out_ready"), 1)
                    elif t == TT - 1:
                        ins.then_inc(sem("ln_done"), 1)

            def conv(chunks, src, dst, tap):
                for j in chunks:
                    last = TS(dst(j), src(j), tap(CONV - 1, j), None, ALU.mult)
                link(last)
                for k in range(1, CONV):
                    for j in chunks:
                        last = STT(dst(j)[:, k:SEQ], src(j)[:, 0:SEQ - k], tap(CONV - 1 - k, j), dst(j)[:, k:SEQ], ALU.mult, ALU.add)
                    if k < CONV - 1:
                        link(last)
                return last

            link(dve.memset(eps_rms[:, :], RMS_EPS))
            turn_copies(0)
            dve.wait_ge(sem("params_turned"), 1)
            dve.tensor_copy(pcol[:, 0:CONV * NXBC], ps[:, 4, 0:CONV * NXBC])
            dve.tensor_copy(pcol[:, P:P + 88], ps[:, 4, P:P + 88])
            dve.tensor_copy(dcol[0:64, :], ssm_db[0:64, :].rearrange("p (j r) -> p j r", r=2)[:, :, 0])
            dve.tensor_copy(dcol[64:128, :], ssm_db[64:128, :].rearrange("p (j r) -> p j r", r=2)[:, :, 1]
                            ).then_inc(sem("params_copied"), 1)
            dve.wait_ge(sem("params_copied"), 1)
            for q in range(NDN // 2):
                dve.wait_ge(sem("dn_proj"), q + 1)
                conv((2 * q, 2 * q + 1), lambda j: ps[:, (j // 2) % 4, (j % 2) * SEQ:(j % 2 + 1) * SEQ],
                     lambda j: dnT[:, j, :], dn_tap).then_inc(sem("dn_conv"), 1)
            for t in range(TT):
                dve.wait_ge(sem("q_proj"), t + 1)
                dve.tensor_copy(qkv[:, t, 0:512].rearrange("p (c g d) -> p g c d", c=4, g=AKV),
                                ps[:, 6 + t, :].rearrange("p (g c d) -> p g c d", c=4, g=AKV))
            for t in range(TT):
                dve.wait_ge(sem("kv_proj"), t + 1)
                dve.tensor_copy(qkv[:, t, 512:768], ps[:, 4 + t, 0:256])
                link(dve.tensor_copy(ba[:, t, :], ps[:, 4 + t, 256:256 + 2 * DH]))
            qk4 = qkv[:, :, 0:640].rearrange("p t (h d) -> p t h d", d=AD)
            x1, x2 = qk4[:, :, :, 0:HALF], qk4[:, :, :, HALF:ROPE]

            def table(c):
                return const[:, c:c + TT * HALF].rearrange("p (t i) -> p t i", t=TT).unsqueeze(2).to_broadcast([P, TT, 10, HALF])

            r4 = [rt[:, i, :].rearrange("p (t h i) -> p t h i", t=TT, h=10) for i in range(4)]
            TTO(r4[0], x1, table(C_COS), ALU.mult)
            TTO(r4[1], x2, table(C_SIN), ALU.mult)
            TTO(r4[2], x2, table(C_COS), ALU.mult)
            link(TTO(r4[3], x1, table(C_SIN), ALU.mult))
            TTO(x1, r4[0], r4[1], ALU.subtract)
            TTO(x2, r4[2], r4[3], ALU.add).then_inc(sem("rope_done"), 1)
            link(TTO(zdn[:, :, :], ba[:, :, DH:2 * DH], over_heads(dn_dtb[:, :], TT), ALU.add))
            STT(adn[:, :, :], zdn[:, :, :], -1.0, zdn[:, :, :], ALU.mult, ALU.max).then_inc(sem("dn_z"), 1)
            for t in range(TT):
                dve.wait_ge(sem("q_turned"), t + 1)
                dve.tensor_copy(qT[:, :, t * P:(t + 1) * P], four(ps[:, t, :])).then_inc(sem("qT_copied"), 1)
            dve.wait_ge(sem("q_turned"), 3)
            dve.tensor_copy(kT[:, :], ps[:, 2, 0:SEQ]).then_inc(sem("qT_copied"), 1)
            am = const[:, C_AM:C_AM + 2 * P]
            for b in range(4):
                dve.wait_ge(sem("scores"), b + 1)
                last = STT(s[:, 2 * b:2 * b + 2, 0:256], ps[:, b, :].rearrange("p (h k) -> p h k", h=2), AD ** -0.5,
                           over_heads(am, 2), ALU.mult, ALU.add)
            for b in range(2):
                dve.wait_ge(sem("scores"), 5 + b)
                last = STT(s[:, 4 * b:4 * b + 4, 256:384], four(ps[:, 4 + b, :]), AD ** -0.5,
                           over_heads(am[:, P:2 * P], 4), ALU.mult, ALU.add)
            link(last)
            dve.tensor_reduce(mx[:, 1, :], s[:, :, 0:256], AX, ALU.max)
            link(dve.tensor_reduce(mx[:, 0, :], s[:, :, 256:384], AX, ALU.max))
            link(TTO(mx[:, :, :], mx[:, :, :], over_heads(sinks[:, :], 2), ALU.max))
            link(TS(nmx[:, :, :], mx[:, :, :], -1.0, None, ALU.mult))
            TTO(sdx[:, :, :], nmx[:, :, :], over_heads(sinks[:, :], 2), ALU.add).then_inc(sem("att_max"), 1)
            dve.wait_ge(sem("att_exp"), 2 * AH + 1)
            link(TTO(den[:, :, :], den[:, :, :], sdx[:, :, :], ALU.add))
            link(dve.reciprocal(rden[:, :, :], den[:, :, :]))
            TTO(s[:, :, 256:384], s[:, :, 256:384], bc(rden[:, 0, :], 128), ALU.mult).then_inc(sem("p_ready"), 1)
            TTO(s[:, :, 0:256], s[:, :, 0:256], bc(rden[:, 1, :], 256), ALU.mult).then_inc(sem("p_ready"), 1)
            for b in (0, 2, 4):
                dve.wait_ge(sem("p_turned"), b + 1)
                dve.tensor_copy(pT[:, 4 * b:4 * b + 4, :], four(ps[:, b, :])).then_inc(sem("pT_copied_dve"), 1)
            dve.wait_ge(sem("dn_e2"), 1)
            dve.wait_ge(sem("dn_eb"), 2)
            link(STT(gdn[:, :, :], zdn[:, :, :], 0.0, e2dn[:, :, :], ALU.max, ALU.add))
            link(STT(gdn[:, :, :], gdn[:, :, :], -1.0, over_heads(eadn[:, :], TT), ALU.mult, ALU.mult))
            link(TS(beta[:, :, :], ebdn[:, :, :], 1.0, None, ALU.add))
            dve.reciprocal(beta[:, :, :], beta[:, :, :]).then_inc(sem("dn_gb"), 1)
            dve.wait_ge(sem("dn_silu"), NDN // 2)
            dve.wait_ge(sem("att_out"), 2)
            for b in range(4):
                TTO(sq[:, 512 * b:512 * b + 512].rearrange("p (k t) -> p k t", k=2), dnT[:, 2 * b:2 * b + 2, :],
                    dnT[:, 2 * b:2 * b + 2, :], ALU.mult).then_inc(sem("dn_sq"), 1)
            rn3 = rn[:, :].rearrange("p (k t) -> p k t", t=SEQ)
            dve.wait_ge(sem("dn_rn"), 4)
            STT(dnT[:, 0:4, :], dnT[:, 0:4, :], DD ** -0.5, rn3[:, 0:4, :], ALU.mult, ALU.mult).then_inc(sem("dn_qk"), 1)
            TTO(dnT[:, 4:8, :], dnT[:, 4:8, :], rn3[:, 4:8, :], ALU.mult).then_inc(sem("dn_qk"), 1)
            dve.wait_ge(sem("dn_gc"), 1)
            link(TS(ngc[:, :, :], ps[:, 4, 0:TT * DH].rearrange("p (t h) -> p t h", t=TT), -1.0, None, ALU.mult))
            TTO(ddk[:, :], ps[:, 4, 8:12], ngc[:, 0, :], ALU.add).then_inc(sem("dn_cols"), 1)
            dve.wait_ge(sem("dn_dke"), 2)
            dve.wait_ge(sem("dn_gb"), 1)
            link(TTO(bege[:, :], beta[:, 1, :], egc1[:, :], ALU.mult))
            for t in range(TT):
                dve.wait_ge(sem("dn_dec"), DH * (t + 1))
                dve.wait_ge(sem("dn_kk"), t + 1)
                hs = slice(t * DH, (t + 1) * DH)
                TTO(attnT[:, hs, :], four(ps[:, 6 + t, :]), decT[:, hs, :], ALU.mult)
                link(TTO(AT[:, hs, :], four(ps[:, 4 + t, :]), decT[:, hs, :], ALU.mult))
                TTO(AT[:, hs, :], AT[:, hs, :], four(ps[:, 2 + t, :]), ALU.mult).then_inc(sem("dn_A"), 1)
            dve.wait_ge(sem("dn_A"), TT)
            dve.wait_ge(sem("kv_turned"), 1)
            TTO(kdec[:, :, :], four(ps[:, 4, :]), bc(dke[:, :], P), ALU.mult)
            dve.wait_ge(sem("kv_turned"), 2)
            TTO(vb[:, 0:4, :], four(ps[:, 5, :]), bc(beta[:, 0, :], P), ALU.mult)
            dve.wait_ge(sem("kv_turned"), 3)
            TTO(kbe[:, :, :], four(ps[:, 6, :]), bc(bege[:, :], P), ALU.mult)
            dve.wait_ge(sem("kv_turned"), 4)
            TTO(vb[:, 4:8, :], four(ps[:, 7, :]), bc(beta[:, 1, :], P), ALU.mult).then_inc(sem("kv_scaled"), 1)
            for lv in range(LEVELS):
                mask = const[:, C_LVL + lv * P:C_LVL + (lv + 1) * P]
                if lv:
                    dve.wait_ge(sem("inv_P"), 2 * lv)
                    dve.wait_ge(sem("inv_X"), 2 * lv)
                for t in range(TT):
                    hs = slice(t * DH, (t + 1) * DH)
                    TTO(LT[:, hs, :], AT[:, hs, :], over_heads(mask, DH), ALU.mult).then_inc(sem("inv_L"), 1)
                for t in range(TT):
                    hs = slice(t * DH, (t + 1) * DH)
                    if lv == 0:
                        dve.wait_ge(sem("inv_L"), t + 1)
                        TTO(XT[:, hs, :], over_heads(ident, DH), LT[:, hs, :], ALU.subtract)
                        dve.wait_ge(sem("inv_P"), t + 1)
                        TTO(X[:, hs, :], over_heads(ident, DH), four(ps[:, t, :]), ALU.subtract).then_inc(sem("inv_X"), 1)
                    else:
                        dve.wait_ge(sem("inv_PX"), 2 * (lv - 1) + t + 1)
                        last = TTO(XT[:, hs, :], XT[:, hs, :], four(ps[:, 4 + t, :]), ALU.subtract)
                        if lv < LEVELS - 1:
                            last = TTO(X[:, hs, :], X[:, hs, :], four(ps[:, 2 + t, :]), ALU.subtract)
                        last.then_inc(sem("inv_X"), 1)
            dve.wait_ge(sem("dn_u"), 1)
            dve.tensor_copy(u[:, 0:4, :], four(ps[:, 0, :])).then_inc(sem("dn_u_copied"), 1)
            dve.wait_ge(sem("dn_u"), 2)
            link(dve.tensor_copy(u[:, 4:8, :], four(ps[:, 1, :])))
            dve.wait_ge(sem("dn_o0"), 1)
            dve.tensor_copy(o[:, 0:4, :], four(ps[:, 3, :]))
            dve.wait_ge(sem("dn_wS"), 1)
            TTO(vnew[:, :, :], u[:, 4:8, :], four(ps[:, 5, :]), ALU.subtract).then_inc(sem("dn_vnew"), 1)
            dve.wait_ge(sem("dn_qS"), 1)
            link(TTO(o[:, 4:8, :], four(ps[:, 6, :]), bc(egc1[:, :], P), ALU.mult))
            dve.wait_ge(sem("dn_o1"), 1)
            link(TTO(o[:, 4:8, :], o[:, 4:8, :], four(ps[:, 7, :]), ALU.add))
            link(TTO(osq[:, :, :], o[:, :, :], o[:, :, :], ALU.mult))
            dve.tensor_reduce(oss[:, :], osq[:, :, :], AX, ALU.add).then_inc(sem("dn_oss"), 1)
            dve.wait_ge(sem("dn_orn"), 1)
            link(TTO(o[:, :, :], o[:, :, :], bc(orn[:, :], P), ALU.mult))
            link(TTO(o[:, :, :], o[:, :, :], over_heads(dn_nw[:, :], TT * DH), ALU.mult))
            dve.wait_ge(sem("gate_silu"), TT)
            TTO(o[:, :, :], o[:, :, :], gate[:, :, :].rearrange("p t (h d) -> p (t h) d", d=DD), ALU.mult).then_inc(sem("o_ready"), 1)
            dve.wait_ge(sem("o_turned"), 1)
            dve.tensor_copy(mixT[:, 4:8, 0:P], four(ps[:, 0, :])).then_inc(sem("mix_dn"), 1)
            layer_norm(0, sem("out_proj"), 2)
            turn_copies(1)
            if limit < 2:
                return

            def ffn_mult(b, step_plus_1, down_free):
                dve.wait_ge(sem("ffn_silu"), step_plus_1)
                if down_free is not None:
                    dve.wait_ge(sem("ffn_down"), down_free + FIRST)
                TTO(hT[:, b].rearrange("p k t -> p (k t)"), sg[:, b, :], ps[:, 2 * b + 1, :], ALU.mult).then_inc(sem("ffn_h"), 1)

            dve.sem_inc(sem("ffn_h"), FIRST)
            ffn_mult(0, 1, None)
            with dve.Fori(0, FSTEPS // 2) as i:
                ffn_mult(1, 2 * i + 2, 2 * i + 1)
                ffn_mult(0, 2 * i + 3, 2 * i + 2)
            layer_norm(1, sem("ffn_down"), FSTEPS + 1 + FIRST)
            turn_copies(2)
            if limit < 3:
                return

            dve.wait_ge(sem("dt_proj"), 1)
            link(TTO(sz[:, :, :], ps[:, 4, 0:TT * SH].rearrange("p (t h) -> p t h", t=TT), over_heads(ssm_dtb[:, :], TT), ALU.add))
            STT(saz[:, :, :], sz[:, :, :], -1.0, sz[:, :, :], ALU.mult, ALU.max).then_inc(sem("ssm_z"), 1)
            for q in range(NXBC // 2):
                dve.wait_ge(sem("xbc_proj"), q + 1)
                conv((2 * q, 2 * q + 1), lambda j: ps[:, (j // 2) % 4, (j % 2) * SEQ:(j % 2 + 1) * SEQ],
                     lambda j: xbcT[:, j, :], ssm_tap).then_inc(sem("ssm_conv"), 1)
            dve.wait_ge(sem("ssm_sp"), 2)
            link(STT(sdt[:, :, :], sz[:, :, :], 0.0, se2[:, :, :], ALU.max, ALU.add))
            STT(dA[:, :, :], sdt[:, :, :], -1.0, over_heads(sea[:, :], TT), ALU.mult, ALU.mult).then_inc(sem("dA_made"), 1)
            for t in range(TT):
                for q in range(4):
                    dve.wait_ge(sem("xs_turned"), 4 * t + q + 1)
                    TTO(xdt[:, t, 512 * q:512 * q + 512].rearrange("p (h d) -> p h d", d=SD),
                        ps[:, 4 * t + q, :].rearrange("p (h d) -> p h d", d=SD), bc(sdt[:, t, 8 * q:8 * q + 8], SD), ALU.mult
                        ).then_inc(sem("xdt_made"), 1)
            dve.wait_ge(sem("acs_made"), 1)
            link(TS(nacs[:, :, :], ps[:, 1, 0:TT * SH].rearrange("p (t h) -> p t h", t=TT), -1.0, None, ALU.mult))
            TTO(sdd[:, :], ps[:, 1, 64:96], nacs[:, 0, :], ALU.add).then_inc(sem("ssm_cols"), 1)
            dve.wait_ge(sem("ssm_dec"), 1)
            TTO(xdec[:, :].rearrange("p (h d) -> p h d", d=SD), xdt[:, 0, :].rearrange("p (h d) -> p h d", d=SD),
                bc(sdec[:, :], SD), ALU.mult).then_inc(sem("xdec_made"), 1)

            def y_diag(i):
                t, g = i // SG, i % SG
                dve.wait_ge(sem("y_made"), i + 1)
                for c in range(4):
                    j = 4 * g + c
                    yj = xbcT[:, j, t * P:(t + 1) * P]
                    last = STT(yj, yj, dcol[:, j:j + 1], ps[:, 4 + i % 2, c * P:(c + 1) * P], ALU.mult, ALU.add)
                last.then_inc(sem("y_added"), 1)

            for i in range(TT * SG):
                dve.wait_ge(sem("seg_made"), 8 * (i + 1))
                dve.wait_ge(sem("cb_copied"), TT)
                if i >= 2:
                    dve.wait_ge(sem("y_made"), i - 1)
                TTO(MT[:, i % 2], seg[:, i % 2], over_heads(cb[:, i, :], 8), ALU.mult).then_inc(sem("MT_made"), 1)
                if i:
                    y_diag(i - 1)
            y_diag(TT * SG - 1)
            dve.wait_ge(sem("y_added"), TT * SG)
            for q in range(4):
                dve.wait_ge(sem("er_made"), q + 1)
                link(TTO(yo[:, q % 2, :], er[:, q % 2, :], ps[:, 2 * (q % 2), :], ALU.mult))
                yq = xbcT[:, 4 * q:4 * q + 4, P:2 * P]
                TTO(yq, yq, four(yo[:, q % 2, :]), ALU.add).then_inc(sem("yoff_added"), 1)
            dve.wait_ge(sem("yoff_added"), 4)
            dve.wait_ge(sem("z_silu"), NX // 2)
            for g in range(SG):
                yg = xbcT[:, 4 * g:4 * g + 4, :]
                link(TTO(yg, yg, zT[:, 4 * g:4 * g + 4, :], ALU.mult))
                if g >= 2:
                    dve.wait_ge(sem("y_ss"), g - 1)
                TTO(ysq[:, g % 2, :].rearrange("p (k t) -> p k t", k=4), yg, yg, ALU.mult).then_inc(sem("ysq_made"), 1)
            for g in range(SG):
                dve.wait_ge(sem("y_rn"), g + 1)
                for j in range(4 * g, 4 * g + 4):
                    last = STT(xbcT[:, j, :], xbcT[:, j, :], ssm_nw(j), yrn[:, g, :], ALU.mult, ALU.mult)
                last.then_inc(sem("y_ready"), 1)
            layer_norm(2, sem("out_proj"), 6)
            turn_copies(3)
            if limit < 5:
                return

            dve.wait_ge(sem("logits"), 1)
            link(TTO(lg[:, :, :], ps[:, 4, 0:TT * E].rearrange("p (t e) -> p t e", t=TT), over_heads(brt[:, :], TT), ALU.add))
            for t in range(TT):
                link(dve.max(top8[:, t, :], lg[:, t, :]))
                link(dve.max_index(idx8[:, t, :].bitcast(U32), top8[:, t, :], lg[:, t, :]))
            TTO(dm[:, :, :], top8[:, :, 1:2], top8[:, :, 0:1], ALU.subtract).then_inc(sem("rt_dm"), 1)
            link(dve.tensor_copy(idxf[:, :, :], idx8[:, :, 0:2].bitcast(U32)))
            for t in range(TT):
                TS(oh1[:, t, :], iota8, idxf[:, t, 0:1], None, ALU.is_equal)
                link(TS(oh2[:, t, :], iota8, idxf[:, t, 1:2], None, ALU.is_equal))
            TTO(sel[:, :, :], oh1[:, :, :], oh2[:, :, :], ALU.add).then_inc(sem("sel_made"), 1)
            dve.wait_ge(sem("rt_e"), 1)
            link(TS(g2[:, :, :], g1[:, :, :], 1.0, None, ALU.add))
            link(dve.reciprocal(g2[:, :, :], g2[:, :, :]))
            link(TTO(g1[:, :, :], g1[:, :, :], g2[:, :, :], ALU.mult))
            for t in range(TT):
                link(TS(comb[:, t, :], oh1[:, t, :], g2[:, t, :], None, ALU.mult))
                link(STT(comb[:, t, :], oh2[:, t, :], g1[:, t, :], comb[:, t, :], ALU.mult, ALU.add))
            dve.wait_ge(sem("ranks"), 1)
            ps_rank = ps[:, 4, 32:32 + TT * E].rearrange("p (t e) -> p t e", t=TT)
            link(STT(rank[:, :, :], ps_rank, 1.0, sel[:, :, :], ALU.add, ALU.mult))
            link(TS(rank[:, :, :], rank[:, :, :], -1.0, None, ALU.add))
            link(TS(rank2[:, :, :], rank[:, :, :], -float(P), None, ALU.add))
            link(dve.tensor_reduce(cnt[:, :], ps[:, 4, 64:64 + E], AX, ALU.max))
            link(TS(cnt[:, :], cnt[:, :], -float(P), 0.0, ALU.add, ALU.max))
            dve.tensor_copy(over[:, :].bitcast(I32), cnt[:, :]).then_inc(sem("overflow_known"), 1)
            for t in range(TT):
                last = TS(yacc[:, t, :], x_tok[:, t, :], ALPHA, None, ALU.mult)
            last.then_inc(sem("yacc_open"), 1)

            def expert_dve(e, it, places):
                def cut_low(n):
                    dve.wait_ge(sem("hi_made"), PPE * it + (n + 1))
                    TTO(w_lo[:, n % CUT, :], raw[:, n % RAW, :], w_hi[:, n % CUT, :].bitcast(F32), ALU.subtract).then_inc(lo_made, 1)

                def mult(j):
                    dve.wait_ge(sem("e_silu"), ESTEPS * it + (j + 1))
                    TTO(eh[:, j % 2, :], esg[:, j % 2, :], ps[:, 2 * (j % 2) + 1, :], ALU.mult).then_inc(sem("e_h"), 1)

                def turned(j):
                    dve.wait_ge(sem("ehT_hi_made"), ESTEPS * it + (j + 1))
                    TTO(ehT_lo[:, j % 2], four(ps[:, 4, :]), ehT_hi[:, j % 2].bitcast(F32), ALU.subtract).then_inc(sem("ehT_made"), 1)

                dve.wait_ge(sem("xg_made"), 2 * it + FIRST)
                for t in range(TT):
                    TS(sel_rows[:, t, :], iota, places[:, t, bass.ds(e, 1)], None, ALU.is_equal)
                for t in range(TT):
                    ins = TS(sel_gate[:, t, :], iota, places[:, t, bass.ds(e, 1)], comb[:, t, bass.ds(e, 1)], ALU.is_equal, ALU.mult)
                ins.then_inc(sem("sel_rows_made"), 1)
                cut_low(0)
                dve.wait_ge(sem("G_turned"), it + 1)
                dve.wait_ge(sem("e_scattered"), 4 * it + FIRST)
                dve.tensor_copy(G[:, :, :], ps[:, 7, 0:TT * P].rearrange("p (t c) -> p t c", t=TT)).then_inc(sem("G_copied"), 1)
                for q in range(2):
                    dve.wait_ge(sem("xg_hi_made"), 2 * it + (q + 1))
                    hs = slice(4 * q, 4 * q + 4)
                    TTO(xg_lo[:, hs, :], four(ps[:, 2 + q, :]), xg_hi[:, hs, :].bitcast(F32), ALU.subtract).then_inc(sem("xg_lo_made"), 1)
                after = {}
                for j in range(ESTEPS):
                    after.setdefault(min(last_piece(j, 1) + 2, PPE - 1), []).append((mult, j))
                for j in range(ESTEPS - 1):
                    after.setdefault(min(last_piece(j + 1, 0) + 2, PPE - 1), []).append((turned, j))
                after.setdefault(PPE - 1, []).append((turned, ESTEPS - 1))
                for n in range(1, PPE):
                    cut_low(n)
                    for do, j in after.get(n, ()):
                        do(j)
                dve.wait_ge(piece_used, PPE * it + (CUT + PPE))
                dve.tensor_copy(oe[:, 0:512], ps[:, 5, :]).then_inc(sem("oe_copied_dve"), 1)
                for q in range(2 * TT):
                    dve.wait_ge(sem("e_scattered"), 4 * it + (q + 1) + FIRST)
                    yq = yacc[:, q // 2, 512 * (q % 2):512 * (q % 2) + 512]
                    TTO(yq, yq, ps[:, 7 if q % 2 == 0 else 4, :], ALU.add).then_inc(sem("e_added"), 1)

            dve.wait_ge(sem("yacc_open"), 1)
            dve.sem_inc(sem("e_h"), FIRST)
            dve.sem_inc(sem("e_added"), FIRST)
            dve.sem_inc(sem("ehT_made"), FIRST)
            with dve.Fori(0, E) as e:
                dve.wait_ge(sem("e_added"), 4 * e + FIRST)
                expert_dve(e, e, rank)
            more = dve.value_load(over[0:1, 0:1].bitcast(I32), min_val=0, max_val=SEQ)
            dve.wait_ge(sem("e_added"), 4 * E + FIRST)
            with dve.If(more > 0):
                with dve.Fori(0, E) as e:
                    dve.wait_ge(sem("e_added"), 4 * e + 4 * E + FIRST)
                    expert_dve(e, e + E, rank2)
                dve.wait_ge(sem("e_added"), 8 * E + FIRST)
            for t in range(TT):
                link(dve.tensor_copy(x_tok[:, t, :], yacc[:, t, :]))
            layer_norm(3, sem("e_added"), 4 * E + FIRST, sub=yacc)

        @block.tensor
        def _(pe):
            mm = pe.matmul

            def turn(n):
                for t in range(TT):
                    for q in range(2):
                        for k in range(4):
                            c = 4 * q + k
                            last = pe.transpose(ps[:, 2 * t + q, k * P:(k + 1) * P], x_tok[:, t, c * P:(c + 1) * P], ident)
                        last.then_inc(sem("x_turned"), 1)

            def arrived(n):
                pe.wait_ge(loaded[n % RING], 32 * (n // RING + 1))

            def wslot(n, k, width):
                return slot(n % RING)[:, 0:k * width].rearrange("p (k n) -> p k n", k=k)

            def channel_major(unit, first_pair, bank0, done, free, free_lag):
                arrived(unit)
                w = wslot(unit, KD, 512)
                for c in range(4):
                    pair = first_pair + c // 2
                    if c % 2 == 0 and pair >= free_lag:
                        pe.wait_ge(free, pair - free_lag + 1)
                    for k in range(KD):
                        last = mm(ps[:, bank0 + pair % 4, (c % 2) * SEQ:(c % 2 + 1) * SEQ], w[:, k, c * P:(c + 1) * P],
                                  xT[:, k, :], start=k == 0, stop=k == KD - 1)
                    if c % 2:
                        last.then_inc(done, 1)

            def token_major(out_ap, w, t):
                for k in range(KD):
                    last = mm(out_ap, xT[:, k, t * P:(t + 1) * P], w[:, k, :], start=k == 0, stop=k == KD - 1)
                return last

            def output_projection(unit0, n_units, src, ready):
                for i in range(n_units):
                    arrived(unit0 + i)
                    w = wslot(unit0 + i, 4, D)
                    for kk in range(4):
                        k = 4 * i + kk
                        ready(k)
                        for t in range(TT):
                            for n in range(2):
                                last = mm(ps[:, 4 + 2 * t + n, :], src[:, k, t * P:(t + 1) * P], w[:, kk, 512 * n:512 * n + 512],
                                          start=k == 0, stop=k == 4 * n_units - 1)
                    last.then_inc(sem("out_proj"), 1)

            pe.wait_ge(sem("x_loaded"), 32)
            turn(0)
            pe.wait_ge(sem("params_loaded"), 16 * 17)
            pe.transpose(ps[:, 4, 0:CONV * NXBC], prow_a[0:CONV * NXBC, :], ident[0:CONV * NXBC, 0:CONV * NXBC])
            pe.transpose(ps[:, 4, P:P + 88], prow_b[0:88, :], ident[0:88, 0:88]).then_inc(sem("params_turned"), 1)
            pe.wait_ge(sem("xT_copied"), 4)
            for i in range(3):
                channel_major(i, 2 * i, 0, sem("dn_proj"), sem("dn_conv"), 4)
            pe.wait_ge(sem("params_copied"), 1)
            arrived(3)
            for t in range(TT):
                last = token_major(ps[:, 4 + t, :], wslot(3, KD, 512), t)
                last.then_inc(sem("gate_proj"), 1)
            arrived(4)
            for t in range(TT):
                token_major(ps[:, 6 + t, :], wslot(4, KD, 512), t).then_inc(sem("q_proj"), 1)
            arrived(5)
            for t in range(TT):
                pe.wait_ge(sem("gate_silu"), t + 1)
                token_major(ps[:, 4 + t, 0:256], wslot(5, KD, 256), t)
                token_major(ps[:, 4 + t, 256:256 + 2 * DH], w_ba, t).then_inc(sem("kv_proj"), 1)
            pe.wait_ge(sem("rope_done"), 1)
            pe.wait_ge(sem("dn_conv"), NDN // 2)
            for t in range(TT):
                for c in range(4):
                    last = pe.transpose(ps[:, t, c * P:(c + 1) * P], qkv[:, t, c * P:(c + 1) * P], ident)
                last.then_inc(sem("q_turned"), 1)
            for t in range(TT):
                last = pe.transpose(ps[:, 2, t * P:(t + 1) * P], qkv[:, t, 512:640], ident)
            last.then_inc(sem("q_turned"), 1)
            pe.wait_ge(sem("qT_copied"), 3)
            for b in range(4):
                for h in (2 * b, 2 * b + 1):
                    r = slice(64 * (h // 4), 64 * (h // 4) + 64)
                    last = mm(ps[:, b, (h % 2) * 256:(h % 2) * 256 + 256], qT[r, h % 4, P:2 * P], kT[r, :], start=True, stop=True)
                last.then_inc(sem("scores"), 1)
            for b in range(2):
                for h in range(4 * b, 4 * b + 4):
                    r = slice(64 * b, 64 * b + 64)
                    last = mm(ps[:, 4 + b, (h % 4) * P:(h % 4 + 1) * P], qT[r, h % 4, 0:P], kT[r, 0:P], start=True, stop=True)
                last.then_inc(sem("scores"), 1)
            for b in range(6):
                pe.wait_ge(sem("p_ready"), 1 if b < 2 else 2)
                for i in range(4 * b, 4 * b + 4):
                    src = s[:, i, 256:384] if i < AH else s[:, (i - AH) // 2, ((i - AH) % 2) * P:((i - AH) % 2 + 1) * P]
                    last = pe.transpose(ps[:, b, (i % 4) * P:(i % 4 + 1) * P], src, ident)
                last.then_inc(sem("p_turned"), 1)
            pe.wait_ge(sem("pT_copied_dve"), 3)
            pe.wait_ge(sem("pT_copied_act"), 3)
            for h in range(AH):
                c, r = h // 2, 64 * (h % 2)
                vcol = 640 + AD * (h // 4)
                o_ = [ps[r:r + 64, 6 + c // 2, (c % 2) * SEQ + t * P:(c % 2) * SEQ + (t + 1) * P] for t in range(TT)]
                mm(o_[0], qkv[:, 0, vcol:vcol + AD], pT[:, h, :], start=True, stop=True)
                mm(o_[1], qkv[:, 0, vcol:vcol + AD], pT[:, AH + 2 * h, :], start=True, stop=False)
                last = mm(o_[1], qkv[:, 1, vcol:vcol + AD], pT[:, AH + 2 * h + 1, :], start=False, stop=True)
                if h % 4 == 3:
                    last.then_inc(sem("att_out"), 1)
            pe.wait_ge(sem("pool_set"), 3)
            for b in range(4):
                pe.wait_ge(sem("dn_sq"), b + 1)
                mm(ps[:, b, :], ones[:, :], sq[:, 512 * b:512 * b + 512], start=True, stop=True).then_inc(sem("dn_ss"), 1)
            pe.wait_ge(sem("dn_gb"), 1)
            g8 = gdn[:, :, :].rearrange("p t h -> p (t h)")
            mm(ps[:, 4, 0:8], tri, g8, start=True, stop=True)
            mm(ps[:, 4, 8:12], ones[:, :], gdn[:, 0, :], start=True, stop=True).then_inc(sem("dn_gc"), 1)
            pe.wait_ge(sem("dn_rn"), 4)
            for t in range(TT):
                mm(ps[:, t, :], identb[:, :], over_heads(maskb[:, :], 4), start=True, stop=False)
                for h in range(DH):
                    last = mm(ps[:, t, h * P:(h + 1) * P], gdn[:, t, h:h + 1].to_broadcast([P, P]), tri, start=False, stop=h == DH - 1)
                last.then_inc(sem("dn_gcrow"), 1)
                for h in range(DH):
                    mm(ps[:, 2 + t, h * P:(h + 1) * P], beta[:, t, h:h + 1].to_broadcast([P, P]), ident, start=True, stop=True)
            pe.wait_ge(sem("dn_qk"), 2)
            pe.wait_ge(sem("dn_cols"), 1)
            pe.wait_ge(sem("mix_att"), 2)
            for t in range(TT):
                ts_ = slice(t * P, (t + 1) * P)
                for h in range(DH):
                    mm(ps[:, 4 + t, h * P:(h + 1) * P], dnT[:, 4 + h, ts_], dnT[:, 4 + h, ts_], start=True, stop=True)
                    last = mm(ps[:, 6 + t, h * P:(h + 1) * P], dnT[:, 4 + h, ts_], dnT[:, h, ts_], start=True, stop=True)
                last.then_inc(sem("dn_kk"), 1)
            pe.wait_ge(sem("dn_A"), TT)
            for t in range(TT):
                for w_ in range(2):
                    for h in range(DH):
                        last = pe.transpose(ps[:, 4 + 2 * t + w_, h * P:(h + 1) * P], dnT[:, 4 + 4 * w_ + h, t * P:(t + 1) * P], ident)
                    last.then_inc(sem("kv_turned"), 1)
            for lv in range(LEVELS):
                for t in range(TT):
                    pe.wait_ge(sem("inv_L"), 2 * lv + t + 1)
                    if lv:
                        pe.wait_ge(sem("inv_X"), 2 * (lv - 1) + t + 1)
                    for h in range(DH):
                        i = t * DH + h
                        last = mm(ps[:, t, h * P:(h + 1) * P], LT[:, i, :], X[:, i, :] if lv else ident, start=True, stop=True)
                    last.then_inc(sem("inv_P"), 1)
                if lv == 0:
                    continue
                if lv == 1:
                    pe.wait_ge(sem("kv_scaled"), 1)
                for t in range(TT):
                    pe.wait_ge(sem("inv_P_copied"), 2 * (lv - 1) + t + 1)
                    for h in range(DH):
                        i = t * DH + h
                        if lv < LEVELS - 1:
                            mm(ps[:, 2 + t, h * P:(h + 1) * P], XT[:, i, :], Pm[:, i, :], start=True, stop=True)
                        last = mm(ps[:, 4 + t, h * P:(h + 1) * P], Pm[:, i, :], XT[:, i, :], start=True, stop=True)
                    last.then_inc(sem("inv_PX"), 1)
            for t in range(TT):
                pe.wait_ge(sem("inv_X"), 2 * (LEVELS - 1) + t + 1)
                for h in range(DH):
                    i = t * DH + h
                    last = mm(ps[:, t, h * P:(h + 1) * P], XT[:, i, :], vb[:, i, :], start=True, stop=True)
                last.then_inc(sem("dn_u"), 1)
            for h in range(DH):
                last = mm(ps[:, 2, h * P:(h + 1) * P], kbe[:, h, :], XT[:, 4 + h, :], start=True, stop=True)
            last.then_inc(sem("dn_w"), 1)
            pe.wait_ge(sem("dn_u_copied"), 1)
            for h in range(DH):
                last = mm(ps[:, 4, h * P:(h + 1) * P], kdec[:, h, :], u[:, h, :], start=True, stop=True)
            last.then_inc(sem("dn_S"), 1)
            for h in range(DH):
                last = mm(ps[:, 3, h * P:(h + 1) * P], attnT[:, h, :], u[:, h, :], start=True, stop=True)
            last.then_inc(sem("dn_o0"), 1)
            pe.wait_ge(sem("dn_w_copied"), 1)
            pe.wait_ge(sem("dn_S_copied"), 1)
            for h in range(DH):
                last = mm(ps[:, 5, h * P:(h + 1) * P], wT[:, h, :], S1[:, h, :], start=True, stop=True)
            last.then_inc(sem("dn_wS"), 1)
            for h in range(DH):
                last = mm(ps[:, 6, h * P:(h + 1) * P], dnT[:, h, P:2 * P], S1[:, h, :], start=True, stop=True)
            last.then_inc(sem("dn_qS"), 1)
            pe.wait_ge(sem("dn_vnew"), 1)
            for h in range(DH):
                last = mm(ps[:, 7, h * P:(h + 1) * P], attnT[:, 4 + h, :], vnew[:, h, :], start=True, stop=True)
            last.then_inc(sem("dn_o1"), 1)
            pe.wait_ge(sem("o_ready"), 1)
            for t in range(TT):
                for h in range(DH):
                    last = pe.transpose(ps[:, t, h * P:(h + 1) * P], o[:, t * DH + h, :], ident)
                last.then_inc(sem("o_turned"), 1)

            def mix_ready(k):
                if k == 0:
                    pe.wait_ge(sem("mix_att"), 2)
                if k == 4:
                    pe.wait_ge(sem("mix_dn"), 2)

            output_projection(6, 2, mixT, mix_ready)
            pe.wait_ge(sem("ln_done"), 1)
            turn(1)
            if limit < 2:
                return

            def open_banks():
                for b in range(4, 8):
                    last = mm(ps[:, b, :], identb[:, :], zerob[:, :], start=True, stop=False)
                last.then_inc(sem("ffn_down"), 1)

            def ffn_gu(i, b, arrive, h_free):
                pe.wait_ge(loaded[i], arrive)
                if h_free is not None:
                    pe.wait_ge(sem("ffn_h"), h_free + FIRST)
                w = slot(i)[:, :].rearrange("p (w k n) -> p w k n", w=2, k=KD)
                for w_ in range(2):
                    for c in range(2):
                        for k in range(KD):
                            last = mm(ps[:, 2 * b + w_, c * SEQ:(c + 1) * SEQ], w[:, w_, k, c * P:(c + 1) * P], xT[:, k, :],
                                      start=k == 0, stop=k == KD - 1)
                last.then_inc(sem("ffn_gu"), 1)
                return last

            def ffn_down(i, b, arrive, h_ready, close):
                pe.wait_ge(loaded[i], arrive)
                pe.wait_ge(sem("ffn_h"), h_ready + FIRST)
                w = slot(i)[:, 0:2 * D].rearrange("p (k n) -> p k n", k=2)
                for c in range(2):
                    for t in range(TT):
                        for n in range(2):
                            last = mm(ps[:, 4 + 2 * t + n, :], hT[:, b, c, t * P:(t + 1) * P], w[:, c, 512 * n:512 * n + 512],
                                      start=False, stop=close and c == 1)
                last.then_inc(sem("ffn_down"), 1)

            R0 = NU0 // RING
            pe.sem_inc(sem("ffn_gu"), FIRST)
            pe.sem_inc(sem("ffn_down"), FIRST)
            pe.wait_ge(sem("xT_copied"), 8)
            open_banks()
            ffn_gu(0, 0, 32 * (R0 + 1), None)
            with pe.Fori(0, FSTEPS // 2) as i:
                ffn_gu(1, 1, 32 * i + 32 * (R0 + 1), 2 * i)
                ffn_down(2, 0, 32 * i + 32 * (R0 + 1), 2 * i + 1, False)
                ffn_gu(3, 0, 32 * i + 32 * (R0 + 1), 2 * i + 1)
                ffn_down(0, 1, 32 * i + 32 * (R0 + 2), 2 * i + 2, False)
            ffn_down(1, 0, 32 * (R0 + FSTEPS // 2 + 1), FSTEPS, True)
            pe.wait_ge(sem("ln_done"), 2)
            turn(2)
            if limit < 3:
                return

            pe.wait_ge(sem("xT_copied"), 12)
            for t in range(TT):
                last = token_major(ps[:, 4, t * SH:(t + 1) * SH], w_dt, t)
            last.then_inc(sem("dt_proj"), 1)
            for i in range(6):
                channel_major(BASE1 + i, 2 * i, 0, sem("xbc_proj"), sem("ssm_conv"), 4)
            pe.wait_ge(sem("ssm_z"), 1)
            for i in range(4):
                channel_major(BASE1 + 6 + i, 2 * i, 4, sem("z_proj"), sem("z_silu"), 4)
            pe.wait_ge(sem("ssm_silu"), NXBC)
            for t in range(TT):
                for q in range(4):
                    if t == 1 and q == 0:
                        pe.wait_ge(sem("z_silu"), NX // 2)
                    for c in range(4):
                        j = 4 * q + c
                        last = pe.transpose(ps[:, 4 * t + q, c * P:(c + 1) * P], xbcT[:, j, t * P:(t + 1) * P], ident)
                    last.then_inc(sem("xs_turned"), 1)
            pe.wait_ge(sem("xdt_made"), 4)
            pe.wait_ge(sem("dA_made"), 1)
            mm(ps[:, 1, 0:64], tri, dA[:, :, :].rearrange("p t h -> p (t h)"), start=True, stop=True)
            mm(ps[:, 1, 64:96], ones[:, :], dA[:, 0, :], start=True, stop=True).then_inc(sem("acs_made"), 1)
            for g in range(SG):
                last = pe.transpose(ps[:, 0, g * P:(g + 1) * P], xbcT[:, NX + g, 0:P], ident)
            last.then_inc(sem("B_turned"), 1)
            for t in range(TT):
                for g in range(SG):
                    last = mm(ps[:, 2 + t, g * P:(g + 1) * P], xbcT[:, NX + g, t * P:(t + 1) * P],
                              xbcT[:, NX + SG + g, t * P:(t + 1) * P], start=True, stop=True)
                last.then_inc(sem("cb_made"), 1)
            pe.wait_ge(sem("B_copied"), 1)
            pe.wait_ge(sem("xdec_made"), 1)
            pe.wait_ge(sem("xdt_made"), 8)
            for g in range(SG):
                mm(ps[:, 4 + g, :], Btok[:, g * P:(g + 1) * P], xdec[:, 512 * g:512 * g + 512], start=True, stop=True
                   ).then_inc(sem("state_made"), 1)

            def acs_rows(i):
                t, g = i // SG, i % SG
                if i == 0:
                    pe.wait_ge(sem("ssm_cols"), 1)
                    pe.wait_ge(sem("B_copied"), 1)
                if i == 1:
                    pe.wait_ge(sem("cb_copied"), TT)
                if i >= 2:
                    pe.wait_ge(sem("seg_made"), 8 * (i - 1))
                for b in range(2):
                    bank = ps[:, 2 * (i % 2) + b, :]
                    mm(bank, identb[:, :], over_heads(maskb[:, :], 4), start=True, stop=False)
                    for r in range(4):
                        h = 8 * g + 4 * b + r
                        last = mm(bank[:, r * P:(r + 1) * P], dA[:, t, h:h + 1].to_broadcast([P, P]), tri, start=False, stop=r == 3)
                last.then_inc(sem("acs_rows"), 1)

            def y_products(i):
                t, g = i // SG, i % SG
                pe.wait_ge(sem("MT_made"), i + 1)
                if i == 0:
                    pe.wait_ge(sem("state_copied"), SG)
                if i >= 2:
                    pe.wait_ge(sem("y_added"), i - 1)
                for r in range(8):
                    h = 8 * g + r
                    last = mm(ps[64 * (r % 2):64 * (r % 2) + 64, 4 + i % 2, (r // 2) * P:(r // 2 + 1) * P],
                              xdt[:, t, SD * h:SD * (h + 1)], MT[:, i % 2, r, :], start=True, stop=True)
                last.then_inc(sem("y_made"), 1)

            acs_rows(0)
            for i in range(TT * SG):
                if i + 1 < TT * SG:
                    acs_rows(i + 1)
                y_products(i)
            pe.wait_ge(sem("seg_made"), 8 * TT * SG)
            for q in range(4):
                b = 2 * (q % 2)
                if q >= 2:
                    pe.wait_ge(sem("yoff_added"), q - 1)
                for c in range(4):
                    j = 4 * q + c
                    mm(ps[:, b, c * P:(c + 1) * P], state[:, j * P:(j + 1) * P], xbcT[:, NX + SG + q, P:2 * P], start=True, stop=True)
                    for r in range(2):
                        last = mm(ps[64 * r:64 * r + 64, b + 1, c * P:(c + 1) * P], dA[:, 1, 2 * j + r:2 * j + r + 1].to_broadcast([P, SD]),
                                  tri, start=True, stop=True)
                last.then_inc(sem("yoff_made"), 1)
            for g in range(SG):
                pe.wait_ge(sem("ysq_made"), g + 1)
                if g == 0:
                    pe.wait_ge(sem("y_added"), TT * SG)
                for c in range(4):
                    last = mm(ps[:, 4 + g, 0:SEQ], ones[:, :], ysq[:, g % 2, c * SEQ:(c + 1) * SEQ], start=c == 0, stop=c == 3)
                last.then_inc(sem("y_ss"), 1)

            def y_ready(k):
                if k % 4 == 0:
                    pe.wait_ge(sem("y_ready"), SG if k == 0 else k // 4 + 1)

            output_projection(BASE1 + 10, 4, xbcT, y_ready)
            pe.wait_ge(sem("ln_done"), 3)
            turn(3)
            if limit < 5:
                return
            pe.wait_ge(sem("xT_copied"), 16)
            for t in range(TT):
                last = token_major(ps[:, 4, t * E:(t + 1) * E], w_rt, t)
            last.then_inc(sem("logits"), 1)
            pe.wait_ge(sem("sel_made"), 1)
            mm(ps[:, 4, 32:32 + E], tris, sel[:, 0, :], start=True, stop=True)
            mm(ps[:, 4, 40:40 + E], tris, sel[:, 1, :], start=True, stop=False)
            mm(ps[:, 4, 40:40 + E], ones[:, :], sel[:, 0, :], start=False, stop=True)
            mm(ps[:, 4, 64:64 + E], ones[:, :], sel[:, 0, :], start=True, stop=False)
            mm(ps[:, 4, 64:64 + E], ones[:, :], sel[:, 1, :], start=False, stop=True).then_inc(sem("ranks"), 1)

            def expert_pe(it):
                pe.wait_ge(sem("sel_rows_made"), it + 1)
                pe.wait_ge(sem("e_added"), 4 * it + FIRST)
                for t in range(TT):
                    last = pe.transpose(ps[:, 7, t * P:(t + 1) * P], sel_gate[:, t, :], ident)
                last.then_inc(sem("G_turned"), 1)
                pe.wait_ge(sem("e_h"), ESTEPS * it + FIRST)
                for q in range(2):
                    for k in range(4):
                        c = 4 * q + k
                        for t in range(TT):
                            last = mm(ps[:, 2 + q, k * P:(k + 1) * P], x_tok[:, t, c * P:(c + 1) * P], sel_rows[:, t, :],
                                      start=t == 0, stop=t == TT - 1)
                    last.then_inc(sem("xg_made"), 1)
                pe.wait_ge(sem("xg_lo_made"), 2 * it + 2)

                def three(out_ap, hi, lo, whi, wlo, start, stop):
                    mm(out_ap, hi, whi, start=start, stop=False)
                    mm(out_ap, hi, wlo, start=False, stop=False)
                    return mm(out_ap, lo, whi, start=False, stop=stop)

                def pieces(n, k):
                    return [w[:, n % CUT, :].rearrange("p (k n) -> p k n", k=k) for w in (w_hi, w_lo)]

                def product(j, what):
                    for half in range(PPU):
                        n = PPU * ORDER.index((j, what)) + half
                        pe.wait_ge(lo_made, PPE * it + (RAW + n + 1))
                        whi, wlo = pieces(n, 4)
                        for kk in range(4):
                            k = 4 * half + kk
                            last = three(ps[:, 2 * (j % 2) + what, :], xg_hi[:, k, :], xg_lo[:, k, :], whi[:, kk, :], wlo[:, kk, :],
                                         k == 0, k == KD - 1)
                        last.then_inc(piece_used, 1)

                def turn_h(j):
                    pe.wait_ge(sem("e_h"), ESTEPS * it + (j + 1) + FIRST)
                    pe.wait_ge(sem("ehT_made"), ESTEPS * it + j + FIRST)
                    for c in range(4):
                        last = pe.transpose(ps[:, 4, c * P:(c + 1) * P], eh[:, j % 2, c * P:(c + 1) * P], ident)
                    last.then_inc(sem("eh_turned"), 1)

                def down(j):
                    pe.wait_ge(sem("ehT_made"), ESTEPS * it + (j + 1) + FIRST)
                    for half in range(PPU):
                        n = PPU * ORDER.index((j, 2)) + half
                        pe.wait_ge(lo_made, PPE * it + (RAW + n + 1))
                        whi, wlo = pieces(n, 2)
                        for cc in range(2):
                            c = 2 * half + cc
                            for h in range(2):
                                cs = slice(512 * h, 512 * h + 512)
                                last = three(ps[:, 5 + h, :], ehT_hi[:, j % 2, c, :], ehT_lo[:, j % 2, c, :], whi[:, cc, cs],
                                             wlo[:, cc, cs], j == 0 and c == 0, j == ESTEPS - 1 and c == 3)
                        last.then_inc(piece_used, 1)

                for j in range(ESTEPS):
                    if j >= 2:
                        pe.wait_ge(sem("e_h"), ESTEPS * it + (j - 1) + FIRST)
                    product(j, 0)
                    if j:
                        turn_h(j - 1)
                    product(j, 1)
                    if j:
                        down(j - 1)
                turn_h(ESTEPS - 1)
                down(ESTEPS - 1)
                pe.wait_ge(sem("G_copied"), it + 1)
                pe.wait_ge(sem("oe_copied_dve"), it + 1)
                pe.wait_ge(sem("oe_copied_act"), it + 1)
                for q in range(2 * TT):
                    if q >= 2:
                        pe.wait_ge(sem("e_added"), 4 * it + (q - 1) + FIRST)
                    mm(ps[:, 7 if q % 2 == 0 else 4, :], G[:, q // 2, :], oe[:, 512 * (q % 2):512 * (q % 2) + 512], start=True, stop=True
                       ).then_inc(sem("e_scattered"), 1)

            pe.sem_inc(piece_used, CUT)
            pe.sem_inc(sem("xg_made"), FIRST)
            pe.sem_inc(sem("e_scattered"), FIRST)
            with pe.Fori(0, E) as e:
                expert_pe(e)
            more = pe.value_load(over[0:1, 0:1].bitcast(I32), min_val=0, max_val=SEQ)
            with pe.If(more > 0):
                with pe.Fori(0, E) as e:
                    expert_pe(e + E)


_INS = ["x", "ln_g", "ln_b", "even_w_in", "swa_sinks", "dn_conv_w", "dn_a_log", "dn_dt_bias", "dn_norm_w", "even_w_out",
        "ssm_w_in", "ssm_conv_w", "ssm_conv_b", "ssm_dt_bias", "ssm_a_log", "ssm_d", "ssm_norm_w", "ssm_w_out",
        "ffn_w_gate", "ffn_w_up", "ffn_w_down", "moe_w_router", "moe_b_router", "moe_w_gate", "moe_w_up", "moe_w_down"]


def kernel(**inputs):
    import ml_dtypes
    from concourse import bacc
    from concourse.bass_utils import run_bass_kernel_spmd

    nc = bacc.Bacc("TRN2", target_bir_lowering=False, num_devices=1)
    arrays = {name: np.ascontiguousarray(inputs[name]) for name in _INS}
    arrays["shape_consts"] = shape_constants()
    arrays["shape_consts_b"] = shape_constants_b(ml_dtypes.bfloat16)
    dram = {}
    for name, a in arrays.items():
        dram[name] = nc.dram_tensor(f"in_{name}", a.shape, mybir.dt.from_np(a.dtype), kind="ExternalInput").ap()
    out = nc.dram_tensor("out", (1, SEQ, D), F32, kind="ExternalOutput").ap()
    build(nc, dram, out)
    r = run_bass_kernel_spmd(nc, [{f"in_{name}": a for name, a in arrays.items()}], core_ids=[0])
    return r.results[0]["out"]
```

```python
from contextlib import ExitStack

import numpy as np

import concourse.bass as bass
from concourse import mybir

ALU = mybir.AluOpType
ACT = mybir.ActivationFunctionType
F32 = mybir.dt.float32
BF16 = mybir.dt.bfloat16
F32R = mybir.dt.float32r
I32 = mybir.dt.int32
U32 = mybir.dt.uint32
AX = mybir.AxisListType.X

P = 128
SEQ = 256
TT = SEQ // P
D = 1024
KD = D // P
DEPTH = 2
ALPHA = (2 * DEPTH) ** 0.25
LN_EPS, RMS_EPS = 1e-5, 1e-6
AH, AKV, AD = 8, 2, 64
ROPE = AD // 4
HALF = ROPE // 2
THETA = 500000.0
DH, DD = 4, 128
CONV = 4
NDN = 3 * DH
LEVELS = 7
Q0, K0 = 0, AH * AD
B0 = K0 + 2 * AKV * AD
G0 = B0 + NDN * P
BA0 = G0 + DH * DD
SI = 2048
SH, SD, SG, SN = 32, 64, 4, 128
NX = SI // P
NXBC = NX + 2 * SG
F = 2816
FW = 256
FSTEPS = F // FW
E = 8
EF = 3584
EW = 512
ESTEPS = EF // EW
NEG = -1e30

FIRST = 1

SLOT = 4096
RING = 4
PIECE = 2048
RAW = 7
CUT = 3
RAW_D = 6
PPU = 2
PPE = 3 * ESTEPS * PPU
assert PPE % RAW == 0 and PPE % CUT == 0
ORDER = [(0, 0), (0, 1)]
for _j in range(1, ESTEPS):
    ORDER += [(_j, 0), (_j, 1), (_j - 1, 2)]
ORDER += [(ESTEPS - 1, 2)]


NFFN = 3 * FSTEPS
PROJ = []
for _g in range(NX // 4):
    PROJ += [(0, 3 * _g), (0, 3 * _g + 1), (1, 2 * _g), (0, 3 * _g + 2), (1, 2 * _g + 1)]
assert len(PROJ) == (NXBC + NX) // 2 and sum(1 - k for k, _ in PROJ) == NXBC // 2
NPRE = NFFN + len(PROJ)


def last_piece(step, what):
    return PPU * ORDER.index((step, what)) + PPU - 1



C_ID, C_TRI, C_TRIS = 0, P, 2 * P
C_LVL = 3 * P
C_AM = C_LVL + LEVELS * P
C_COS = C_AM + 2 * P
C_SIN = C_COS + TT * HALF
C_IOTA = C_SIN + TT * HALF
C_I8 = C_IOTA + P
C_W = C_I8 + E


def shape_constants():
    c = np.zeros((P, C_W), np.float32)
    r = np.arange(P)
    c[:, C_ID:C_ID + P] = np.eye(P)
    c[:, C_TRI:C_TRI + P] = r[:, None] <= r[None, :]
    c[:, C_TRIS:C_TRIS + P] = r[:, None] < r[None, :]
    for lv in range(LEVELS):
        b = 1 << lv
        same = (r[:, None] // (2 * b)) == (r[None, :] // (2 * b))
        c[:, C_LVL + lv * P:C_LVL + (lv + 1) * P] = same & ((r[None, :] // b) % 2 == 1) & ((r[:, None] // b) % 2 == 0)
    c[:, C_AM:C_AM + P] = np.where(r[None, :] > r[:, None], 0, NEG)
    c[:, C_AM + P:C_AM + 2 * P] = np.where(r[None, :] <= r[:, None], 0, NEG)
    inv = THETA ** (-np.arange(HALF, dtype=np.float64) / HALF)
    for t in range(TT):
        ang = (r[:, None] + t * P) * inv[None, :]
        c[:, C_COS + t * HALF:C_COS + (t + 1) * HALF] = np.cos(ang)
        c[:, C_SIN + t * HALF:C_SIN + (t + 1) * HALF] = np.sin(ang)
    c[:, C_IOTA:C_IOTA + P] = r[None, :]
    c[:, C_I8:C_I8 + E] = np.arange(E)[None, :]
    return c


def shape_constants_b(dtype):
    r = np.arange(P)
    return np.concatenate([np.eye(P), np.where(r[:, None] <= r[None, :], 0, NEG)], axis=1).astype(dtype)


def build(nc, dram, out, limit=99):
    with ExitStack() as ctx:
        def sb(name, shape, dt=F32):
            return ctx.enter_context(nc.sbuf_tensor(name, [P] + shape, dt))

        sems = {}

        def sem(name):
            if name not in sems:
                sems[name] = ctx.enter_context(nc.semaphore(name))
            return sems[name]

        ps = ctx.enter_context(nc.psum_tensor("ps", [P, 8, 512], F32))

        const = sb("const", [C_W])
        identb = sb("identb", [P], BF16)
        maskb = sb("maskb", [P], BF16)
        zerob = sb("zerob", [512], BF16)
        ones = sb("ones", [P])
        x_tok = sb("x_tok", [TT, D])
        xT = sb("xT", [KD, SEQ])
        ln_gb = sb("ln_gb", [2, D])
        prow_a = sb("prow_a", [P])
        prow_b = sb("prow_b", [P])
        pcol = sb("pcol", [2 * P])
        w_ba = sb("w_ba", [KD, 2 * DH])
        w_dt = sb("w_dt", [KD, SH])
        w_rt = sb("w_rt", [KD, E])
        sinks = sb("sinks", [AH])
        dn_al = sb("dn_al", [DH])
        dn_dtb = sb("dn_dtb", [DH])
        dn_nw = sb("dn_nw", [DD])
        ssm_al = sb("ssm_al", [SH])
        ssm_dtb = sb("ssm_dtb", [SH])
        ssm_db = sb("ssm_db", [SH])
        dcol = sb("dcol", [NX])
        brt = sb("brt", [E])
        stats = sb("stats", [TT, 2, 6])
        mv = sb("mv", [TT, 2])
        rstd = sb("rstd", [TT])
        nhalf = sb("nhalf", [TT])
        eps_rms = sb("eps_rms", [1])
        with ExitStack() as early:
            ring = early.enter_context(nc.sbuf_tensor("ring", [P, RING * SLOT], F32))
            arena = early.enter_context(nc.sbuf_tensor("arena", [P, 27200], F32))
        raw = sb("raw", [RAW, PIECE])
        w_hi = sb("w_hi", [CUT, PIECE], F32R)
        w_lo = sb("w_lo", [CUT, PIECE], F32R)
        xT_hi = sb("xT_hi", [KD, SEQ], F32R)
        xT_lo = sb("xT_lo", [KD, SEQ], F32R)
        xg_hi = sb("xg_hi", [KD, P], F32R)
        xg_lo = sb("xg_lo", [KD, P], F32R)
        ehT_hi = sb("ehT_hi", [2, 4, P], F32R)
        ehT_lo = sb("ehT_lo", [2, 4, P], F32R)
        esg = sb("esg", [2, EW])
        eh = sb("eh", [2, EW])
        sel_rows = sb("sel_rows", [TT, P])
        sel_gate = sb("sel_gate", [TT, P])
        G = sb("G", [TT, P])
        oe = sb("oe", [D])
        yacc = sb("yacc", [TT, D])
        lg = sb("lg", [TT, E])
        top8 = sb("top8", [TT, 8])
        idx8 = sb("idx8", [TT, 8])
        idxf = sb("idxf", [TT, 2])
        oh1 = sb("oh1", [TT, E])
        oh2 = sb("oh2", [TT, E])
        dm = sb("dm", [TT, 1])
        g1 = sb("g1", [TT, 1])
        g2 = sb("g2", [TT, 1])
        comb = sb("comb", [TT, E])
        sel = sb("sel", [TT, E])
        rank = sb("rank", [TT, E])
        rank2 = sb("rank2", [TT, E])
        cnt = sb("cnt", [1])
        over = sb("over", [1])

        ident = const[:, C_ID:C_ID + P]
        tri = const[:, C_TRI:C_TRI + P]
        tris = const[:, C_TRIS:C_TRIS + P]
        iota = const[:, C_IOTA:C_IOTA + P]
        iota8 = const[:, C_I8:C_I8 + E]

        def ssm_tap(k, j):
            return pcol[:, k * NXBC + j:k * NXBC + j + 1]

        def dn_tap(k, j):
            return pcol[:, P + k * NDN + j:P + k * NDN + j + 1]

        def ssm_nw(j):
            return pcol[:, P + CONV * NDN + j:P + CONV * NDN + j + 1]

        def ssm_cb(j):
            return pcol[:, P + CONV * NDN + NX + j:P + CONV * NDN + NX + j + 1]

        CUT_END = RAW * PIECE + 2 * CUT * PIECE + 2 * KD * SEQ - RING * SLOT

        top = [0]

        def take(*shape, at=None):
            n = int(np.prod(shape))
            if at is not None:
                top[0] = at
            a = arena[:, top[0]:top[0] + n]
            top[0] += n
            assert top[0] <= 27200, top[0]
            if len(shape) == 2:
                a = a.rearrange("p (a b) -> p a b", b=shape[1])
            if len(shape) == 3:
                a = a.rearrange("p (a b c) -> p a b c", b=shape[1], c=shape[2])
            return a

        dnT = take(NDN, SEQ, at=CUT_END)
        qkv = take(TT, 768)
        gate = take(TT, DH * DD)
        mixT = take(KD, SEQ)
        rt = take(4, TT * 10 * HALF)
        ba = take(TT, 2 * DH)
        beta = take(TT, DH)
        gdn = take(TT, DH)
        zdn = take(TT, DH)
        adn = take(TT, DH)
        e2dn = take(TT, DH)
        ebdn = take(TT, DH)
        eadn = take(DH)
        mx = take(2, AH)
        nmx = take(2, AH)
        sdx = take(2, AH)
        den = take(2, AH)
        rden = take(2, AH)
        ngc = take(TT, DH)
        ddk = take(DH)
        dke = take(DH)
        egc1 = take(DH)
        bege = take(DH)
        oss = take(TT * DH)
        orn = take(TT * DH)
        pT = take(3 * AH, P)
        qT = take(4, SEQ)
        s = take(AH, 384, at=0)
        kT = take(SEQ)
        sq = take(2048, at=0)
        rn = take(2048)
        decT = take(8, P)
        attnT = take(8, P)
        AT = take(8, P)
        LT = take(2, 8, P)
        X = take(8, P)
        XT = take(8, P)
        Pm = take(8, P)
        vb = take(8, P)
        kdec = take(4, P)
        kbe = take(4, P)
        u = take(8, P, at=0)
        wT = take(4, P)
        S1 = take(4, P)
        vnew = take(4, P)
        o = take(8, P, at=4096 + 3072)
        osq = take(8, P)

        sg = take(2, 512, at=20480)
        hT = take(512)

        hT_hi = ehT_hi[:, 0].rearrange("p k t -> p (k t)").rearrange("p (k t) -> p k t", k=2)
        hT_lo = ehT_lo[:, 0].rearrange("p k t -> p (k t)").rearrange("p (k t) -> p k t", k=2)

        xdt = take(TT, SI, at=0)
        xdec = take(SI)
        Btok = take(SG * SN)
        state = take(SI)
        seg = take(2, 8, P)
        MT = take(2, 8, P)
        cb = take(8, P)
        xbcT = take(NXBC, SEQ, at=CUT_END)
        zT = take(NX, SEQ)
        er = take(2, 512)
        yo = take(2, 512)
        ysq = MT.rearrange("p a b c -> p a (b c)")
        yrn = seg[:, 0].rearrange("p a b -> p (a b)").rearrange("p (g t) -> p g t", g=SG)
        sz = take(TT, SH)
        sdt = take(TT, SH)
        saz = take(TT, SH)
        se2 = take(TT, SH)
        dA = take(TT, SH)
        sea = take(SH)
        nacs = take(TT, SH)
        sdd = take(SH)
        sdec = take(SH)

        def bc(ap, n):
            return ap.unsqueeze(2).to_broadcast([P, ap.shape[1], n])

        def over_heads(ap, n):
            return ap.unsqueeze(1).to_broadcast([P, n, ap.shape[1]])

        def slot(i):
            return ring[:, i * SLOT:(i + 1) * SLOT]

        w_in0, w_out0 = dram["even_w_in"][0], dram["even_w_out"][0]
        w_in1, w_out1 = dram["ssm_w_in"][0], dram["ssm_w_out"][0]

        def cols(w, a, n):
            return w.rearrange("(k p) n -> p k n", p=P)[:, :, a:a + n]

        def rows(w, a, n):
            return w.rearrange("(k p) n -> p k n", p=P)[:, a:a + n, :]

        units0 = [(cols(w_in0, B0 + 512 * i, 512), 512) for i in range(3)]
        units0 += [(cols(w_in0, G0, 512), 512), (cols(w_in0, Q0, 512), 512), (cols(w_in0, K0, 256), 256)]
        units0 += [(rows(w_out0, 4 * i, 4), D) for i in range(2)]
        NU0 = len(units0)
        units1 = [(rows(w_out1, 4 * i, 4), D) for i in range(4)]
        BASE1 = NU0
        assert NU0 % RING == 0
        loaded = [sem(f"slot{i}_loaded") for i in range(RING)]
        raw_loaded = [sem(f"raw{i}_loaded") for i in range(RAW)]
        lo_made = sem("lo_made")
        piece_used = sem("piece_used")
        d_lo_made = sem("dense_lo_made")
        d_piece_used = sem("dense_piece_used")

        def raw_before(i):
            return 16 * len(range(i, NPRE, RAW_D)) if i < RAW_D else 0

        block = ctx.enter_context(nc.Block())

        @block.sync
        def _(sp):
            sp.dma_start(x_tok[:, :, :], dram["x"][0].rearrange("(t p) d -> p t d", p=P)).then_inc(sem("x_loaded"), 16)
            sp.dma_start(const[:, :], dram["shape_consts"]).then_inc(sem("x_loaded"), 16)

            def fill(dst, src, s_):
                k = src.shape[1] // 2
                sp.dma_start(dst[:, 0:k, :], src[:, 0:k, :]).then_inc(s_, 16)
                sp.dma_start(dst[:, k:2 * k, :], src[:, k:2 * k, :]).then_inc(s_, 16)

            done0 = [("dn_proj", 2), ("dn_proj", 4), ("dn_proj", 6), ("gate_proj", 2), ("q_proj", 2), ("kv_proj", 2),
                     ("out_proj", 1), ("out_proj", 2)]
            def unit(n, src, width, before):
                if before:
                    sp.wait_ge(sem(before[0]), before[1])
                k = src.shape[1]
                dst = slot(n % RING)[:, 0:k * width].rearrange("p (k n) -> p k n", k=k)
                fill(dst, src, loaded[n % RING])

            for n, (src, width) in enumerate(units0):
                unit(n, src, width, done0[n - RING] if n >= RING else None)
            if limit < 2:
                return
            wg, wu, wd = dram["ffn_w_gate"][0], dram["ffn_w_up"][0], dram["ffn_w_down"][0]

            def piece(n, i, src):
                sp.wait_ge(d_lo_made, n + 1)
                sp.dma_start(raw[:, i, :].rearrange("p (k n) -> p k n", k=src.shape[1]), src).then_inc(raw_loaded[i], 16)

            def gu_piece(w, step):
                return w.rearrange("(k p) n -> p k n", p=P)[:, :, bass.ds(step * FW, FW)]

            def d_piece(step):
                return wd.rearrange("(s k p) n -> s p k n", k=2, p=P)[step]

            sp.wait_ge(sem("q_proj"), 2)
            sp.sem_inc(d_lo_made, 2)
            piece(0, 0, gu_piece(wg, 0))
            piece(1, 1, gu_piece(wu, 0))
            sp.wait_ge(sem("kv_proj"), 2)
            sp.sem_inc(d_lo_made, 2)
            sp.wait_ge(sem("out_proj"), 1)
            sp.sem_inc(d_lo_made, 2)
            with sp.Fori(0, FSTEPS // 2) as i:
                piece(6 * i + 2, 2, gu_piece(wg, 2 * i + 1))
                piece(6 * i + 3, 3, gu_piece(wu, 2 * i + 1))
                piece(6 * i + 4, 4, d_piece(2 * i))
                piece(6 * i + 5, 5, gu_piece(wg, 2 * i + 2))
                piece(6 * i + 6, 0, gu_piece(wu, 2 * i + 2))
                piece(6 * i + 7, 1, d_piece(2 * i + 1))
            piece(NFFN - 1, (NFFN - 1) % RAW_D, d_piece(FSTEPS - 1))
            if limit < 3:
                return
            for m, (kind, pair) in enumerate(PROJ):
                n = NFFN + m
                piece(n, n % RAW_D, cols(w_in1, (SI if kind == 0 else 0) + 2 * P * pair, 2 * P))
            for i, (src, width) in enumerate(units1):
                sp.wait_ge(d_lo_made, RAW_D + NPRE)
                if i == RING - 1:
                    sp.wait_ge(d_piece_used, CUT + NPRE)
                unit(BASE1 + i, src, width, None)
            if limit < 5:
                return

            eg, eu, ed = dram["moe_w_gate"][0], dram["moe_w_up"][0], dram["moe_w_down"][0]
            for i in range(RING):
                sp.wait_ge(sem("out_proj"), 2 + i + 1)
                sp.sem_inc(lo_made, min(2, RAW - 2 * i))

            def expert_loads(e, it):
                for n in range(PPE):
                    (j, what), half = ORDER[n // PPU], n % PPU
                    sp.wait_ge(lo_made, PPE * it + (n + 1))
                    i = n % RAW
                    if what < 2:
                        src = (eg, eu)[what][e].rearrange("(k p) n -> p k n", p=P)[:, 4 * half:4 * half + 4, EW * j:EW * (j + 1)]
                    else:
                        src = ed[e].rearrange("(k p) n -> p k n", p=P)[:, 4 * j + 2 * half:4 * j + 2 * half + 2, :]
                    sp.dma_start(raw[:, i, :].rearrange("p (k n) -> p k n", k=src.shape[1]), src).then_inc(raw_loaded[i], 16)

            with sp.Fori(0, E) as e:
                expert_loads(e, e)
            sp.wait_ge(sem("overflow_known"), 1)
            more = sp.value_load(over[0:1, 0:1].bitcast(I32), min_val=0, max_val=SEQ)
            with sp.If(more > 0):
                with sp.Fori(0, E) as e:
                    expert_loads(e, e + E)

        @block.gpsimd
        def _(pool):
            pool.memset(ones[:, :], 1.0).then_inc(sem("pool_set"), 1)
            pool.memset(zerob[:, :], 0.0).then_inc(sem("pool_set"), 1)
            pool.memset(nhalf[:, :], -0.5).then_inc(sem("pool_set"), 1)
            pool.wait_ge(sem("pool_set"), 3)
            for n in range(2 * DEPTH):
                if n >= limit:
                    break
                for t in range(TT):
                    pool.wait_ge(sem("ln_var"), TT * n + t + 1)
                    pool.tensor_tensor(rstd[:, t:t + 1], mv[:, t, 1:2], nhalf[:, t:t + 1], ALU.pow).then_inc(sem("ln_rstd"), 1)

        @block.scalar
        def _(act):
            def small(dst, src, loaded_="params_loaded"):
                act.dma_start(dst, src).then_inc(sem(loaded_), 16)

            def row(name, *idx):
                a = dram[name]
                for i in idx:
                    a = a[i]
                return a.partition_broadcast(P)

            small(prow_b[0:CONV * NDN, :], dram["dn_conv_w"][0].rearrange("k (j p) -> (k j) p", p=P), "taps_loaded")
            small(prow_b[CONV * NDN:CONV * NDN + NX, :], dram["ssm_norm_w"][0].rearrange("(j p) -> j p", p=P), "taps_loaded")
            small(prow_b[CONV * NDN + NX:CONV * NDN + NX + NXBC, :], dram["ssm_conv_b"][0].rearrange("(j p) -> j p", p=P), "taps_loaded")
            small(prow_a[0:CONV * NXBC, :], dram["ssm_conv_w"][0].rearrange("k (j p) -> (k j) p", p=P), "taps_loaded")
            small(w_ba[:, :, :], cols(w_in0, BA0, 2 * DH))
            small(identb[:, :], dram["shape_consts_b"][:, 0:P])
            small(maskb[:, :], dram["shape_consts_b"][:, P:2 * P])
            small(sinks[:, :], row("swa_sinks", 0))
            small(dn_al[:, :], row("dn_a_log", 0))
            small(dn_dtb[:, :], row("dn_dt_bias", 0))
            small(dn_nw[:, :], row("dn_norm_w", 0))
            small(w_dt[:, :, :], cols(w_in1, SI + NXBC * P, SH))
            small(ssm_al[:, :], row("ssm_a_log", 0))
            small(ssm_dtb[:, :], row("ssm_dt_bias", 0))
            small(ssm_db[:, :], row("ssm_d", 0))
            small(w_rt[:, :, :], cols(dram["moe_w_router"][0], 0, E))
            small(brt[:, :], row("moe_b_router", 0))

            def load_ln(n):
                if n:
                    act.wait_ge(sem("ln_done"), TT * n)
                act.dma_start(ln_gb[:, 0], dram["ln_g"][n // 2][n % 2].partition_broadcast(P)).then_inc(sem("ln_loaded"), 16)
                act.dma_start(ln_gb[:, 1], dram["ln_b"][n // 2][n % 2].partition_broadcast(P)).then_inc(sem("ln_loaded"), 16)

            def turn_high(n):
                for b in range(4):
                    t, q = b // 2, b % 2
                    act.wait_ge(sem("x_turned"), 4 * n + b + 1)
                    act.copy(xT_hi[:, 4 * q:4 * q + 4, t * P:(t + 1) * P], ps[:, b, :].rearrange("p (k t) -> p k t", k=4)
                             ).then_inc(sem("xT_hi_made"), 1)

            def dense_high(n, i, c, rounds):
                act.wait_ge(raw_loaded[i], 16 * rounds)
                act.wait_ge(d_piece_used, n + 1)
                act.copy(w_hi[:, c, :], raw[:, i, :]).then_inc(sem("dense_hi_made"), 1)

            def turn_copies(n):
                for b in range(3):
                    t, q = b // 2, b % 2
                    act.wait_ge(sem("x_turned"), 4 * n + b + 1)
                    act.copy(xT[:, 4 * q:4 * q + 4, t * P:(t + 1) * P], ps[:, b, :].rearrange("p (k t) -> p k t", k=4)
                             ).then_inc(sem("xT_copied"), 1)

            act_step = [0]

            def link(ins):
                act_step[0] += 1
                ins.then_inc(sem("act_step"), 1)
                act.wait_ge(sem("act_step"), act_step[0])

            turn_copies(0)
            for q in range(NDN // 2):
                act.wait_ge(sem("dn_conv"), q + 1)
                act.activation(dnT[:, 2 * q:2 * q + 2, :], dnT[:, 2 * q:2 * q + 2, :], ACT.Silu).then_inc(sem("dn_silu"), 1)
            load_ln(0)
            for t in range(TT):
                act.wait_ge(sem("gate_proj"), t + 1)
                act.activation(gate[:, t, :], ps[:, 4 + t, :], ACT.Silu).then_inc(sem("gate_silu"), 1)
            for b in range(4):
                act.wait_ge(sem("dn_ss"), b + 1)
                link(act.activation(rn[:, 512 * b:512 * b + 512], ps[:, b, :], ACT.Ln, bias=eps_rms[:, 0:1]))
                act.activation(rn[:, 512 * b:512 * b + 512], rn[:, 512 * b:512 * b + 512], ACT.Exp, scale=-0.5).then_inc(sem("dn_rn"), 1)
            act.wait_ge(sem("params_loaded"), 16 * 13)
            act.activation(eadn[:, :], dn_al[:, :], ACT.Exp).then_inc(sem("dn_eb"), 1)
            act.wait_ge(sem("dn_z"), 1)
            act.activation(adn[:, :, :], adn[:, :, :], ACT.Exp, scale=-1.0).then_inc(sem("dn_e1"), 1)
            act.activation(ebdn[:, :, :], ba[:, :, 0:DH], ACT.Exp, scale=-1.0).then_inc(sem("dn_eb"), 1)
            act.wait_ge(sem("dn_e1"), 1)
            act.activation(e2dn[:, :, :], adn[:, :, :], ACT.Ln, bias=1.0).then_inc(sem("dn_e2"), 1)
            act.wait_ge(sem("dn_cols"), 1)
            act.activation(dke[:, :], ddk[:, :], ACT.Exp).then_inc(sem("dn_dke"), 1)
            act.activation(egc1[:, :], ngc[:, 1, :], ACT.Exp, scale=-1.0).then_inc(sem("dn_dke"), 1)
            for t in range(TT):
                act.wait_ge(sem("dn_gcrow"), t + 1)
                for h in range(DH):
                    act.activation(decT[:, t * DH + h, :], ps[:, t, h * P:(h + 1) * P], ACT.Exp, bias=ngc[:, t, h:h + 1]
                                   ).then_inc(sem("dn_dec"), 1)

            def exponentials(n):
                act.wait_ge(sem("att_max"), 1)
                for h in range(AH):
                    seg_ = s[:, h, 0:256] if n == 1 else s[:, h, 256:384]
                    act.activation(seg_, seg_, ACT.Exp, bias=nmx[:, n, h:h + 1], accum_out=den[:, n, h:h + 1]
                                   ).then_inc(sem("att_exp"), 1)
                if n == 1:
                    act.activation(sdx[:, :, :], sdx[:, :, :], ACT.Exp).then_inc(sem("att_exp"), 1)

            def copy_p(b):
                act.wait_ge(sem("p_turned"), b + 1)
                act.copy(pT[:, 4 * b:4 * b + 4, :], ps[:, 7, :].rearrange("p (k t) -> p k t", k=4)).then_inc(sem("pT_copied_act"), 1)

            def copy_mix(b):
                act.wait_ge(sem("att_out"), b + 1)
                act.copy(mixT[:, 2 * b:2 * b + 2, :], ps[:, 6 + b, :].rearrange("p (k t) -> p k t", k=2)).then_inc(sem("mix_att"), 1)

            def attention(lv, half):
                at = (lv, half)
                if at == (3, 0):
                    exponentials(0)
                elif at == (3, 1):
                    exponentials(1)
                elif at == (4, 1):
                    copy_p(1)
                elif at == (5, 0):
                    copy_p(3)
                elif at == (5, 1):
                    copy_p(5)
                elif at == (6, 0):
                    copy_mix(0)
                elif at == (6, 1):
                    copy_mix(1)
            for lv in range(1, LEVELS):
                for t in range(TT):
                    act.wait_ge(sem("inv_P"), 2 * lv + t + 1)
                    act.copy(Pm[:, t * DH:(t + 1) * DH, :], ps[:, t, :].rearrange("p (h c) -> p h c", h=DH)).then_inc(sem("inv_P_copied"), 1)
                attention(lv, 0)
                attention(lv, 1)
            act.wait_ge(sem("dn_w"), 1)
            act.copy(wT[:, :, :], ps[:, 2, :].rearrange("p (h c) -> p h c", h=DH)).then_inc(sem("dn_w_copied"), 1)
            act.wait_ge(sem("dn_S"), 1)
            act.copy(S1[:, :, :], ps[:, 4, :].rearrange("p (h c) -> p h c", h=DH)).then_inc(sem("dn_S_copied"), 1)
            act.wait_ge(sem("dn_oss"), 1)
            link(act.activation(orn[:, :], oss[:, :], ACT.Ln, bias=eps_rms[:, 0:1], scale=1.0 / DD))
            act.activation(orn[:, :], orn[:, :], ACT.Exp, scale=-0.5).then_inc(sem("dn_orn"), 1)
            act.wait_ge(sem("o_turned"), 2)
            act.copy(mixT[:, 4:8, P:2 * P], ps[:, 1, :].rearrange("p (h c) -> p h c", h=DH)).then_inc(sem("mix_dn"), 1)
            if limit < 2:
                load_ln(1)
                act.wait_ge(sem("ln_loaded"), 64)
                return
            act.wait_ge(sem("out_proj"), 2)
            for n in range(CUT):
                dense_high(n, n, n, 1)
            load_ln(1)
            turn_high(1)

            def ffn_silu(b, step):
                act.wait_ge(d_piece_used, 3 * step + (CUT + 2))
                act.activation(sg[:, b, :], ps[:, 2 * b, :], ACT.Silu).then_inc(sem("ffn_silu"), 1)

            with act.Fori(0, FSTEPS // 2) as i:
                dense_high(6 * i + 3, 3, 0, i + 1)
                ffn_silu(0, 2 * i)
                dense_high(6 * i + 4, 4, 1, i + 1)
                dense_high(6 * i + 5, 5, 2, i + 1)
                dense_high(6 * i + 6, 0, 0, i + 2)
                ffn_silu(1, 2 * i + 1)
                dense_high(6 * i + 7, 1, 1, i + 2)
                dense_high(6 * i + 8, 2, 2, i + 2)
            ffn_silu(0, FSTEPS - 1)
            if limit < 3:
                load_ln(2)
                act.wait_ge(sem("ln_loaded"), 96)
                return
            for n in range(NFFN, NFFN + CUT):
                dense_high(n, n % RAW_D, n % CUT, n // RAW_D + 1)
            load_ln(2)
            turn_high(2)
            for m, (kind, q) in enumerate(PROJ):
                n = NFFN + m + CUT
                if n < NPRE:
                    dense_high(n, n % RAW_D, n % CUT, n // RAW_D + 1)
                if kind == 0:
                    act.wait_ge(sem("ssm_conv"), q + 1)
                    for j in (2 * q, 2 * q + 1):
                        act.activation(xbcT[:, j, :], xbcT[:, j, :], ACT.Silu, bias=ssm_cb(j)).then_inc(sem("ssm_silu"), 1)
                else:
                    act.wait_ge(d_piece_used, CUT + NFFN + m + 1)
                    act.activation(zT[:, 2 * q:2 * q + 2, :], ps[:, 4 + q % 4, :].rearrange("p (k t) -> p k t", k=2), ACT.Silu
                                   ).then_inc(sem("z_silu"), 1)
            act.wait_ge(sem("ssm_z"), 1)
            link(act.activation(saz[:, :, :], saz[:, :, :], ACT.Exp, scale=-1.0))
            act.activation(se2[:, :, :], saz[:, :, :], ACT.Ln, bias=1.0).then_inc(sem("ssm_sp"), 1)
            act.activation(sea[:, :], ssm_al[:, :], ACT.Exp).then_inc(sem("ssm_sp"), 1)
            act.wait_ge(sem("B_turned"), 1)
            act.copy(Btok[:, :], ps[:, 0, :]).then_inc(sem("B_copied"), 1)
            act.wait_ge(sem("ssm_cols"), 1)
            act.activation(sdec[:, :], sdd[:, :], ACT.Exp).then_inc(sem("ssm_dec"), 1)
            for t in range(TT):
                act.wait_ge(sem("cb_made"), t + 1)
                act.copy(cb[:, 4 * t:4 * t + 4, :], ps[:, 2 + t, :].rearrange("p (g c) -> p g c", g=SG)).then_inc(sem("cb_copied"), 1)
            for g in range(SG):
                act.wait_ge(sem("state_made"), g + 1)
                act.copy(state[:, 512 * g:512 * g + 512], ps[:, 4 + g, :]).then_inc(sem("state_copied"), 1)
            for i in range(TT * SG):
                t, g = i // SG, i % SG
                act.wait_ge(sem("acs_rows"), i + 1)
                if i >= 2:
                    act.wait_ge(sem("MT_made"), i - 1)
                for r in range(8):
                    h = 8 * g + r
                    act.activation(seg[:, i % 2, r, :], ps[:, 2 * (i % 2) + r // 4, (r % 4) * P:(r % 4 + 1) * P], ACT.Exp,
                                   bias=nacs[:, t, h:h + 1]).then_inc(sem("seg_made"), 1)
            for q in range(4):
                act.wait_ge(sem("yoff_made"), q + 1)
                if q >= 2:
                    act.wait_ge(sem("yoff_added"), q - 1)
                act.activation(er[:, q % 2, :], ps[:, 1 + 2 * (q % 2), :], ACT.Exp).then_inc(sem("er_made"), 1)
            for g in range(SG):
                act.wait_ge(sem("y_ss"), g + 1)
                link(act.activation(yrn[:, g, :], ps[:, 4 + g, 0:SEQ], ACT.Ln, bias=eps_rms[:, 0:1], scale=1.0 / (SI // SG)))
                act.activation(yrn[:, g, :], yrn[:, g, :], ACT.Exp, scale=-0.5).then_inc(sem("y_rn"), 1)
            load_ln(3)
            turn_copies(3)
            if limit < 5:
                act.wait_ge(sem("ln_loaded"), 128)
                return
            act.wait_ge(sem("rt_dm"), 1)
            act.activation(g1[:, :, :], dm[:, :, :], ACT.Exp).then_inc(sem("rt_e"), 1)

            def expert_act(it):
                def cut_high(n):
                    i = n % RAW
                    act.wait_ge(raw_loaded[i], 16 * (PPE // RAW) * it + (16 * (n // RAW + 1) + raw_before(i)))
                    act.wait_ge(piece_used, PPE * it + (n + 1))
                    act.copy(w_hi[:, n % CUT, :], raw[:, i, :]).then_inc(sem("hi_made"), 1)

                def silu(j):
                    act.wait_ge(piece_used, PPE * it + (CUT + last_piece(j, 1) + 1))
                    if j >= 2:
                        act.wait_ge(sem("e_h"), ESTEPS * it + (j - 1) + FIRST)
                    else:
                        act.wait_ge(sem("e_h"), ESTEPS * it + FIRST)
                    act.activation(esg[:, j % 2, :], ps[:, 2 * (j % 2), :], ACT.Silu).then_inc(sem("e_silu"), 1)

                def turned(j):
                    act.wait_ge(sem("eh_turned"), ESTEPS * it + (j + 1))
                    act.copy(ehT_hi[:, j % 2], ps[:, 4, :].rearrange("p (k t) -> p k t", k=4)).then_inc(sem("ehT_hi_made"), 1)

                after = {}
                for j in range(ESTEPS):
                    after.setdefault(min(last_piece(j, 1) + 2, PPE - 1), []).append((silu, j))
                for j in range(ESTEPS - 1):
                    after.setdefault(min(last_piece(j + 1, 0) + 2, PPE - 1), []).append((turned, j))
                after.setdefault(PPE - 1, []).append((turned, ESTEPS - 1))
                for n in range(CUT):
                    cut_high(n)
                for q in range(2):
                    act.wait_ge(sem("xg_made"), 2 * it + q + 1 + FIRST)
                    act.copy(xg_hi[:, 4 * q:4 * q + 4, :], ps[:, 2 + q, :].rearrange("p (k t) -> p k t", k=4)
                             ).then_inc(sem("xg_hi_made"), 1)
                for n in range(CUT, PPE):
                    cut_high(n)
                    for do, j in after.get(n, ()):
                        do(j)
                act.wait_ge(piece_used, PPE * it + (CUT + PPE))
                act.copy(oe[:, 512:1024], ps[:, 6, :]).then_inc(sem("oe_copied_act"), 1)

            with act.Fori(0, E) as e:
                expert_act(e)
            act.wait_ge(sem("overflow_known"), 1)
            more = act.value_load(over[0:1, 0:1].bitcast(I32), min_val=0, max_val=SEQ)
            with act.If(more > 0):
                with act.Fori(0, E) as e:
                    expert_act(e + E)
            for t in range(TT):
                act.wait_ge(sem("ln_done"), TT * 3 + t + 1)
                act.dma_start(out[0, t * P:(t + 1) * P, :], x_tok[:, t, :]).then_inc(sem("out_stored"), 16)
            act.wait_ge(sem("out_stored"), 16 * TT)

        @block.vector
        def _(dve):
            step = [0]

            def link(ins):
                step[0] += 1
                ins.then_inc(sem("dve_step"), 1)
                dve.wait_ge(sem("dve_step"), step[0])

            TTO, TS, STT = dve.tensor_tensor, dve.tensor_scalar, dve.scalar_tensor_tensor

            def four(ap):
                return ap.rearrange("p (k t) -> p k t", k=4)

            def turn_copies(n):
                dve.wait_ge(sem("x_turned"), 4 * n + 4)
                dve.tensor_copy(xT[:, 4:8, P:2 * P], four(ps[:, 3, :])).then_inc(sem("xT_copied"), 1)

            def turn_low(n):
                for b in range(4):
                    t, q = b // 2, b % 2
                    ks = slice(4 * q, 4 * q + 4)
                    dve.wait_ge(sem("xT_hi_made"), 4 * (n - 1) + b + 1)
                    TTO(xT_lo[:, ks, t * P:(t + 1) * P], four(ps[:, b, :]), xT_hi[:, ks, t * P:(t + 1) * P].bitcast(F32),
                        ALU.subtract).then_inc(sem("xT_lo_made"), 1)

            def dense_low(n, i, c):
                dve.wait_ge(sem("dense_hi_made"), n + 1)
                TTO(w_lo[:, c, :], raw[:, i, :], w_hi[:, c, :].bitcast(F32), ALU.subtract).then_inc(d_lo_made, 1)

            def layer_norm(n, ready, add=True):
                dve.wait_ge(sem("ln_loaded"), 32 * (n + 1))
                for t in range(TT):
                    xt = x_tok[:, t, :]
                    dve.wait_ge(*ready[t])
                    if add:
                        halves = xt.rearrange("p (b n) -> p b n", b=2)
                        link(STT(halves, halves, ALPHA, ps[:, 4 + 2 * t:6 + 2 * t, :], ALU.mult, ALU.add))
                    dve.bn_stats(stats[:, t, 0, :], xt[:, 0:512])
                    link(dve.bn_stats(stats[:, t, 1, :], xt[:, 512:1024]))
                    link(dve.bn_aggr(mv[:, t, :], stats[:, t, :, :].rearrange("p b s -> p (b s)")))
                    TS(mv[:, t, 1:2], mv[:, t, 1:2], LN_EPS, None, ALU.add).then_inc(sem("ln_var"), 1)
                    link(STT(xt, xt, mv[:, t, 0:1], ln_gb[:, 0, :], ALU.subtract, ALU.mult))
                    dve.wait_ge(sem("ln_rstd"), TT * n + t + 1)
                    STT(xt, xt, rstd[:, t:t + 1], ln_gb[:, 1, :], ALU.mult, ALU.add).then_inc(sem("ln_done"), 1)

            def conv(chunks, src, dst, tap):
                for j in chunks:
                    last = TS(dst(j), src(j), tap(CONV - 1, j), None, ALU.mult)
                link(last)
                for k in range(1, CONV):
                    for j in chunks:
                        last = STT(dst(j)[:, k:SEQ], src(j)[:, 0:SEQ - k], tap(CONV - 1 - k, j), dst(j)[:, k:SEQ], ALU.mult, ALU.add)
                    if k < CONV - 1:
                        link(last)
                return last

            link(dve.memset(eps_rms[:, :], RMS_EPS))
            turn_copies(0)
            dve.wait_ge(sem("params_turned"), 1)
            dve.wait_ge(sem("params_loaded"), 16 * 13)
            dve.tensor_copy(pcol[:, 0:CONV * NXBC], ps[:, 4, 0:CONV * NXBC])
            dve.tensor_copy(pcol[:, P:P + 88], ps[:, 4, P:P + 88])
            dve.tensor_copy(dcol[0:64, :], ssm_db[0:64, :].rearrange("p (j r) -> p j r", r=2)[:, :, 0])
            dve.tensor_copy(dcol[64:128, :], ssm_db[64:128, :].rearrange("p (j r) -> p j r", r=2)[:, :, 1]
                            ).then_inc(sem("params_copied"), 1)
            dve.wait_ge(sem("params_copied"), 1)
            for q in range(NDN // 2):
                dve.wait_ge(sem("dn_proj"), q + 1)
                conv((2 * q, 2 * q + 1), lambda j: ps[:, (j // 2) % 4, (j % 2) * SEQ:(j % 2 + 1) * SEQ],
                     lambda j: dnT[:, j, :], dn_tap).then_inc(sem("dn_conv"), 1)
            dve.wait_ge(sem("dn_silu"), NDN // 2)
            for b in range(4):
                TTO(sq[:, 512 * b:512 * b + 512].rearrange("p (k t) -> p k t", k=2), dnT[:, 2 * b:2 * b + 2, :],
                    dnT[:, 2 * b:2 * b + 2, :], ALU.mult).then_inc(sem("dn_sq"), 1)
            rn3 = rn[:, :].rearrange("p (k t) -> p k t", t=SEQ)
            dve.wait_ge(sem("dn_rn"), 4)
            STT(dnT[:, 0:4, :], dnT[:, 0:4, :], DD ** -0.5, rn3[:, 0:4, :], ALU.mult, ALU.mult).then_inc(sem("dn_qk"), 1)
            TTO(dnT[:, 4:8, :], dnT[:, 4:8, :], rn3[:, 4:8, :], ALU.mult).then_inc(sem("dn_qk"), 1)
            for t in range(TT):
                dve.wait_ge(sem("q_proj"), t + 1)
                dve.tensor_copy(qkv[:, t, 0:512].rearrange("p (c g d) -> p g c d", c=4, g=AKV),
                                ps[:, 6 + t, :].rearrange("p (g c d) -> p g c d", c=4, g=AKV)).then_inc(sem("q_copied"), 1)
            for t in range(TT):
                dve.wait_ge(sem("kv_proj"), t + 1)
                dve.tensor_copy(qkv[:, t, 512:768], ps[:, 4 + t, 0:256]).then_inc(sem("kv_copied"), 1)
                link(dve.tensor_copy(ba[:, t, :], ps[:, 4 + t, 256:256 + 2 * DH]))
            link(TTO(zdn[:, :, :], ba[:, :, DH:2 * DH], over_heads(dn_dtb[:, :], TT), ALU.add))
            STT(adn[:, :, :], zdn[:, :, :], -1.0, zdn[:, :, :], ALU.mult, ALU.max).then_inc(sem("dn_z"), 1)
            dve.wait_ge(sem("q_copied"), TT)
            dve.wait_ge(sem("kv_copied"), TT)
            qk4 = qkv[:, :, 0:640].rearrange("p t (h d) -> p t h d", d=AD)
            x1, x2 = qk4[:, :, :, 0:HALF], qk4[:, :, :, HALF:ROPE]

            def table(c):
                return const[:, c:c + TT * HALF].rearrange("p (t i) -> p t i", t=TT).unsqueeze(2).to_broadcast([P, TT, 10, HALF])

            r4 = [rt[:, i, :].rearrange("p (t h i) -> p t h i", t=TT, h=10) for i in range(4)]
            TTO(r4[0], x1, table(C_COS), ALU.mult)
            TTO(r4[1], x2, table(C_SIN), ALU.mult)
            TTO(r4[2], x2, table(C_COS), ALU.mult)
            link(TTO(r4[3], x1, table(C_SIN), ALU.mult))
            TTO(x1, r4[0], r4[1], ALU.subtract)
            TTO(x2, r4[2], r4[3], ALU.add).then_inc(sem("rope_done"), 1)
            dve.wait_ge(sem("dn_e2"), 1)
            dve.wait_ge(sem("dn_eb"), 2)
            link(STT(gdn[:, :, :], zdn[:, :, :], 0.0, e2dn[:, :, :], ALU.max, ALU.add))
            link(STT(gdn[:, :, :], gdn[:, :, :], -1.0, over_heads(eadn[:, :], TT), ALU.mult, ALU.mult))
            link(TS(beta[:, :, :], ebdn[:, :, :], 1.0, None, ALU.add))
            dve.reciprocal(beta[:, :, :], beta[:, :, :]).then_inc(sem("dn_gb"), 1)
            dve.wait_ge(sem("dn_gc"), 1)
            link(TS(ngc[:, :, :], ps[:, 4, 0:TT * DH].rearrange("p (t h) -> p t h", t=TT), -1.0, None, ALU.mult))
            TTO(ddk[:, :], ps[:, 4, 8:12], ngc[:, 0, :], ALU.add).then_inc(sem("dn_cols"), 1)
            dve.wait_ge(sem("dn_dke"), 2)
            dve.wait_ge(sem("dn_gb"), 1)
            link(TTO(bege[:, :], beta[:, 1, :], egc1[:, :], ALU.mult))
            for t in range(TT):
                dve.wait_ge(sem("dn_dec"), DH * (t + 1))
                dve.wait_ge(sem("dn_kk"), TT)
                hs = slice(t * DH, (t + 1) * DH)
                TTO(attnT[:, hs, :], four(ps[:, 6 + t, :]), decT[:, hs, :], ALU.mult)
                link(TTO(AT[:, hs, :], four(ps[:, 4 + t, :]), decT[:, hs, :], ALU.mult))
                TTO(AT[:, hs, :], AT[:, hs, :], four(ps[:, 2 + t, :]), ALU.mult).then_inc(sem("dn_A"), 1)
            dve.wait_ge(sem("dn_A"), TT)
            dve.wait_ge(sem("kv_turned"), 1)
            TTO(kdec[:, :, :], four(ps[:, 4, :]), bc(dke[:, :], P), ALU.mult)
            dve.wait_ge(sem("kv_turned"), 2)
            TTO(vb[:, 0:4, :], four(ps[:, 5, :]), bc(beta[:, 0, :], P), ALU.mult)
            dve.wait_ge(sem("kv_turned"), 3)
            TTO(kbe[:, :, :], four(ps[:, 6, :]), bc(bege[:, :], P), ALU.mult)
            dve.wait_ge(sem("kv_turned"), 4)
            TTO(vb[:, 4:8, :], four(ps[:, 7, :]), bc(beta[:, 1, :], P), ALU.mult).then_inc(sem("kv_scaled"), 1)
            def level(lv):
                if lv >= 2:
                    dve.wait_ge(sem("inv_P"), 2 * (lv - 1))
                mask = const[:, C_LVL + lv * P:C_LVL + (lv + 1) * P]
                for t in range(TT):
                    hs = slice(t * DH, (t + 1) * DH)
                    TTO(LT[:, lv % 2, hs, :], AT[:, hs, :], over_heads(mask, DH), ALU.mult).then_inc(sem("inv_L"), 1)

            am = const[:, C_AM:C_AM + 2 * P]

            def copy_qk(n):
                dve.wait_ge(sem("q_turned"), n + 1)
                if n < TT:
                    dve.tensor_copy(qT[:, :, n * P:(n + 1) * P], four(ps[:, 6 + n, :])).then_inc(sem("qT_copied"), 1)
                else:
                    dve.tensor_copy(kT[:, :], ps[:, 6, 0:SEQ]).then_inc(sem("qT_copied"), 1)

            def mask_scores(b):
                dve.wait_ge(sem("scores"), b + 1)
                bank = ps[:, 7 - b % 2, :]
                if b < 4:
                    ins = STT(s[:, 2 * b:2 * b + 2, 0:256], bank.rearrange("p (h k) -> p h k", h=2), AD ** -0.5,
                              over_heads(am, 2), ALU.mult, ALU.add)
                else:
                    ins = STT(s[:, 4 * (b - 4):4 * (b - 4) + 4, 256:384], four(bank), AD ** -0.5,
                              over_heads(am[:, P:2 * P], 4), ALU.mult, ALU.add)
                ins.then_inc(sem("scores_masked"), 1)

            def maximum():
                dve.wait_ge(sem("scores_masked"), 6)
                dve.tensor_reduce(mx[:, 1, :], s[:, :, 0:256], AX, ALU.max)
                link(dve.tensor_reduce(mx[:, 0, :], s[:, :, 256:384], AX, ALU.max))
                link(TTO(mx[:, :, :], mx[:, :, :], over_heads(sinks[:, :], 2), ALU.max))
                link(TS(nmx[:, :, :], mx[:, :, :], -1.0, None, ALU.mult))
                TTO(sdx[:, :, :], nmx[:, :, :], over_heads(sinks[:, :], 2), ALU.add).then_inc(sem("att_max"), 1)

            def divide(n):
                if n == 0:
                    dve.wait_ge(sem("att_exp"), 2 * AH + 1)
                    link(TTO(den[:, :, :], den[:, :, :], sdx[:, :, :], ALU.add))
                    link(dve.reciprocal(rden[:, :, :], den[:, :, :]))
                p_ = s[:, :, 256:384] if n == 0 else s[:, :, 0:256]
                TTO(p_, p_, bc(rden[:, n, :], 128 * (n + 1)), ALU.mult).then_inc(sem("p_ready"), 1)

            def copy_p(b):
                dve.wait_ge(sem("p_turned"), b + 1)
                dve.tensor_copy(pT[:, 4 * b:4 * b + 4, :], four(ps[:, 6, :])).then_inc(sem("pT_copied_dve"), 1)

            def attention(lv, half):
                at = (lv, half)
                if at == (0, 1):
                    copy_qk(0)
                    copy_qk(1)
                elif at == (1, 0):
                    copy_qk(2)
                elif at == (1, 1):
                    mask_scores(0)
                    mask_scores(1)
                elif at == (2, 0):
                    mask_scores(2)
                    mask_scores(3)
                elif at == (2, 1):
                    mask_scores(4)
                    mask_scores(5)
                    maximum()
                elif at == (4, 0):
                    divide(0)
                elif at == (4, 1):
                    divide(1)
                    copy_p(0)
                elif at == (5, 0):
                    copy_p(2)
                elif at == (5, 1):
                    copy_p(4)

            level(0)
            for lv in range(LEVELS):
                if lv == 1:
                    dve.wait_ge(sem("inv_X"), 2)
                if lv < LEVELS - 1:
                    level(lv + 1)
                attention(lv, 0)
                for t in range(TT):
                    hs = slice(t * DH, (t + 1) * DH)
                    if lv == 0:
                        dve.wait_ge(sem("inv_L"), t + 1)
                        TTO(XT[:, hs, :], over_heads(ident, DH), LT[:, 0, hs, :], ALU.subtract)
                        dve.wait_ge(sem("inv_P"), t + 1)
                        TTO(X[:, hs, :], over_heads(ident, DH), four(ps[:, t, :]), ALU.subtract).then_inc(sem("inv_X"), 1)
                    else:
                        dve.wait_ge(sem("inv_PX"), 2 * (lv - 1) + t + 1)
                        last = TTO(XT[:, hs, :], XT[:, hs, :], four(ps[:, 4 + t, :]), ALU.subtract)
                        if lv < LEVELS - 1:
                            last = TTO(X[:, hs, :], X[:, hs, :], four(ps[:, 2 + t, :]), ALU.subtract)
                        last.then_inc(sem("inv_X"), 1)
                attention(lv, 1)
            dve.wait_ge(sem("dn_u"), 1)
            dve.tensor_copy(u[:, 0:4, :], four(ps[:, 0, :])).then_inc(sem("dn_u_copied"), 1)
            dve.wait_ge(sem("dn_u"), 2)
            link(dve.tensor_copy(u[:, 4:8, :], four(ps[:, 1, :])))
            dve.wait_ge(sem("dn_o0"), 1)
            dve.tensor_copy(o[:, 0:4, :], four(ps[:, 3, :]))
            dve.wait_ge(sem("dn_wS"), 1)
            TTO(vnew[:, :, :], u[:, 4:8, :], four(ps[:, 5, :]), ALU.subtract).then_inc(sem("dn_vnew"), 1)
            dve.wait_ge(sem("dn_qS"), 1)
            link(TTO(o[:, 4:8, :], four(ps[:, 6, :]), bc(egc1[:, :], P), ALU.mult))
            dve.wait_ge(sem("dn_o1"), 1)
            link(TTO(o[:, 4:8, :], o[:, 4:8, :], four(ps[:, 7, :]), ALU.add))
            link(TTO(osq[:, :, :], o[:, :, :], o[:, :, :], ALU.mult))
            dve.tensor_reduce(oss[:, :], osq[:, :, :], AX, ALU.add).then_inc(sem("dn_oss"), 1)
            dve.wait_ge(sem("dn_orn"), 1)
            link(TTO(o[:, :, :], o[:, :, :], bc(orn[:, :], P), ALU.mult))
            link(TTO(o[:, :, :], o[:, :, :], over_heads(dn_nw[:, :], TT * DH), ALU.mult))
            dve.wait_ge(sem("gate_silu"), TT)
            TTO(o[:, :, :], o[:, :, :], gate[:, :, :].rearrange("p t (h d) -> p (t h) d", d=DD), ALU.mult).then_inc(sem("o_ready"), 1)
            dve.wait_ge(sem("o_turned"), 1)
            dve.tensor_copy(mixT[:, 4:8, 0:P], four(ps[:, 0, :])).then_inc(sem("mix_dn"), 1)
            layer_norm(0, [(sem("out_tile"), 1), (sem("out_proj"), 2)])
            if limit < 2:
                return
            for n in range(2):
                dense_low(n, n, n)
            turn_low(1)
            dense_low(2, 2, 2)

            def ffn_h(b, step):
                dve.wait_ge(sem("ffn_silu"), step + 1)
                dve.wait_ge(d_piece_used, 3 * step + (CUT + 2))
                dve.wait_ge(sem("ffn_h"), step + FIRST)
                TTO(hT[:, :], sg[:, b, :], ps[:, 2 * b + 1, :], ALU.mult).then_inc(sem("ffn_h_full"), 1)
                dve.wait_ge(sem("ffn_h_full"), step + 1)
                dve.tensor_copy(hT_hi[:, :, :], hT[:, :].rearrange("p (k t) -> p k t", k=2)).then_inc(sem("ffn_h_hi"), 1)
                dve.wait_ge(sem("ffn_h_hi"), step + 1)
                TTO(hT_lo[:, :, :], hT[:, :].rearrange("p (k t) -> p k t", k=2), hT_hi[:, :, :].bitcast(F32), ALU.subtract
                    ).then_inc(sem("ffn_h"), 1)

            dve.sem_inc(sem("ffn_h"), FIRST)
            with dve.Fori(0, FSTEPS // 2) as i:
                dense_low(6 * i + 3, 3, 0)
                ffn_h(0, 2 * i)
                dense_low(6 * i + 4, 4, 1)
                dense_low(6 * i + 5, 5, 2)
                dense_low(6 * i + 6, 0, 0)
                ffn_h(1, 2 * i + 1)
                dense_low(6 * i + 7, 1, 1)
                dense_low(6 * i + 8, 2, 2)
            ffn_h(0, FSTEPS - 1)
            if limit >= 3:
                for n in range(NFFN, NFFN + 2):
                    dense_low(n, n % RAW_D, n % CUT)
            layer_norm(1, [(sem("ffn_tile"), 1), (d_piece_used, CUT + NFFN)])
            if limit < 3:
                return
            turn_low(2)
            n = NFFN + 2
            dense_low(n, n % RAW_D, n % CUT)

            dve.wait_ge(sem("dt_proj"), 1)
            link(TTO(sz[:, :, :], ps[:, 4, 0:TT * SH].rearrange("p (t h) -> p t h", t=TT), over_heads(ssm_dtb[:, :], TT), ALU.add))
            STT(saz[:, :, :], sz[:, :, :], -1.0, sz[:, :, :], ALU.mult, ALU.max).then_inc(sem("ssm_z"), 1)
            for m, (kind, q) in enumerate(PROJ):
                n = NFFN + m + CUT
                if n < NPRE:
                    dense_low(n, n % RAW_D, n % CUT)
                if kind == 0:
                    dve.wait_ge(d_piece_used, CUT + NFFN + m + 1)
                    conv((2 * q, 2 * q + 1), lambda j: ps[:, (j // 2) % 4, (j % 2) * SEQ:(j % 2 + 1) * SEQ],
                         lambda j: xbcT[:, j, :], ssm_tap).then_inc(sem("ssm_conv"), 1)
            dve.wait_ge(sem("ssm_sp"), 2)
            link(STT(sdt[:, :, :], sz[:, :, :], 0.0, se2[:, :, :], ALU.max, ALU.add))
            STT(dA[:, :, :], sdt[:, :, :], -1.0, over_heads(sea[:, :], TT), ALU.mult, ALU.mult).then_inc(sem("dA_made"), 1)
            for t in range(TT):
                for q in range(4):
                    dve.wait_ge(sem("xs_turned"), 4 * t + q + 1)
                    TTO(xdt[:, t, 512 * q:512 * q + 512].rearrange("p (h d) -> p h d", d=SD),
                        ps[:, 4 * t + q, :].rearrange("p (h d) -> p h d", d=SD), bc(sdt[:, t, 8 * q:8 * q + 8], SD), ALU.mult
                        ).then_inc(sem("xdt_made"), 1)
            dve.wait_ge(sem("acs_made"), 1)
            link(TS(nacs[:, :, :], ps[:, 1, 0:TT * SH].rearrange("p (t h) -> p t h", t=TT), -1.0, None, ALU.mult))
            TTO(sdd[:, :], ps[:, 1, 64:96], nacs[:, 0, :], ALU.add).then_inc(sem("ssm_cols"), 1)
            dve.wait_ge(sem("ssm_dec"), 1)
            TTO(xdec[:, :].rearrange("p (h d) -> p h d", d=SD), xdt[:, 0, :].rearrange("p (h d) -> p h d", d=SD),
                bc(sdec[:, :], SD), ALU.mult).then_inc(sem("xdec_made"), 1)

            def y_diag(i):
                t, g = i // SG, i % SG
                dve.wait_ge(sem("y_made"), i + 1)
                for c in range(4):
                    j = 4 * g + c
                    yj = xbcT[:, j, t * P:(t + 1) * P]
                    last = STT(yj, yj, dcol[:, j:j + 1], ps[:, 4 + i % 2, c * P:(c + 1) * P], ALU.mult, ALU.add)
                last.then_inc(sem("y_added"), 1)

            for i in range(TT * SG):
                dve.wait_ge(sem("seg_made"), 8 * (i + 1))
                dve.wait_ge(sem("cb_copied"), TT)
                if i >= 2:
                    dve.wait_ge(sem("y_made"), i - 1)
                TTO(MT[:, i % 2], seg[:, i % 2], over_heads(cb[:, i, :], 8), ALU.mult).then_inc(sem("MT_made"), 1)
                if i:
                    y_diag(i - 1)
            y_diag(TT * SG - 1)
            dve.wait_ge(sem("y_added"), TT * SG)
            for q in range(4):
                dve.wait_ge(sem("er_made"), q + 1)
                link(TTO(yo[:, q % 2, :], er[:, q % 2, :], ps[:, 2 * (q % 2), :], ALU.mult))
                yq = xbcT[:, 4 * q:4 * q + 4, P:2 * P]
                TTO(yq, yq, four(yo[:, q % 2, :]), ALU.add).then_inc(sem("yoff_added"), 1)
            dve.wait_ge(sem("yoff_added"), 4)
            dve.wait_ge(sem("z_silu"), NX // 2)
            for g in range(SG):
                yg = xbcT[:, 4 * g:4 * g + 4, :]
                link(TTO(yg, yg, zT[:, 4 * g:4 * g + 4, :], ALU.mult))
                if g >= 2:
                    dve.wait_ge(sem("y_ss"), g - 1)
                TTO(ysq[:, g % 2, :].rearrange("p (k t) -> p k t", k=4), yg, yg, ALU.mult).then_inc(sem("ysq_made"), 1)
            for g in range(SG):
                dve.wait_ge(sem("y_rn"), g + 1)
                for j in range(4 * g, 4 * g + 4):
                    last = STT(xbcT[:, j, :], xbcT[:, j, :], ssm_nw(j), yrn[:, g, :], ALU.mult, ALU.mult)
                last.then_inc(sem("y_ready"), 1)
            layer_norm(2, [(sem("out_tile"), 2), (sem("out_proj"), 6)])
            turn_copies(3)
            if limit < 5:
                return

            dve.wait_ge(sem("logits"), 1)
            link(TTO(lg[:, :, :], ps[:, 4, 0:TT * E].rearrange("p (t e) -> p t e", t=TT), over_heads(brt[:, :], TT), ALU.add))
            for t in range(TT):
                link(dve.max(top8[:, t, :], lg[:, t, :]))
                link(dve.max_index(idx8[:, t, :].bitcast(U32), top8[:, t, :], lg[:, t, :]))
            TTO(dm[:, :, :], top8[:, :, 1:2], top8[:, :, 0:1], ALU.subtract).then_inc(sem("rt_dm"), 1)
            link(dve.tensor_copy(idxf[:, :, :], idx8[:, :, 0:2].bitcast(U32)))
            for t in range(TT):
                TS(oh1[:, t, :], iota8, idxf[:, t, 0:1], None, ALU.is_equal)
                link(TS(oh2[:, t, :], iota8, idxf[:, t, 1:2], None, ALU.is_equal))
            TTO(sel[:, :, :], oh1[:, :, :], oh2[:, :, :], ALU.add).then_inc(sem("sel_made"), 1)
            dve.wait_ge(sem("rt_e"), 1)
            link(TS(g2[:, :, :], g1[:, :, :], 1.0, None, ALU.add))
            link(dve.reciprocal(g2[:, :, :], g2[:, :, :]))
            link(TTO(g1[:, :, :], g1[:, :, :], g2[:, :, :], ALU.mult))
            for t in range(TT):
                link(TS(comb[:, t, :], oh1[:, t, :], g2[:, t, :], None, ALU.mult))
                link(STT(comb[:, t, :], oh2[:, t, :], g1[:, t, :], comb[:, t, :], ALU.mult, ALU.add))
            dve.wait_ge(sem("ranks"), 1)
            ps_rank = ps[:, 4, 32:32 + TT * E].rearrange("p (t e) -> p t e", t=TT)
            link(STT(rank[:, :, :], ps_rank, 1.0, sel[:, :, :], ALU.add, ALU.mult))
            link(TS(rank[:, :, :], rank[:, :, :], -1.0, None, ALU.add))
            link(TS(rank2[:, :, :], rank[:, :, :], -float(P), None, ALU.add))
            link(dve.tensor_reduce(cnt[:, :], ps[:, 4, 64:64 + E], AX, ALU.max))
            link(TS(cnt[:, :], cnt[:, :], -float(P), 0.0, ALU.add, ALU.max))
            dve.tensor_copy(over[:, :].bitcast(I32), cnt[:, :]).then_inc(sem("overflow_known"), 1)
            for t in range(TT):
                last = TS(yacc[:, t, :], x_tok[:, t, :], ALPHA, None, ALU.mult)
            last.then_inc(sem("yacc_open"), 1)

            def expert_dve(e, it, places):
                def cut_low(n):
                    dve.wait_ge(sem("hi_made"), PPE * it + (n + 1))
                    TTO(w_lo[:, n % CUT, :], raw[:, n % RAW, :], w_hi[:, n % CUT, :].bitcast(F32), ALU.subtract).then_inc(lo_made, 1)

                def mult(j):
                    dve.wait_ge(sem("e_silu"), ESTEPS * it + (j + 1))
                    TTO(eh[:, j % 2, :], esg[:, j % 2, :], ps[:, 2 * (j % 2) + 1, :], ALU.mult).then_inc(sem("e_h"), 1)

                def turned(j):
                    dve.wait_ge(sem("ehT_hi_made"), ESTEPS * it + (j + 1))
                    TTO(ehT_lo[:, j % 2], four(ps[:, 4, :]), ehT_hi[:, j % 2].bitcast(F32), ALU.subtract).then_inc(sem("ehT_made"), 1)

                dve.wait_ge(sem("xg_made"), 2 * it + FIRST)
                for t in range(TT):
                    TS(sel_rows[:, t, :], iota, places[:, t, bass.ds(e, 1)], None, ALU.is_equal)
                for t in range(TT):
                    ins = TS(sel_gate[:, t, :], iota, places[:, t, bass.ds(e, 1)], comb[:, t, bass.ds(e, 1)], ALU.is_equal, ALU.mult)
                ins.then_inc(sem("sel_rows_made"), 1)
                cut_low(0)
                dve.wait_ge(sem("G_turned"), it + 1)
                dve.wait_ge(sem("e_scattered"), 4 * it + FIRST)
                dve.tensor_copy(G[:, :, :], ps[:, 7, 0:TT * P].rearrange("p (t c) -> p t c", t=TT)).then_inc(sem("G_copied"), 1)
                for q in range(2):
                    dve.wait_ge(sem("xg_hi_made"), 2 * it + (q + 1))
                    hs = slice(4 * q, 4 * q + 4)
                    TTO(xg_lo[:, hs, :], four(ps[:, 2 + q, :]), xg_hi[:, hs, :].bitcast(F32), ALU.subtract).then_inc(sem("xg_lo_made"), 1)
                after = {}
                for j in range(ESTEPS):
                    after.setdefault(min(last_piece(j, 1) + 2, PPE - 1), []).append((mult, j))
                for j in range(ESTEPS - 1):
                    after.setdefault(min(last_piece(j + 1, 0) + 2, PPE - 1), []).append((turned, j))
                after.setdefault(PPE - 1, []).append((turned, ESTEPS - 1))
                for n in range(1, PPE):
                    cut_low(n)
                    for do, j in after.get(n, ()):
                        do(j)
                dve.wait_ge(piece_used, PPE * it + (CUT + PPE))
                dve.tensor_copy(oe[:, 0:512], ps[:, 5, :]).then_inc(sem("oe_copied_dve"), 1)
                for q in range(2 * TT):
                    dve.wait_ge(sem("e_scattered"), 4 * it + (q + 1) + FIRST)
                    yq = yacc[:, q // 2, 512 * (q % 2):512 * (q % 2) + 512]
                    TTO(yq, yq, ps[:, 7 if q % 2 == 0 else 4, :], ALU.add).then_inc(sem("e_added"), 1)

            dve.wait_ge(sem("yacc_open"), 1)
            dve.sem_inc(sem("e_h"), FIRST)
            dve.sem_inc(sem("e_added"), FIRST)
            dve.sem_inc(sem("ehT_made"), FIRST)
            with dve.Fori(0, E) as e:
                dve.wait_ge(sem("e_added"), 4 * e + FIRST)
                expert_dve(e, e, rank)
            more = dve.value_load(over[0:1, 0:1].bitcast(I32), min_val=0, max_val=SEQ)
            dve.wait_ge(sem("e_added"), 4 * E + FIRST)
            with dve.If(more > 0):
                with dve.Fori(0, E) as e:
                    dve.wait_ge(sem("e_added"), 4 * e + 4 * E + FIRST)
                    expert_dve(e, e + E, rank2)
                dve.wait_ge(sem("e_added"), 8 * E + FIRST)
            for t in range(TT):
                link(dve.tensor_copy(x_tok[:, t, :], yacc[:, t, :]))
            layer_norm(3, [(sem("e_added"), 4 * E + FIRST)] * TT, add=False)

        @block.tensor
        def _(pe):
            mm = pe.matmul

            def turn(n):
                for t in range(TT):
                    if n:
                        pe.wait_ge(sem("ln_done"), TT * (n - 1) + t + 1)
                    for q in range(2):
                        for k in range(4):
                            c = 4 * q + k
                            last = pe.transpose(ps[:, 2 * t + q, k * P:(k + 1) * P], x_tok[:, t, c * P:(c + 1) * P], ident)
                        last.then_inc(sem("x_turned"), 1)

            def arrived(n):
                pe.wait_ge(loaded[n % RING], 32 * (n // RING + 1))

            def wslot(n, k, width):
                return slot(n % RING)[:, 0:k * width].rearrange("p (k n) -> p k n", k=k)

            def channel_major(unit, first_pair, bank0, done, free, free_lag):
                arrived(unit)
                w = wslot(unit, KD, 512)
                for c in range(4):
                    pair = first_pair + c // 2
                    if c % 2 == 0 and pair >= free_lag:
                        pe.wait_ge(free, pair - free_lag + 1)
                    for k in range(KD):
                        last = mm(ps[:, bank0 + pair % 4, (c % 2) * SEQ:(c % 2 + 1) * SEQ], w[:, k, c * P:(c + 1) * P],
                                  xT[:, k, :], start=k == 0, stop=k == KD - 1)
                    if c % 2:
                        last.then_inc(done, 1)

            def token_major(out_ap, w, t):
                for k in range(KD):
                    last = mm(out_ap, xT[:, k, t * P:(t + 1) * P], w[:, k, :], start=k == 0, stop=k == KD - 1)
                return last

            def output_projection(unit0, n_units, src, ready):
                for t in range(TT):
                    for i in range(n_units):
                        arrived(unit0 + i)
                        w = wslot(unit0 + i, 4, D)
                        for kk in range(4):
                            k = 4 * i + kk
                            ready(k)
                            for n in range(2):
                                last = mm(ps[:, 4 + 2 * t + n, :], src[:, k, t * P:(t + 1) * P], w[:, kk, 512 * n:512 * n + 512],
                                          start=k == 0, stop=k == 4 * n_units - 1)
                        if t == TT - 1:
                            last.then_inc(sem("out_proj"), 1)
                        elif i == n_units - 1:
                            last.then_inc(sem("out_tile"), 1)

            pe.wait_ge(sem("x_loaded"), 32)
            turn(0)
            pe.wait_ge(sem("xT_copied"), 4)
            channel_major(0, 0, 0, sem("dn_proj"), sem("dn_conv"), 4)
            pe.wait_ge(sem("taps_loaded"), 16 * 4)
            pe.transpose(ps[:, 4, 0:CONV * NXBC], prow_a[0:CONV * NXBC, :], ident[0:CONV * NXBC, 0:CONV * NXBC])
            pe.transpose(ps[:, 4, P:P + 88], prow_b[0:88, :], ident[0:88, 0:88]).then_inc(sem("params_turned"), 1)
            for i in range(1, 3):
                channel_major(i, 2 * i, 0, sem("dn_proj"), sem("dn_conv"), 4)
            pe.wait_ge(sem("params_copied"), 1)
            arrived(3)
            for t in range(TT):
                last = token_major(ps[:, 4 + t, :], wslot(3, KD, 512), t)
                last.then_inc(sem("gate_proj"), 1)
            pe.wait_ge(sem("pool_set"), 3)
            pe.wait_ge(sem("dn_conv"), NDN // 2)
            for b in range(4):
                pe.wait_ge(sem("dn_sq"), b + 1)
                mm(ps[:, b, :], ones[:, :], sq[:, 512 * b:512 * b + 512], start=True, stop=True).then_inc(sem("dn_ss"), 1)
            arrived(4)
            for t in range(TT):
                token_major(ps[:, 6 + t, :], wslot(4, KD, 512), t).then_inc(sem("q_proj"), 1)
            arrived(5)
            for t in range(TT):
                pe.wait_ge(sem("gate_silu"), t + 1)
                token_major(ps[:, 4 + t, 0:256], wslot(5, KD, 256), t)
                token_major(ps[:, 4 + t, 256:256 + 2 * DH], w_ba, t).then_inc(sem("kv_proj"), 1)
            def kk_products(t):
                ts_ = slice(t * P, (t + 1) * P)
                for h in range(DH):
                    mm(ps[:, 4 + t, h * P:(h + 1) * P], dnT[:, 4 + h, ts_], dnT[:, 4 + h, ts_], start=True, stop=True)
                    last = mm(ps[:, 6 + t, h * P:(h + 1) * P], dnT[:, 4 + h, ts_], dnT[:, h, ts_], start=True, stop=True)
                last.then_inc(sem("dn_kk"), 1)

            pe.wait_ge(sem("dn_qk"), 2)
            pe.wait_ge(sem("dn_z"), 1)
            kk_products(1)
            pe.wait_ge(sem("dn_gb"), 1)
            g8 = gdn[:, :, :].rearrange("p t h -> p (t h)")
            mm(ps[:, 4, 0:8], tri, g8, start=True, stop=True)
            mm(ps[:, 4, 8:12], ones[:, :], gdn[:, 0, :], start=True, stop=True).then_inc(sem("dn_gc"), 1)
            pe.wait_ge(sem("dn_rn"), 4)
            for t in range(TT):
                mm(ps[:, t, :], identb[:, :], over_heads(maskb[:, :], 4), start=True, stop=False)
                for h in range(DH):
                    last = mm(ps[:, t, h * P:(h + 1) * P], gdn[:, t, h:h + 1].to_broadcast([P, P]), tri, start=False, stop=h == DH - 1)
                last.then_inc(sem("dn_gcrow"), 1)
                for h in range(DH):
                    mm(ps[:, 2 + t, h * P:(h + 1) * P], beta[:, t, h:h + 1].to_broadcast([P, P]), ident, start=True, stop=True)
            pe.wait_ge(sem("dn_cols"), 1)
            kk_products(0)
            pe.wait_ge(sem("dn_A"), TT)
            for t in range(TT):
                for w_ in range(2):
                    for h in range(DH):
                        last = pe.transpose(ps[:, 4 + 2 * t + w_, h * P:(h + 1) * P], dnT[:, 4 + 4 * w_ + h, t * P:(t + 1) * P], ident)
                    last.then_inc(sem("kv_turned"), 1)

            def turn_qk(n):
                if n == 0:
                    pe.wait_ge(sem("rope_done"), 1)
                    pe.wait_ge(sem("kv_scaled"), 1)
                if n < TT:
                    for c in range(4):
                        last = pe.transpose(ps[:, 6 + n, c * P:(c + 1) * P], qkv[:, n, c * P:(c + 1) * P], ident)
                else:
                    pe.wait_ge(sem("qT_copied"), 1)
                    for t in range(TT):
                        last = pe.transpose(ps[:, 6, t * P:(t + 1) * P], qkv[:, t, 512:640], ident)
                last.then_inc(sem("q_turned"), 1)

            def score_products(b):
                if b < 2:
                    pe.wait_ge(sem("qT_copied"), 3)
                else:
                    pe.wait_ge(sem("scores_masked"), b - 1)
                bank = ps[:, 7 - b % 2, :]
                if b < 4:
                    for h in (2 * b, 2 * b + 1):
                        r = slice(64 * (h // 4), 64 * (h // 4) + 64)
                        last = mm(bank[:, (h % 2) * 256:(h % 2) * 256 + 256], qT[r, h % 4, P:2 * P], kT[r, :], start=True, stop=True)
                else:
                    r = slice(64 * (b - 4), 64 * (b - 4) + 64)
                    for h in range(4):
                        last = mm(bank[:, h * P:(h + 1) * P], qT[r, h, 0:P], kT[r, 0:P], start=True, stop=True)
                last.then_inc(sem("scores"), 1)

            def turn_p(b):
                pe.wait_ge(sem("p_ready"), 1 if b < 2 else 2)
                if b < 2:
                    pe.wait_ge(sem("scores_masked"), 6)
                elif b % 2 == 0:
                    pe.wait_ge(sem("pT_copied_dve"), b // 2)
                else:
                    pe.wait_ge(sem("pT_copied_act"), b // 2)
                for i in range(4 * b, 4 * b + 4):
                    src = s[:, i, 256:384] if i < AH else s[:, (i - AH) // 2, ((i - AH) % 2) * P:((i - AH) % 2 + 1) * P]
                    last = pe.transpose(ps[:, 6 + b % 2, (i % 4) * P:(i % 4 + 1) * P], src, ident)
                last.then_inc(sem("p_turned"), 1)

            def weigh_v(b):
                pe.wait_ge(sem("pT_copied_dve"), 3)
                pe.wait_ge(sem("pT_copied_act"), 3)
                for h in range(4 * b, 4 * b + 4):
                    c, r = h // 2, 64 * (h % 2)
                    vcol = 640 + AD * (h // 4)
                    o_ = [ps[r:r + 64, 6 + b, (c % 2) * SEQ + t * P:(c % 2) * SEQ + (t + 1) * P] for t in range(TT)]
                    mm(o_[0], qkv[:, 0, vcol:vcol + AD], pT[:, h, :], start=True, stop=True)
                    mm(o_[1], qkv[:, 0, vcol:vcol + AD], pT[:, AH + 2 * h, :], start=True, stop=False)
                    last = mm(o_[1], qkv[:, 1, vcol:vcol + AD], pT[:, AH + 2 * h + 1, :], start=False, stop=True)
                last.then_inc(sem("att_out"), 1)

            def attention(lv, half):
                at = (lv, half)
                if at == (0, 1):
                    turn_qk(0)
                    turn_qk(1)
                elif at == (1, 0):
                    turn_qk(2)
                elif at == (1, 1):
                    score_products(0)
                    score_products(1)
                elif at == (2, 0):
                    score_products(2)
                    score_products(3)
                elif at == (2, 1):
                    score_products(4)
                    score_products(5)
                elif at == (4, 1):
                    turn_p(0)
                    turn_p(1)
                elif at == (5, 0):
                    turn_p(2)
                    turn_p(3)
                elif at == (5, 1):
                    turn_p(4)
                    turn_p(5)
                elif at == (6, 0):
                    weigh_v(0)
                elif at == (6, 1):
                    weigh_v(1)

            for lv in range(LEVELS):
                for t in range(TT):
                    pe.wait_ge(sem("inv_L"), 2 * lv + t + 1)
                    if lv:
                        pe.wait_ge(sem("inv_X"), 2 * (lv - 1) + t + 1)
                    for h in range(DH):
                        i = t * DH + h
                        last = mm(ps[:, t, h * P:(h + 1) * P], LT[:, lv % 2, i, :], X[:, i, :] if lv else ident, start=True, stop=True)
                    last.then_inc(sem("inv_P"), 1)
                attention(lv, 0)
                if lv == 1:
                    pe.wait_ge(sem("kv_scaled"), 1)
                for t in range(TT if lv else 0):
                    pe.wait_ge(sem("inv_P_copied"), 2 * (lv - 1) + t + 1)
                    for h in range(DH):
                        i = t * DH + h
                        if lv < LEVELS - 1:
                            mm(ps[:, 2 + t, h * P:(h + 1) * P], XT[:, i, :], Pm[:, i, :], start=True, stop=True)
                        last = mm(ps[:, 4 + t, h * P:(h + 1) * P], Pm[:, i, :], XT[:, i, :], start=True, stop=True)
                    last.then_inc(sem("inv_PX"), 1)
                attention(lv, 1)
            for t in range(TT):
                pe.wait_ge(sem("inv_X"), 2 * (LEVELS - 1) + t + 1)
                for h in range(DH):
                    i = t * DH + h
                    last = mm(ps[:, t, h * P:(h + 1) * P], XT[:, i, :], vb[:, i, :], start=True, stop=True)
                last.then_inc(sem("dn_u"), 1)
            for h in range(DH):
                last = mm(ps[:, 2, h * P:(h + 1) * P], kbe[:, h, :], XT[:, 4 + h, :], start=True, stop=True)
            last.then_inc(sem("dn_w"), 1)
            pe.wait_ge(sem("dn_u_copied"), 1)
            for h in range(DH):
                last = mm(ps[:, 4, h * P:(h + 1) * P], kdec[:, h, :], u[:, h, :], start=True, stop=True)
            last.then_inc(sem("dn_S"), 1)
            for h in range(DH):
                last = mm(ps[:, 3, h * P:(h + 1) * P], attnT[:, h, :], u[:, h, :], start=True, stop=True)
            last.then_inc(sem("dn_o0"), 1)
            pe.wait_ge(sem("dn_w_copied"), 1)
            pe.wait_ge(sem("dn_S_copied"), 1)
            for h in range(DH):
                last = mm(ps[:, 5, h * P:(h + 1) * P], wT[:, h, :], S1[:, h, :], start=True, stop=True)
            last.then_inc(sem("dn_wS"), 1)
            pe.wait_ge(sem("mix_att"), 2)
            for h in range(DH):
                last = mm(ps[:, 6, h * P:(h + 1) * P], dnT[:, h, P:2 * P], S1[:, h, :], start=True, stop=True)
            last.then_inc(sem("dn_qS"), 1)
            pe.wait_ge(sem("dn_vnew"), 1)
            for h in range(DH):
                last = mm(ps[:, 7, h * P:(h + 1) * P], attnT[:, 4 + h, :], vnew[:, h, :], start=True, stop=True)
            last.then_inc(sem("dn_o1"), 1)
            pe.wait_ge(sem("o_ready"), 1)
            for t in range(TT):
                for h in range(DH):
                    last = pe.transpose(ps[:, t, h * P:(h + 1) * P], o[:, t * DH + h, :], ident)
                last.then_inc(sem("o_turned"), 1)

            def mix_ready(k):
                if k == 0:
                    pe.wait_ge(sem("mix_att"), 2)
                if k == 4:
                    pe.wait_ge(sem("mix_dn"), 2)

            output_projection(6, 2, mixT, mix_ready)
            turn(1)
            if limit < 2:
                return

            def open_banks():
                for b in range(4, 8):
                    mm(ps[:, b, :], identb[:, :], zerob[:, :], start=True, stop=False)

            def three_wx(out_ap, c, k, cs, first, last_):
                whi, wlo = [w[:, c, :].rearrange("p (k n) -> p k n", k=KD)[:, k, cs] for w in (w_hi, w_lo)]
                mm(out_ap, whi, xT_hi[:, k, :], start=first, stop=False)
                mm(out_ap, whi, xT_lo[:, k, :], start=False, stop=False)
                return mm(out_ap, wlo, xT_hi[:, k, :], start=False, stop=last_)

            def columns(n, c, bank):
                pe.wait_ge(d_lo_made, n + (RAW_D + 1))
                for j in range(2):
                    for k in range(KD):
                        last = three_wx(ps[:, bank, j * SEQ:(j + 1) * SEQ], c, k, slice(j * P, (j + 1) * P), k == 0, k == KD - 1)
                last.then_inc(d_piece_used, 1)

            def ffn_down(n, c, step, close):
                pe.wait_ge(d_lo_made, n + (RAW_D + 1))
                pe.wait_ge(sem("ffn_h"), step + (1 + FIRST))
                whi, wlo = [w[:, c, :].rearrange("p (k n) -> p k n", k=2) for w in (w_hi, w_lo)]
                for t in range(TT):
                    ts_ = slice(t * P, (t + 1) * P)
                    for h in range(2):
                        cs = slice(512 * h, 512 * h + 512)
                        for k in range(2):
                            out_ap = ps[:, 4 + 2 * t + h, :]
                            mm(out_ap, hT_hi[:, k, ts_], whi[:, k, cs], start=False, stop=False)
                            mm(out_ap, hT_hi[:, k, ts_], wlo[:, k, cs], start=False, stop=False)
                            last = mm(out_ap, hT_lo[:, k, ts_], whi[:, k, cs], start=False, stop=close and k == 1)
                    if close and t == 0:
                        last.then_inc(sem("ffn_tile"), 1)
                last.then_inc(d_piece_used, 1)

            pe.sem_inc(d_piece_used, CUT)
            open_banks()
            pe.wait_ge(sem("xT_lo_made"), 4)
            columns(0, 0, 0)
            columns(1, 1, 1)
            with pe.Fori(0, FSTEPS // 2) as i:
                columns(6 * i + 2, 2, 2)
                columns(6 * i + 3, 0, 3)
                ffn_down(6 * i + 4, 1, 2 * i, False)
                columns(6 * i + 5, 2, 0)
                columns(6 * i + 6, 0, 1)
                ffn_down(6 * i + 7, 1, 2 * i + 1, False)
            ffn_down(NFFN - 1, (NFFN - 1) % CUT, FSTEPS - 1, True)
            turn(2)
            if limit < 3:
                return

            pe.wait_ge(sem("xT_lo_made"), 8)
            for t in range(TT):
                for part, xt in enumerate((xT_hi, xT_lo)):
                    for k in range(KD):
                        last = mm(ps[:, 4, t * SH:(t + 1) * SH], xt[:, k, t * P:(t + 1) * P].bitcast(F32), w_dt[:, k, :],
                                  start=part == 0 and k == 0, stop=part == 1 and k == KD - 1)
            last.then_inc(sem("dt_proj"), 1)
            for m, (kind, q) in enumerate(PROJ):
                n = NFFN + m
                if kind == 0 and q >= 4:
                    pe.wait_ge(sem("ssm_conv"), q - 3)
                if kind == 1 and q == 0:
                    pe.wait_ge(sem("ssm_z"), 1)
                if kind == 1 and q >= 4:
                    pe.wait_ge(sem("z_silu"), q - 3)
                columns(n, n % CUT, (0 if kind == 0 else 4) + q % 4)
            pe.wait_ge(sem("ssm_silu"), NXBC)
            for t in range(TT):
                for q in range(4):
                    if t == 1 and q == 0:
                        pe.wait_ge(sem("z_silu"), NX // 2)
                    for c in range(4):
                        j = 4 * q + c
                        last = pe.transpose(ps[:, 4 * t + q, c * P:(c + 1) * P], xbcT[:, j, t * P:(t + 1) * P], ident)
                    last.then_inc(sem("xs_turned"), 1)
            pe.wait_ge(sem("xdt_made"), 4)
            pe.wait_ge(sem("dA_made"), 1)
            mm(ps[:, 1, 0:64], tri, dA[:, :, :].rearrange("p t h -> p (t h)"), start=True, stop=True)
            mm(ps[:, 1, 64:96], ones[:, :], dA[:, 0, :], start=True, stop=True).then_inc(sem("acs_made"), 1)
            for g in range(SG):
                last = pe.transpose(ps[:, 0, g * P:(g + 1) * P], xbcT[:, NX + g, 0:P], ident)
            last.then_inc(sem("B_turned"), 1)
            for t in range(TT):
                for g in range(SG):
                    last = mm(ps[:, 2 + t, g * P:(g + 1) * P], xbcT[:, NX + g, t * P:(t + 1) * P],
                              xbcT[:, NX + SG + g, t * P:(t + 1) * P], start=True, stop=True)
                last.then_inc(sem("cb_made"), 1)
            pe.wait_ge(sem("B_copied"), 1)
            pe.wait_ge(sem("xdec_made"), 1)
            pe.wait_ge(sem("xdt_made"), 8)
            for g in range(SG):
                mm(ps[:, 4 + g, :], Btok[:, g * P:(g + 1) * P], xdec[:, 512 * g:512 * g + 512], start=True, stop=True
                   ).then_inc(sem("state_made"), 1)

            def acs_rows(i):
                t, g = i // SG, i % SG
                if i == 0:
                    pe.wait_ge(sem("ssm_cols"), 1)
                    pe.wait_ge(sem("B_copied"), 1)
                if i == 1:
                    pe.wait_ge(sem("cb_copied"), TT)
                if i >= 2:
                    pe.wait_ge(sem("seg_made"), 8 * (i - 1))
                for b in range(2):
                    bank = ps[:, 2 * (i % 2) + b, :]
                    mm(bank, identb[:, :], over_heads(maskb[:, :], 4), start=True, stop=False)
                    for r in range(4):
                        h = 8 * g + 4 * b + r
                        last = mm(bank[:, r * P:(r + 1) * P], dA[:, t, h:h + 1].to_broadcast([P, P]), tri, start=False, stop=r == 3)
                last.then_inc(sem("acs_rows"), 1)

            def y_products(i):
                t, g = i // SG, i % SG
                pe.wait_ge(sem("MT_made"), i + 1)
                if i == 0:
                    pe.wait_ge(sem("state_copied"), SG)
                if i >= 2:
                    pe.wait_ge(sem("y_added"), i - 1)
                for r in range(8):
                    h = 8 * g + r
                    last = mm(ps[64 * (r % 2):64 * (r % 2) + 64, 4 + i % 2, (r // 2) * P:(r // 2 + 1) * P],
                              xdt[:, t, SD * h:SD * (h + 1)], MT[:, i % 2, r, :], start=True, stop=True)
                last.then_inc(sem("y_made"), 1)

            acs_rows(0)
            for i in range(TT * SG):
                if i + 1 < TT * SG:
                    acs_rows(i + 1)
                y_products(i)
            pe.wait_ge(sem("seg_made"), 8 * TT * SG)
            for q in range(4):
                b = 2 * (q % 2)
                if q >= 2:
                    pe.wait_ge(sem("yoff_added"), q - 1)
                for c in range(4):
                    j = 4 * q + c
                    mm(ps[:, b, c * P:(c + 1) * P], state[:, j * P:(j + 1) * P], xbcT[:, NX + SG + q, P:2 * P], start=True, stop=True)
                    for r in range(2):
                        last = mm(ps[64 * r:64 * r + 64, b + 1, c * P:(c + 1) * P], dA[:, 1, 2 * j + r:2 * j + r + 1].to_broadcast([P, SD]),
                                  tri, start=True, stop=True)
                last.then_inc(sem("yoff_made"), 1)
            for g in range(SG):
                pe.wait_ge(sem("ysq_made"), g + 1)
                if g == 0:
                    pe.wait_ge(sem("y_added"), TT * SG)
                for c in range(4):
                    last = mm(ps[:, 4 + g, 0:SEQ], ones[:, :], ysq[:, g % 2, c * SEQ:(c + 1) * SEQ], start=c == 0, stop=c == 3)
                last.then_inc(sem("y_ss"), 1)

            def y_ready(k):
                if k % 4 == 0:
                    pe.wait_ge(sem("y_ready"), SG if k == 0 else k // 4 + 1)

            output_projection(BASE1, 4, xbcT, y_ready)
            turn(3)
            if limit < 5:
                return
            pe.wait_ge(sem("xT_copied"), 8)
            for t in range(TT):
                last = token_major(ps[:, 4, t * E:(t + 1) * E], w_rt, t)
            last.then_inc(sem("logits"), 1)
            pe.wait_ge(sem("sel_made"), 1)
            mm(ps[:, 4, 32:32 + E], tris, sel[:, 0, :], start=True, stop=True)
            mm(ps[:, 4, 40:40 + E], tris, sel[:, 1, :], start=True, stop=False)
            mm(ps[:, 4, 40:40 + E], ones[:, :], sel[:, 0, :], start=False, stop=True)
            mm(ps[:, 4, 64:64 + E], ones[:, :], sel[:, 0, :], start=True, stop=False)
            mm(ps[:, 4, 64:64 + E], ones[:, :], sel[:, 1, :], start=False, stop=True).then_inc(sem("ranks"), 1)

            def expert_pe(it):
                pe.wait_ge(sem("sel_rows_made"), it + 1)
                pe.wait_ge(sem("e_added"), 4 * it + FIRST)
                for t in range(TT):
                    last = pe.transpose(ps[:, 7, t * P:(t + 1) * P], sel_gate[:, t, :], ident)
                last.then_inc(sem("G_turned"), 1)
                pe.wait_ge(sem("e_h"), ESTEPS * it + FIRST)
                for q in range(2):
                    for k in range(4):
                        c = 4 * q + k
                        for t in range(TT):
                            last = mm(ps[:, 2 + q, k * P:(k + 1) * P], x_tok[:, t, c * P:(c + 1) * P], sel_rows[:, t, :],
                                      start=t == 0, stop=t == TT - 1)
                    last.then_inc(sem("xg_made"), 1)
                pe.wait_ge(sem("xg_lo_made"), 2 * it + 2)

                def three(out_ap, hi, lo, whi, wlo, start, stop):
                    mm(out_ap, hi, whi, start=start, stop=False)
                    mm(out_ap, hi, wlo, start=False, stop=False)
                    return mm(out_ap, lo, whi, start=False, stop=stop)

                def pieces(n, k):
                    return [w[:, n % CUT, :].rearrange("p (k n) -> p k n", k=k) for w in (w_hi, w_lo)]

                def product(j, what):
                    for half in range(PPU):
                        n = PPU * ORDER.index((j, what)) + half
                        pe.wait_ge(lo_made, PPE * it + (RAW + n + 1))
                        whi, wlo = pieces(n, 4)
                        for kk in range(4):
                            k = 4 * half + kk
                            last = three(ps[:, 2 * (j % 2) + what, :], xg_hi[:, k, :], xg_lo[:, k, :], whi[:, kk, :], wlo[:, kk, :],
                                         k == 0, k == KD - 1)
                        last.then_inc(piece_used, 1)

                def turn_h(j):
                    pe.wait_ge(sem("e_h"), ESTEPS * it + (j + 1) + FIRST)
                    pe.wait_ge(sem("ehT_made"), ESTEPS * it + j + FIRST)
                    for c in range(4):
                        last = pe.transpose(ps[:, 4, c * P:(c + 1) * P], eh[:, j % 2, c * P:(c + 1) * P], ident)
                    last.then_inc(sem("eh_turned"), 1)

                def down(j):
                    pe.wait_ge(sem("ehT_made"), ESTEPS * it + (j + 1) + FIRST)
                    for half in range(PPU):
                        n = PPU * ORDER.index((j, 2)) + half
                        pe.wait_ge(lo_made, PPE * it + (RAW + n + 1))
                        whi, wlo = pieces(n, 2)
                        for cc in range(2):
                            c = 2 * half + cc
                            for h in range(2):
                                cs = slice(512 * h, 512 * h + 512)
                                last = three(ps[:, 5 + h, :], ehT_hi[:, j % 2, c, :], ehT_lo[:, j % 2, c, :], whi[:, cc, cs],
                                             wlo[:, cc, cs], j == 0 and c == 0, j == ESTEPS - 1 and c == 3)
                        last.then_inc(piece_used, 1)

                for j in range(ESTEPS):
                    if j >= 2:
                        pe.wait_ge(sem("e_h"), ESTEPS * it + (j - 1) + FIRST)
                    product(j, 0)
                    if j:
                        turn_h(j - 1)
                    product(j, 1)
                    if j:
                        down(j - 1)
                turn_h(ESTEPS - 1)
                down(ESTEPS - 1)
                pe.wait_ge(sem("G_copied"), it + 1)
                pe.wait_ge(sem("oe_copied_dve"), it + 1)
                pe.wait_ge(sem("oe_copied_act"), it + 1)
                for q in range(2 * TT):
                    if q >= 2:
                        pe.wait_ge(sem("e_added"), 4 * it + (q - 1) + FIRST)
                    mm(ps[:, 7 if q % 2 == 0 else 4, :], G[:, q // 2, :], oe[:, 512 * (q % 2):512 * (q % 2) + 512], start=True, stop=True
                       ).then_inc(sem("e_scattered"), 1)

            pe.sem_inc(piece_used, CUT)
            pe.sem_inc(sem("xg_made"), FIRST)
            pe.sem_inc(sem("e_scattered"), FIRST)
            with pe.Fori(0, E) as e:
                expert_pe(e)
            more = pe.value_load(over[0:1, 0:1].bitcast(I32), min_val=0, max_val=SEQ)
            with pe.If(more > 0):
                with pe.Fori(0, E) as e:
                    expert_pe(e + E)


_INS = ["x", "ln_g", "ln_b", "even_w_in", "swa_sinks", "dn_conv_w", "dn_a_log", "dn_dt_bias", "dn_norm_w", "even_w_out",
        "ssm_w_in", "ssm_conv_w", "ssm_conv_b", "ssm_dt_bias", "ssm_a_log", "ssm_d", "ssm_norm_w", "ssm_w_out",
        "ffn_w_gate", "ffn_w_up", "ffn_w_down", "moe_w_router", "moe_b_router", "moe_w_gate", "moe_w_up", "moe_w_down"]


def kernel(**inputs):
    import ml_dtypes
    from concourse import bacc
    from concourse.bass_utils import run_bass_kernel_spmd

    nc = bacc.Bacc("TRN2", target_bir_lowering=False, num_devices=1)
    arrays = {name: np.ascontiguousarray(inputs[name]) for name in _INS}
    arrays["shape_consts"] = shape_constants()
    arrays["shape_consts_b"] = shape_constants_b(ml_dtypes.bfloat16)
    dram = {}
    for name, a in arrays.items():
        dram[name] = nc.dram_tensor(f"in_{name}", a.shape, mybir.dt.from_np(a.dtype), kind="ExternalInput").ap()
    out = nc.dram_tensor("out", (1, SEQ, D), F32, kind="ExternalOutput").ap()
    build(nc, dram, out)
    r = run_bass_kernel_spmd(nc, [{f"in_{name}": a for name, a in arrays.items()}], core_ids=[0])
    return r.results[0]["out"]
```

```python
from contextlib import ExitStack

import numpy as np

import concourse.bass as bass
from concourse import mybir

ALU = mybir.AluOpType
ACT = mybir.ActivationFunctionType
F32 = mybir.dt.float32
BF16 = mybir.dt.bfloat16
F32R = mybir.dt.float32r
I32 = mybir.dt.int32
U32 = mybir.dt.uint32
AX = mybir.AxisListType.X

P = 128
SEQ = 256
TT = SEQ // P
D = 1024
KD = D // P
DEPTH = 2
ALPHA = (2 * DEPTH) ** 0.25
LN_EPS, RMS_EPS = 1e-5, 1e-6
AH, AKV, AD = 8, 2, 64
ROPE = AD // 4
HALF = ROPE // 2
THETA = 500000.0
DH, DD = 4, 128
CONV = 4
NDN = 3 * DH
LEVELS = 7
Q0, K0 = 0, AH * AD
B0 = K0 + 2 * AKV * AD
G0 = B0 + NDN * P
BA0 = G0 + DH * DD
SI = 2048
SH, SD, SG, SN = 32, 64, 4, 128
NX = SI // P
NXBC = NX + 2 * SG
F = 2816
FW = 256
FSTEPS = F // FW
E = 8
EF = 3584
EW = 512
ESTEPS = EF // EW
NEG = -1e30

FIRST = 1

SLOT = 4096
RING = 4
PIECE = 2048
RAW = 7
CUT = 3
RAW_D = 6
PPU = 2
PPE = 3 * ESTEPS * PPU
assert PPE % RAW == 0 and PPE % CUT == 0
ORDER = [(0, 0), (0, 1)]
for _j in range(1, ESTEPS):
    ORDER += [(_j, 0), (_j, 1), (_j - 1, 2)]
ORDER += [(ESTEPS - 1, 2)]


N_DN = (0, 1, 4, 5, 8, 9)
N_GATE, N_Q, N_KV = 2, 6, 10
N0 = N_KV + 2
assert N0 % RAW_D == 0 and N0 % CUT == 0
N1 = N0 + 3 * FSTEPS
PROJ = []
for _g in range(NX // 4):
    PROJ += [(0, 3 * _g), (0, 3 * _g + 1), (1, 2 * _g), (0, 3 * _g + 2), (1, 2 * _g + 1)]
assert len(PROJ) == (NXBC + NX) // 2 and sum(1 - k for k, _ in PROJ) == NXBC // 2
N2 = N1 + len(PROJ)
N_OUT = NX // 2
NPRE = N2 + N_OUT
DT_AT = 3


def last_piece(step, what):
    return PPU * ORDER.index((step, what)) + PPU - 1


G_AT = CUT + 2


C_ID, C_TRI, C_TRIS = 0, P, 2 * P
C_LVL = 3 * P
C_AM = C_LVL + LEVELS * P
C_COS = C_AM + 2 * P
C_SIN = C_COS + TT * HALF
C_IOTA = C_SIN + TT * HALF
C_I8 = C_IOTA + P
C_W = C_I8 + E


def shape_constants():
    c = np.zeros((P, C_W), np.float32)
    r = np.arange(P)
    c[:, C_ID:C_ID + P] = np.eye(P)
    c[:, C_TRI:C_TRI + P] = r[:, None] <= r[None, :]
    c[:, C_TRIS:C_TRIS + P] = r[:, None] < r[None, :]
    for lv in range(LEVELS):
        b = 1 << lv
        same = (r[:, None] // (2 * b)) == (r[None, :] // (2 * b))
        c[:, C_LVL + lv * P:C_LVL + (lv + 1) * P] = same & ((r[None, :] // b) % 2 == 1) & ((r[:, None] // b) % 2 == 0)
    c[:, C_AM:C_AM + P] = np.where(r[None, :] > r[:, None], 0, NEG)
    c[:, C_AM + P:C_AM + 2 * P] = np.where(r[None, :] <= r[:, None], 0, NEG)
    inv = THETA ** (-np.arange(HALF, dtype=np.float64) / HALF)
    for t in range(TT):
        ang = (r[:, None] + t * P) * inv[None, :]
        c[:, C_COS + t * HALF:C_COS + (t + 1) * HALF] = np.cos(ang)
        c[:, C_SIN + t * HALF:C_SIN + (t + 1) * HALF] = np.sin(ang)
    c[:, C_IOTA:C_IOTA + P] = r[None, :]
    c[:, C_I8:C_I8 + E] = np.arange(E)[None, :]
    return c


def shape_constants_b(dtype):
    r = np.arange(P)
    return np.concatenate([np.eye(P), np.where(r[:, None] <= r[None, :], 0, NEG)], axis=1).astype(dtype)


def build(nc, dram, out, limit=99):
    with ExitStack() as ctx:
        def sb(name, shape, dt=F32):
            return ctx.enter_context(nc.sbuf_tensor(name, [P] + shape, dt))

        sems = {}

        def sem(name):
            if name not in sems:
                sems[name] = ctx.enter_context(nc.semaphore(name))
            return sems[name]

        ps = ctx.enter_context(nc.psum_tensor("ps", [P, 8, 512], F32))

        const = sb("const", [C_W])
        identb = sb("identb", [P], BF16)
        maskb = sb("maskb", [P], BF16)
        zerob = sb("zerob", [512], BF16)
        ones = sb("ones", [P])
        x_tok = sb("x_tok", [TT, D])
        xT = sb("xT", [KD, SEQ])
        ln_gb = sb("ln_gb", [2, D])
        prow_a = sb("prow_a", [P])
        prow_b = sb("prow_b", [P])
        pcol = sb("pcol", [2 * P])
        w_ba = sb("w_ba", [KD, 2 * DH])
        w_dt = sb("w_dt", [KD, SH])
        w_rt = sb("w_rt", [KD, E])
        sinks = sb("sinks", [AH])
        dn_al = sb("dn_al", [DH])
        dn_dtb = sb("dn_dtb", [DH])
        dn_nw = sb("dn_nw", [DD])
        ssm_al = sb("ssm_al", [SH])
        ssm_dtb = sb("ssm_dtb", [SH])
        ssm_db = sb("ssm_db", [SH])
        dcol = sb("dcol", [NX])
        brt = sb("brt", [E])
        stats = sb("stats", [TT, 2, 6])
        mv = sb("mv", [TT, 2])
        rstd = sb("rstd", [TT])
        nhalf = sb("nhalf", [TT])
        eps_rms = sb("eps_rms", [1])
        with ExitStack() as early:
            ring = early.enter_context(nc.sbuf_tensor("ring", [P, RING * SLOT], F32))
            arena = early.enter_context(nc.sbuf_tensor("arena", [P, 27200], F32))
        raw = sb("raw", [RAW, PIECE])
        w_hi = sb("w_hi", [CUT, PIECE], F32R)
        w_lo = sb("w_lo", [CUT, PIECE], F32R)
        xT_hi = sb("xT_hi", [KD, SEQ], F32R)
        xT_lo = sb("xT_lo", [KD, SEQ], F32R)
        xg_hi = sb("xg_hi", [KD, P], F32R)
        xg_lo = sb("xg_lo", [KD, P], F32R)
        ehT_hi = sb("ehT_hi", [2, 4, P], F32R)
        ehT_lo = sb("ehT_lo", [2, 4, P], F32R)
        esg = sb("esg", [2, EW])
        eh = sb("eh", [2, EW])
        with ExitStack() as late:
            y_hi = late.enter_context(nc.sbuf_tensor("y_hi", [P, NX, SEQ], F32R))
        sel_rows = sb("sel_rows", [TT, P])
        sel_gate = sb("sel_gate", [TT, P])
        G = sb("G", [TT, P])
        oe = sb("oe", [D])
        yacc = sb("yacc", [TT, D])
        lg = sb("lg", [TT, E])
        top8 = sb("top8", [TT, 8])
        idx8 = sb("idx8", [TT, 8])
        idxf = sb("idxf", [TT, 2])
        oh1 = sb("oh1", [TT, E])
        oh2 = sb("oh2", [TT, E])
        dm = sb("dm", [TT, 1])
        g1 = sb("g1", [TT, 1])
        g2 = sb("g2", [TT, 1])
        comb = sb("comb", [TT, E])
        sel = sb("sel", [TT, E])
        rank = sb("rank", [TT, E])
        rank2 = sb("rank2", [TT, E])
        cnt = sb("cnt", [1])
        over = sb("over", [1])

        ident = const[:, C_ID:C_ID + P]
        tri = const[:, C_TRI:C_TRI + P]
        tris = const[:, C_TRIS:C_TRIS + P]
        iota = const[:, C_IOTA:C_IOTA + P]
        iota8 = const[:, C_I8:C_I8 + E]

        def ssm_tap(k, j):
            return pcol[:, k * NXBC + j:k * NXBC + j + 1]

        def dn_tap(k, j):
            return pcol[:, P + k * NDN + j:P + k * NDN + j + 1]

        def ssm_nw(j):
            return pcol[:, P + CONV * NDN + j:P + CONV * NDN + j + 1]

        def ssm_cb(j):
            return pcol[:, P + CONV * NDN + NX + j:P + CONV * NDN + NX + j + 1]

        CUT_END = RAW * PIECE + 2 * CUT * PIECE + 2 * KD * SEQ - RING * SLOT

        top = [0]

        def take(*shape, at=None):
            n = int(np.prod(shape))
            if at is not None:
                top[0] = at
            a = arena[:, top[0]:top[0] + n]
            top[0] += n
            assert top[0] <= 27200, top[0]
            if len(shape) == 2:
                a = a.rearrange("p (a b) -> p a b", b=shape[1])
            if len(shape) == 3:
                a = a.rearrange("p (a b c) -> p a b c", b=shape[1], c=shape[2])
            return a

        dnT = take(NDN, SEQ, at=CUT_END)
        qkv = take(TT, 768)
        gate = take(TT, DH * DD)
        mixT = take(KD, SEQ)
        rt = take(4, TT * 10 * HALF)
        ba = take(TT, 2 * DH)
        beta = take(TT, DH)
        gdn = take(TT, DH)
        zdn = take(TT, DH)
        adn = take(TT, DH)
        e2dn = take(TT, DH)
        ebdn = take(TT, DH)
        eadn = take(DH)
        mx = take(2, AH)
        nmx = take(2, AH)
        sdx = take(2, AH)
        den = take(2, AH)
        rden = take(2, AH)
        ngc = take(TT, DH)
        ddk = take(DH)
        dke = take(DH)
        egc1 = take(DH)
        bege = take(DH)
        oss = take(TT * DH)
        orn = take(TT * DH)
        tail = top[0]
        pT = take(3 * AH, P)
        qT = take(4, SEQ)
        s = take(AH, 384, at=0)
        kT = take(SEQ)
        sq = pT.rearrange("p a b -> p (a b)")[:, 0:2048]
        rn = arena[:, tail + 2048:tail + 4096]
        top[0] = 4096
        decT = take(8, P)
        attnT = take(8, P)
        AT = take(8, P)
        LT = take(2, 8, P)
        X = take(8, P)
        XT = take(8, P)
        Pm = take(8, P)
        vb = take(8, P)
        kdec = take(4, P)
        kbe = take(4, P)
        u = take(8, P, at=0)
        wT = take(4, P)
        S1 = take(4, P)
        vnew = take(4, P)
        o = take(8, P, at=4096 + 3072)
        osq = take(8, P)

        sg = take(2, 512, at=20480)
        hT = take(512)

        hT_hi = ehT_hi[:, 0].rearrange("p k t -> p (k t)").rearrange("p (k t) -> p k t", k=2)
        hT_lo = ehT_lo[:, 0].rearrange("p k t -> p (k t)").rearrange("p (k t) -> p k t", k=2)

        xdt = take(TT, SI, at=0)
        xdec = take(SI)
        Btok = take(SG * SN)
        state = take(SI)
        seg = take(2, 8, P)
        MT = take(2, 8, P)
        cb = take(8, P)
        xbcT = take(NXBC, SEQ, at=CUT_END)
        zT = take(NX, SEQ)
        er = take(2, 512)
        yo = take(2, 512)
        ysq = xbcT[:, NX:NXBC, :].rearrange("p (a b) t -> p a (b t)", a=2)
        yrn = er.rearrange("p a b -> p (a b)").rearrange("p (g t) -> p g t", g=SG)

        def y_lo(k):
            if isinstance(k, int):
                return (xT_hi, xT_lo)[k // KD][:, k % KD, :]
            return (xT_hi, xT_lo)[k.start // KD][:, k.start % KD:k.start % KD + k.stop - k.start, :]

        sz = take(TT, SH)
        sdt = take(TT, SH)
        saz = take(TT, SH)
        se2 = take(TT, SH)
        dA = take(TT, SH)
        sea = take(SH)
        nacs = take(TT, SH)
        sdd = take(SH)
        sdec = take(SH)

        def bc(ap, n):
            return ap.unsqueeze(2).to_broadcast([P, ap.shape[1], n])

        def over_heads(ap, n):
            return ap.unsqueeze(1).to_broadcast([P, n, ap.shape[1]])

        def slot(i):
            return ring[:, i * SLOT:(i + 1) * SLOT]

        w_in0, w_out0 = dram["even_w_in"][0], dram["even_w_out"][0]
        w_in1, w_out1 = dram["ssm_w_in"][0], dram["ssm_w_out"][0]

        def cols(w, a, n):
            return w.rearrange("(k p) n -> p k n", p=P)[:, :, a:a + n]

        def rows(w, a, n):
            return w.rearrange("(k p) n -> p k n", p=P)[:, a:a + n, :]

        pieces0 = {n: cols(w_in0, B0 + 2 * P * q, 2 * P) for q, n in enumerate(N_DN)}
        for n, at, width in ((N_GATE, G0, 512), (N_Q, Q0, 512), (N_KV, K0, 256)):
            for half in range(2):
                pieces0[n + half] = cols(w_in0, at, width)[:, 4 * half:4 * half + 4, :]
        out_units = [(rows(w_out0, 4 * i, 4), 2 + i) for i in range(2)]
        loaded = [sem(f"slot{i}_loaded") for i in range(RING)]
        raw_loaded = [sem(f"raw{i}_loaded") for i in range(RAW)]
        lo_made = sem("lo_made")
        piece_used = sem("piece_used")
        d_lo_made = sem("dense_lo_made")
        d_piece_used = sem("dense_piece_used")

        def piece_size(n):
            return PIECE // 2 if isinstance(n, int) and N_KV <= n < N0 else PIECE

        def raw_before(i):
            return 16 * len(range(i, NPRE, RAW_D)) if i < RAW_D else 0

        block = ctx.enter_context(nc.Block())

        @block.sync
        def _(sp):
            sp.dma_start(x_tok[:, :, :], dram["x"][0].rearrange("(t p) d -> p t d", p=P)).then_inc(sem("x_loaded"), 16)
            sp.dma_start(const[:, :], dram["shape_consts"]).then_inc(sem("x_loaded"), 16)

            def fill(dst, src, s_):
                k = src.shape[1] // 2
                sp.dma_start(dst[:, 0:k, :], src[:, 0:k, :]).then_inc(s_, 16)
                sp.dma_start(dst[:, k:2 * k, :], src[:, k:2 * k, :]).then_inc(s_, 16)

            def unit(src, i):
                fill(slot(i)[:, :].rearrange("p (k n) -> p k n", n=D), src, loaded[i])

            wg, wu, wd = dram["ffn_w_gate"][0], dram["ffn_w_up"][0], dram["ffn_w_down"][0]

            def piece(n, i, src):
                sp.wait_ge(d_lo_made, n + 1)
                k, width = src.shape[1], src.shape[2]
                sp.dma_start(raw[:, i, 0:k * width].rearrange("p (k n) -> p k n", k=k), src).then_inc(raw_loaded[i], 16)

            def gu_piece(w, step):
                return w.rearrange("(k p) n -> p k n", p=P)[:, :, bass.ds(step * FW, FW)]

            def d_piece(step):
                return wd.rearrange("(s k p) n -> s p k n", k=2, p=P)[step]

            sp.sem_inc(d_lo_made, RAW_D)
            for n in range(N0):
                piece(n, n % RAW_D, pieces0[n])
            sp.wait_ge(d_lo_made, RAW_D + N0)
            unit(*out_units[0])
            sp.wait_ge(d_piece_used, CUT + N0)
            unit(*out_units[1])
            if limit < 2:
                return
            piece(N0, 0, gu_piece(wg, 0))
            piece(N0 + 1, 1, gu_piece(wu, 0))
            with sp.Fori(0, FSTEPS // 2) as i:
                piece(6 * i + (N0 + 2), 2, gu_piece(wg, 2 * i + 1))
                piece(6 * i + (N0 + 3), 3, gu_piece(wu, 2 * i + 1))
                sp.wait_ge(sem("out_proj"), 1)
                piece(6 * i + (N0 + 4), 4, d_piece(2 * i))
                piece(6 * i + (N0 + 5), 5, gu_piece(wg, 2 * i + 2))
                piece(6 * i + (N0 + 6), 0, gu_piece(wu, 2 * i + 2))
                piece(6 * i + (N0 + 7), 1, d_piece(2 * i + 1))
            piece(N1 - 1, (N1 - 1) % RAW_D, d_piece(FSTEPS - 1))
            if limit < 3:
                return
            for m, (kind, pair) in enumerate(PROJ):
                n = N1 + m
                piece(n, n % RAW_D, cols(w_in1, (SI if kind == 0 else 0) + 2 * P * pair, 2 * P))
            for i in range(N_OUT):
                n = N2 + i
                piece(n, n % RAW_D, rows(w_out1, 2 * i, 2))
            if limit < 5:
                return

            eg, eu, ed = dram["moe_w_gate"][0], dram["moe_w_up"][0], dram["moe_w_down"][0]
            for i in range(RAW):
                if i < RAW_D:
                    sp.wait_ge(d_lo_made, RAW_D + (NPRE - 1 - (NPRE - 1 - i) % RAW_D) + 1)
                sp.sem_inc(lo_made, 1)

            def expert_loads(e, it):
                for n in range(PPE):
                    (j, what), half = ORDER[n // PPU], n % PPU
                    sp.wait_ge(lo_made, PPE * it + (n + 1))
                    i = n % RAW
                    if what < 2:
                        src = (eg, eu)[what][e].rearrange("(k p) n -> p k n", p=P)[:, 4 * half:4 * half + 4, EW * j:EW * (j + 1)]
                    else:
                        src = ed[e].rearrange("(k p) n -> p k n", p=P)[:, 4 * j + 2 * half:4 * j + 2 * half + 2, :]
                    sp.dma_start(raw[:, i, :].rearrange("p (k n) -> p k n", k=src.shape[1]), src).then_inc(raw_loaded[i], 16)

            with sp.Fori(0, E) as e:
                expert_loads(e, e)
            sp.wait_ge(sem("overflow_known"), 1)
            more = sp.value_load(over[0:1, 0:1].bitcast(I32), min_val=0, max_val=SEQ)
            with sp.If(more > 0):
                with sp.Fori(0, E) as e:
                    expert_loads(e, e + E)

        @block.gpsimd
        def _(pool):
            pool.memset(ones[:, :], 1.0).then_inc(sem("pool_set"), 1)
            pool.memset(zerob[:, :], 0.0).then_inc(sem("pool_set"), 1)
            pool.memset(nhalf[:, :], -0.5).then_inc(sem("pool_set"), 1)
            pool.wait_ge(sem("pool_set"), 3)
            def join(n):
                pool.wait_ge(sem("xT_lo_made"), 4 * (n + 1))
                pool.tensor_tensor(xT[:, :, :], xT_hi[:, :, :].bitcast(F32), xT_lo[:, :, :].bitcast(F32), ALU.add
                                   ).then_inc(sem("xT_joined"), 1)

            join(0)
            for n in range(2 * DEPTH):
                if n >= limit:
                    break
                for t in range(TT):
                    pool.wait_ge(sem("ln_var"), TT * n + t + 1)
                    pool.tensor_tensor(rstd[:, t:t + 1], mv[:, t, 1:2], nhalf[:, t:t + 1], ALU.pow).then_inc(sem("ln_rstd"), 1)
                if n == 1 and limit > 2:
                    join(2)

        @block.scalar
        def _(act):
            def small(dst, src, loaded_="params_loaded"):
                act.dma_start(dst, src).then_inc(sem(loaded_), 16)

            def row(name, *idx):
                a = dram[name]
                for i in idx:
                    a = a[i]
                return a.partition_broadcast(P)

            small(prow_b[0:CONV * NDN, :], dram["dn_conv_w"][0].rearrange("k (j p) -> (k j) p", p=P), "taps_loaded")
            small(prow_b[CONV * NDN:CONV * NDN + NX, :], dram["ssm_norm_w"][0].rearrange("(j p) -> j p", p=P), "taps_loaded")
            small(prow_b[CONV * NDN + NX:CONV * NDN + NX + NXBC, :], dram["ssm_conv_b"][0].rearrange("(j p) -> j p", p=P), "taps_loaded")
            small(prow_a[0:CONV * NXBC, :], dram["ssm_conv_w"][0].rearrange("k (j p) -> (k j) p", p=P), "taps_loaded")
            small(w_ba[:, :, :], cols(w_in0, BA0, 2 * DH))
            small(identb[:, :], dram["shape_consts_b"][:, 0:P])
            small(maskb[:, :], dram["shape_consts_b"][:, P:2 * P])
            small(sinks[:, :], row("swa_sinks", 0))
            small(dn_al[:, :], row("dn_a_log", 0))
            small(dn_dtb[:, :], row("dn_dt_bias", 0))
            small(dn_nw[:, :], row("dn_norm_w", 0))
            small(w_dt[:, :, :], cols(w_in1, SI + NXBC * P, SH))
            small(ssm_al[:, :], row("ssm_a_log", 0))
            small(ssm_dtb[:, :], row("ssm_dt_bias", 0))
            small(ssm_db[:, :], row("ssm_d", 0))
            small(w_rt[:, :, :], cols(dram["moe_w_router"][0], 0, E))
            small(brt[:, :], row("moe_b_router", 0))

            def load_ln(n):
                if n:
                    act.wait_ge(sem("ln_done"), TT * n)
                act.dma_start(ln_gb[:, 0], dram["ln_g"][n // 2][n % 2].partition_broadcast(P)).then_inc(sem("ln_loaded"), 16)
                act.dma_start(ln_gb[:, 1], dram["ln_b"][n // 2][n % 2].partition_broadcast(P)).then_inc(sem("ln_loaded"), 16)

            def turn_high(n):
                for b in range(4):
                    t, q = b // 2, b % 2
                    act.wait_ge(sem("x_turned"), 4 * n + b + 1)
                    act.copy(xT_hi[:, 4 * q:4 * q + 4, t * P:(t + 1) * P], ps[:, b, :].rearrange("p (k t) -> p k t", k=4)
                             ).then_inc(sem("xT_hi_made"), 1)

            def dense_high(n, i, c, rounds):
                act.wait_ge(raw_loaded[i], 16 * rounds)
                act.wait_ge(d_piece_used, n + 1)
                size = piece_size(n)
                act.copy(w_hi[:, c, 0:size], raw[:, i, 0:size]).then_inc(sem("dense_hi_made"), 1)

            def turn_copies(n, quarters):
                for b in quarters:
                    t, q = b // 2, b % 2
                    act.wait_ge(sem("x_turned"), 4 * n + b + 1)
                    act.copy(xT[:, 4 * q:4 * q + 4, t * P:(t + 1) * P], ps[:, b, :].rearrange("p (k t) -> p k t", k=4)
                             ).then_inc(sem("xT_copied"), 1)

            act_step = [0]

            def link(ins):
                act_step[0] += 1
                ins.then_inc(sem("act_step"), 1)
                act.wait_ge(sem("act_step"), act_step[0])

            turn_high(0)
            for n in range(CUT):
                dense_high(n, n, n, 1)
            for m in range(N0):
                n = m + CUT
                if n < N0:
                    dense_high(n, n % RAW_D, n % CUT, n // RAW_D + 1)
                if m in N_DN:
                    q = N_DN.index(m)
                    act.wait_ge(sem("dn_conv"), q + 1)
                    act.activation(dnT[:, 2 * q:2 * q + 2, :], dnT[:, 2 * q:2 * q + 2, :], ACT.Silu).then_inc(sem("dn_silu"), 1)
                if m == N_GATE + 1:
                    act.wait_ge(d_piece_used, CUT + m + 1)
                    for t in range(TT):
                        act.activation(gate[:, t, :], ps[:, 4 + t, :], ACT.Silu).then_inc(sem("gate_silu"), 1)
            load_ln(0)
            act.wait_ge(sem("params_loaded"), 16 * 13)
            act.activation(eadn[:, :], dn_al[:, :], ACT.Exp).then_inc(sem("dn_eb"), 1)
            act.wait_ge(sem("dn_z"), 1)
            act.activation(adn[:, :, :], adn[:, :, :], ACT.Exp, scale=-1.0).then_inc(sem("dn_e1"), 1)
            act.activation(ebdn[:, :, :], ba[:, :, 0:DH], ACT.Exp, scale=-1.0).then_inc(sem("dn_eb"), 1)
            act.wait_ge(sem("dn_e1"), 1)
            act.activation(e2dn[:, :, :], adn[:, :, :], ACT.Ln, bias=1.0).then_inc(sem("dn_e2"), 1)
            for b in range(4):
                act.wait_ge(sem("dn_ss"), b + 1)
                act.activation(rn[:, 512 * b:512 * b + 512], ps[:, b, :], ACT.Ln, bias=eps_rms[:, 0:1]).then_inc(sem("norm_ln"), 1)
            for b in range(4):
                act.wait_ge(sem("norm_ln"), b + 1)
                act.activation(rn[:, 512 * b:512 * b + 512], rn[:, 512 * b:512 * b + 512], ACT.Exp, scale=-0.5).then_inc(sem("dn_rn"), 1)
            act.wait_ge(sem("dn_cols"), 1)
            act.activation(dke[:, :], ddk[:, :], ACT.Exp).then_inc(sem("dn_dke"), 1)
            act.activation(egc1[:, :], ngc[:, 1, :], ACT.Exp, scale=-1.0).then_inc(sem("dn_dke"), 1)
            for t in range(TT):
                act.wait_ge(sem("dn_gcrow"), t + 1)
                for h in range(DH):
                    act.activation(decT[:, t * DH + h, :], ps[:, t, h * P:(h + 1) * P], ACT.Exp, bias=ngc[:, t, h:h + 1]
                                   ).then_inc(sem("dn_dec"), 1)

            def exponentials(n):
                act.wait_ge(sem("att_max"), 1)
                for h in range(AH):
                    seg_ = s[:, h, 0:256] if n == 1 else s[:, h, 256:384]
                    act.activation(seg_, seg_, ACT.Exp, bias=nmx[:, n, h:h + 1], accum_out=den[:, n, h:h + 1]
                                   ).then_inc(sem("att_exp"), 1)
                if n == 1:
                    act.activation(sdx[:, :, :], sdx[:, :, :], ACT.Exp).then_inc(sem("att_exp"), 1)

            def copy_p(b):
                act.wait_ge(sem("p_turned"), b + 1)
                act.copy(pT[:, 4 * b:4 * b + 4, :], ps[:, 7, :].rearrange("p (k t) -> p k t", k=4)).then_inc(sem("pT_copied_act"), 1)

            def copy_mix(b):
                act.wait_ge(sem("att_out"), b + 1)
                act.copy(mixT[:, 2 * b:2 * b + 2, :], ps[:, 6 + b, :].rearrange("p (k t) -> p k t", k=2)).then_inc(sem("mix_att"), 1)

            def attention(lv, half):
                at = (lv, half)
                if at == (3, 0):
                    exponentials(0)
                elif at == (3, 1):
                    exponentials(1)
                elif at == (4, 1):
                    copy_p(1)
                elif at == (5, 0):
                    copy_p(3)
                elif at == (5, 1):
                    copy_p(5)
                elif at == (6, 0):
                    copy_mix(0)
                elif at == (6, 1):
                    copy_mix(1)
            for lv in range(1, LEVELS):
                for t in range(TT):
                    act.wait_ge(sem("inv_P"), 2 * lv + t + 1)
                    act.copy(Pm[:, t * DH:(t + 1) * DH, :], ps[:, t, :].rearrange("p (h c) -> p h c", h=DH)).then_inc(sem("inv_P_copied"), 1)
                attention(lv, 0)
                attention(lv, 1)
            act.wait_ge(sem("dn_w"), 1)
            act.copy(wT[:, :, :], ps[:, 2, :].rearrange("p (h c) -> p h c", h=DH)).then_inc(sem("dn_w_copied"), 1)
            act.wait_ge(sem("dn_S"), 1)
            act.copy(S1[:, :, :], ps[:, 4, :].rearrange("p (h c) -> p h c", h=DH)).then_inc(sem("dn_S_copied"), 1)
            act.wait_ge(sem("dn_oss"), 1)
            link(act.activation(orn[:, :], oss[:, :], ACT.Ln, bias=eps_rms[:, 0:1], scale=1.0 / DD))
            act.activation(orn[:, :], orn[:, :], ACT.Exp, scale=-0.5).then_inc(sem("dn_orn"), 1)
            act.wait_ge(sem("o_turned"), 2)
            act.copy(mixT[:, 4:8, P:2 * P], ps[:, 1, :].rearrange("p (h c) -> p h c", h=DH)).then_inc(sem("mix_dn"), 1)
            if limit < 2:
                load_ln(1)
                act.wait_ge(sem("ln_loaded"), 64)
                return
            act.wait_ge(sem("out_proj"), 2)
            for n in range(N0, N0 + CUT):
                dense_high(n, n % RAW_D, n % CUT, n // RAW_D + 1)
            load_ln(1)
            turn_high(1)

            def ffn_silu(b, step):
                act.wait_ge(d_piece_used, 3 * step + (CUT + N0 + 2))
                act.activation(sg[:, b, :], ps[:, 2 * b, :], ACT.Silu).then_inc(sem("ffn_silu"), 1)

            with act.Fori(0, FSTEPS // 2) as i:
                dense_high(6 * i + (N0 + 3), 3, 0, i + (N0 // RAW_D + 1))
                ffn_silu(0, 2 * i)
                dense_high(6 * i + (N0 + 4), 4, 1, i + (N0 // RAW_D + 1))
                dense_high(6 * i + (N0 + 5), 5, 2, i + (N0 // RAW_D + 1))
                dense_high(6 * i + (N0 + 6), 0, 0, i + (N0 // RAW_D + 2))
                ffn_silu(1, 2 * i + 1)
                dense_high(6 * i + (N0 + 7), 1, 1, i + (N0 // RAW_D + 2))
                dense_high(6 * i + (N0 + 8), 2, 2, i + (N0 // RAW_D + 2))
            ffn_silu(0, FSTEPS - 1)
            if limit < 3:
                load_ln(2)
                act.wait_ge(sem("ln_loaded"), 96)
                return
            for n in range(N1, N1 + CUT):
                dense_high(n, n % RAW_D, n % CUT, n // RAW_D + 1)
            load_ln(2)
            turn_high(2)
            for m, (kind, q) in enumerate(PROJ):
                n = N1 + m + CUT
                if n < N2:
                    dense_high(n, n % RAW_D, n % CUT, n // RAW_D + 1)
                if kind == 0:
                    act.wait_ge(sem("ssm_conv"), q + 1)
                    for j in (2 * q, 2 * q + 1):
                        act.activation(xbcT[:, j, :], xbcT[:, j, :], ACT.Silu, bias=ssm_cb(j)).then_inc(sem("ssm_silu"), 1)
                else:
                    act.wait_ge(d_piece_used, CUT + N1 + m + 1)
                    act.activation(zT[:, 2 * q:2 * q + 2, :], ps[:, 4 + q % 4, :].rearrange("p (k t) -> p k t", k=2), ACT.Silu
                                   ).then_inc(sem("z_silu"), 1)
            act.wait_ge(sem("ssm_z"), 1)
            link(act.activation(saz[:, :, :], saz[:, :, :], ACT.Exp, scale=-1.0))
            act.activation(se2[:, :, :], saz[:, :, :], ACT.Ln, bias=1.0).then_inc(sem("ssm_sp"), 1)
            act.activation(sea[:, :], ssm_al[:, :], ACT.Exp).then_inc(sem("ssm_sp"), 1)
            act.wait_ge(sem("B_turned"), 1)
            act.copy(Btok[:, :], ps[:, 0, :]).then_inc(sem("B_copied"), 1)
            act.wait_ge(sem("ssm_cols"), 1)
            act.activation(sdec[:, :], sdd[:, :], ACT.Exp).then_inc(sem("ssm_dec"), 1)
            for t in range(TT):
                act.wait_ge(sem("cb_made"), t + 1)
                act.copy(cb[:, 4 * t:4 * t + 4, :], ps[:, 2 + t, :].rearrange("p (g c) -> p g c", g=SG)).then_inc(sem("cb_copied"), 1)
            for g in range(SG):
                act.wait_ge(sem("state_made"), g + 1)
                act.copy(state[:, 512 * g:512 * g + 512], ps[:, 4 + g, :]).then_inc(sem("state_copied"), 1)
            for i in range(TT * SG):
                t, g = i // SG, i % SG
                act.wait_ge(sem("acs_rows"), i + 1)
                if i >= 2:
                    act.wait_ge(sem("MT_made"), i - 1)
                for r in range(8):
                    h = 8 * g + r
                    act.activation(seg[:, i % 2, r, :], ps[:, 2 * (i % 2) + r // 4, (r % 4) * P:(r % 4 + 1) * P], ACT.Exp,
                                   bias=nacs[:, t, h:h + 1]).then_inc(sem("seg_made"), 1)
            for q in range(4):
                act.wait_ge(sem("yoff_made"), q + 1)
                if q >= 2:
                    act.wait_ge(sem("yoff_added"), q - 1)
                act.activation(er[:, q % 2, :], ps[:, 1 + 2 * (q % 2), :], ACT.Exp).then_inc(sem("er_made"), 1)
            dense_high(N2, N2 % RAW_D, N2 % CUT, N2 // RAW_D + 1)
            act.wait_ge(sem("yoff_added"), 4)
            for g in range(SG):
                act.wait_ge(sem("y_ss"), g + 1)
                act.activation(yrn[:, g, :], ps[:, 4 + g, 0:SEQ], ACT.Ln, bias=eps_rms[:, 0:1], scale=1.0 / (SI // SG)
                               ).then_inc(sem("norm_ln"), 1)
            for g in range(SG):
                act.wait_ge(sem("norm_ln"), 4 + g + 1)
                act.activation(yrn[:, g, :], yrn[:, g, :], ACT.Exp, scale=-0.5).then_inc(sem("y_rn"), 1)
            for g in range(SG):
                act.wait_ge(sem("y_full"), g + 1)
                act.copy(y_hi[:, 4 * g:4 * g + 4, :], xbcT[:, 4 * g:4 * g + 4, :]).then_inc(sem("y_hi_made"), 1)
                if g < CUT - 1:
                    n = N2 + g + 1
                    dense_high(n, n % RAW_D, n % CUT, n // RAW_D + 1)
            for n in range(N2 + CUT, NPRE):
                dense_high(n, n % RAW_D, n % CUT, n // RAW_D + 1)
            def cut_high(n, it):
                i = n % RAW
                act.wait_ge(raw_loaded[i], 16 * (PPE // RAW) * it + (16 * (n // RAW + 1) + raw_before(i)))
                act.wait_ge(piece_used, PPE * it + (n + 1))
                act.copy(w_hi[:, n % CUT, :], raw[:, i, :]).then_inc(sem("hi_made"), 1)

            if limit >= 5:
                act.wait_ge(d_piece_used, CUT + NPRE)
                cut_high(0, 0)
            turn_copies(3, (0, 1))
            if limit >= 5:
                cut_high(1, 0)
                cut_high(2, 0)
            turn_copies(3, (2,))
            load_ln(3)
            if limit < 5:
                act.wait_ge(sem("ln_loaded"), 128)
                return
            act.wait_ge(sem("rt_dm"), 1)
            act.activation(g1[:, :, :], dm[:, :, :], ACT.Exp).then_inc(sem("rt_e"), 1)

            def gathered_high(it):
                for q in range(2):
                    act.wait_ge(sem("xg_made"), 2 * it + (q + 1 + FIRST))
                    act.copy(xg_hi[:, 4 * q:4 * q + 4, :], ps[:, 2 + q, :].rearrange("p (k t) -> p k t", k=4)
                             ).then_inc(sem("xg_hi_made"), 1)

            def expert_act(it, following):
                def silu(j):
                    act.wait_ge(piece_used, PPE * it + (CUT + last_piece(j, 1) + 1))
                    if j >= 2:
                        act.wait_ge(sem("e_h"), ESTEPS * it + (j - 1) + FIRST)
                    else:
                        act.wait_ge(sem("e_h"), ESTEPS * it + FIRST)
                    act.activation(esg[:, j % 2, :], ps[:, 2 * (j % 2), :], ACT.Silu).then_inc(sem("e_silu"), 1)

                def turned(j):
                    act.wait_ge(sem("eh_turned"), ESTEPS * it + (j + 1))
                    act.copy(ehT_hi[:, j % 2], ps[:, 4, :].rearrange("p (k t) -> p k t", k=4)).then_inc(sem("ehT_hi_made"), 1)

                for n in range(CUT, PPE):
                    cut_high(n, it)
                    for j in range(ESTEPS):
                        if n == last_piece(j, 1) + 2:
                            silu(j)
                        if j and n == last_piece(j, 0) + 2:
                            turned(j - 1)
                    if n == PPE - 2 and following is not None:
                        gathered_high(following)
                turned(ESTEPS - 1)
                if following is not None:
                    cut_high(0, following)
                    cut_high(1, following)
                act.wait_ge(piece_used, PPE * it + (CUT + PPE))
                act.copy(oe[:, 512:1024], ps[:, 6, :]).then_inc(sem("oe_copied_act"), 1)
                if following is not None:
                    cut_high(2, following)

            gathered_high(0)
            with act.Fori(0, E - 1) as e:
                expert_act(e, e + 1)
            expert_act(E - 1, None)
            act.wait_ge(sem("overflow_known"), 1)
            more = act.value_load(over[0:1, 0:1].bitcast(I32), min_val=0, max_val=SEQ)
            with act.If(more > 0):
                with act.Fori(0, E) as e:
                    for n in range(CUT):
                        cut_high(n, e + E)
                    gathered_high(e + E)
                    expert_act(e + E, None)
            for t in range(TT):
                act.wait_ge(sem("ln_done"), TT * 3 + t + 1)
                act.dma_start(out[0, t * P:(t + 1) * P, :], yacc[:, t, :]).then_inc(sem("out_stored"), 16)
            act.wait_ge(sem("out_stored"), 16 * TT)

        @block.vector
        def _(dve):
            step = [0]

            def link(ins):
                step[0] += 1
                ins.then_inc(sem("dve_step"), 1)
                dve.wait_ge(sem("dve_step"), step[0])

            TTO, TS, STT = dve.tensor_tensor, dve.tensor_scalar, dve.scalar_tensor_tensor

            def four(ap):
                return ap.rearrange("p (k t) -> p k t", k=4)

            def turn_copies(n):
                dve.wait_ge(sem("x_turned"), 4 * n + 4)
                dve.tensor_copy(xT[:, 4:8, P:2 * P], four(ps[:, 3, :])).then_inc(sem("xT_copied"), 1)

            def turn_low(n):
                for b in range(4):
                    t, q = b // 2, b % 2
                    ks = slice(4 * q, 4 * q + 4)
                    dve.wait_ge(sem("xT_hi_made"), 4 * n + b + 1)
                    TTO(xT_lo[:, ks, t * P:(t + 1) * P], four(ps[:, b, :]), xT_hi[:, ks, t * P:(t + 1) * P].bitcast(F32),
                        ALU.subtract).then_inc(sem("xT_lo_made"), 1)

            def dense_low(n, i, c):
                dve.wait_ge(sem("dense_hi_made"), n + 1)
                size = piece_size(n)
                TTO(w_lo[:, c, 0:size], raw[:, i, 0:size], w_hi[:, c, 0:size].bitcast(F32), ALU.subtract).then_inc(d_lo_made, 1)

            def layer_norm(n, ready, x=x_tok, add=True):
                dve.wait_ge(sem("ln_loaded"), 32 * (n + 1))
                for t in range(TT):
                    xt = x[:, t, :]
                    dve.wait_ge(*ready[t])
                    if add:
                        halves = xt.rearrange("p (b n) -> p b n", b=2)
                        link(STT(halves, halves, ALPHA, ps[:, 4 + 2 * t:6 + 2 * t, :], ALU.mult, ALU.add))
                    dve.bn_stats(stats[:, t, 0, :], xt[:, 0:512])
                    link(dve.bn_stats(stats[:, t, 1, :], xt[:, 512:1024]))
                    link(dve.bn_aggr(mv[:, t, :], stats[:, t, :, :].rearrange("p b s -> p (b s)")))
                    TS(mv[:, t, 1:2], mv[:, t, 1:2], LN_EPS, None, ALU.add).then_inc(sem("ln_var"), 1)
                    link(STT(xt, xt, mv[:, t, 0:1], ln_gb[:, 0, :], ALU.subtract, ALU.mult))
                    dve.wait_ge(sem("ln_rstd"), TT * n + t + 1)
                    STT(xt, xt, rstd[:, t:t + 1], ln_gb[:, 1, :], ALU.mult, ALU.add).then_inc(sem("ln_done"), 1)

            def conv(chunks, src, dst, tap):
                for j in chunks:
                    last = TS(dst(j), src(j), tap(CONV - 1, j), None, ALU.mult)
                link(last)
                for k in range(1, CONV):
                    for j in chunks:
                        last = STT(dst(j)[:, k:SEQ], src(j)[:, 0:SEQ - k], tap(CONV - 1 - k, j), dst(j)[:, k:SEQ], ALU.mult, ALU.add)
                    if k < CONV - 1:
                        link(last)
                return last

            link(dve.memset(eps_rms[:, :], RMS_EPS))
            turn_low(0)
            for n in range(CUT):
                dense_low(n, n, n)
            dve.wait_ge(sem("params_turned"), 1)
            dve.wait_ge(sem("params_loaded"), 16 * 13)
            dve.tensor_copy(pcol[:, 0:CONV * NXBC], ps[:, 7, 0:CONV * NXBC])
            dve.tensor_copy(pcol[:, P:P + 88], ps[:, 7, P:P + 88])
            dve.tensor_copy(dcol[0:64, :], ssm_db[0:64, :].rearrange("p (j r) -> p j r", r=2)[:, :, 0])
            dve.tensor_copy(dcol[64:128, :], ssm_db[64:128, :].rearrange("p (j r) -> p j r", r=2)[:, :, 1]
                            ).then_inc(sem("params_copied"), 1)
            dve.wait_ge(sem("params_copied"), 1)
            for m in range(N0):
                n = m + CUT
                if n < N0:
                    dense_low(n, n % RAW_D, n % CUT)
                if m in N_DN:
                    q = N_DN.index(m)
                    dve.wait_ge(d_piece_used, CUT + m + 1)
                    conv((2 * q, 2 * q + 1), lambda j: ps[:, (j // 2) % 4, (j % 2) * SEQ:(j % 2 + 1) * SEQ],
                         lambda j: dnT[:, j, :], dn_tap).then_inc(sem("dn_conv"), 1)
            for t in range(TT):
                dve.tensor_copy(qkv[:, t, 0:512].rearrange("p (c g d) -> p g c d", c=4, g=AKV),
                                ps[:, 6 + t, :].rearrange("p (g c d) -> p g c d", c=4, g=AKV)).then_inc(sem("q_copied"), 1)
            dve.wait_ge(sem("dn_silu"), NDN // 2)
            for b in range(4):
                TTO(sq[:, 512 * b:512 * b + 512].rearrange("p (k t) -> p k t", k=2), dnT[:, 2 * b:2 * b + 2, :],
                    dnT[:, 2 * b:2 * b + 2, :], ALU.mult).then_inc(sem("dn_sq"), 1)
            for t in range(TT):
                dve.wait_ge(sem("kv_proj"), t + 1)
                dve.tensor_copy(qkv[:, t, 512:768], ps[:, 4 + t, 0:256]).then_inc(sem("kv_copied"), 1)
                link(dve.tensor_copy(ba[:, t, :], ps[:, 4 + t, 256:256 + 2 * DH]))
            link(TTO(zdn[:, :, :], ba[:, :, DH:2 * DH], over_heads(dn_dtb[:, :], TT), ALU.add))
            STT(adn[:, :, :], zdn[:, :, :], -1.0, zdn[:, :, :], ALU.mult, ALU.max).then_inc(sem("dn_z"), 1)
            rn3 = rn[:, :].rearrange("p (k t) -> p k t", t=SEQ)
            dve.wait_ge(sem("dn_rn"), 2)
            STT(dnT[:, 0:4, :], dnT[:, 0:4, :], DD ** -0.5, rn3[:, 0:4, :], ALU.mult, ALU.mult).then_inc(sem("dn_qk"), 1)
            dve.wait_ge(sem("dn_rn"), 4)
            TTO(dnT[:, 4:8, :], dnT[:, 4:8, :], rn3[:, 4:8, :], ALU.mult).then_inc(sem("dn_qk"), 1)
            dve.wait_ge(sem("q_copied"), TT)
            dve.wait_ge(sem("kv_copied"), TT)
            qk4 = qkv[:, :, 0:640].rearrange("p t (h d) -> p t h d", d=AD)
            x1, x2 = qk4[:, :, :, 0:HALF], qk4[:, :, :, HALF:ROPE]

            def table(c):
                return const[:, c:c + TT * HALF].rearrange("p (t i) -> p t i", t=TT).unsqueeze(2).to_broadcast([P, TT, 10, HALF])

            r4 = [rt[:, i, :].rearrange("p (t h i) -> p t h i", t=TT, h=10) for i in range(4)]
            TTO(r4[0], x1, table(C_COS), ALU.mult)
            TTO(r4[1], x2, table(C_SIN), ALU.mult)
            TTO(r4[2], x2, table(C_COS), ALU.mult)
            link(TTO(r4[3], x1, table(C_SIN), ALU.mult))
            TTO(x1, r4[0], r4[1], ALU.subtract)
            TTO(x2, r4[2], r4[3], ALU.add).then_inc(sem("rope_done"), 1)
            dve.wait_ge(sem("dn_e2"), 1)
            dve.wait_ge(sem("dn_eb"), 2)
            link(STT(gdn[:, :, :], zdn[:, :, :], 0.0, e2dn[:, :, :], ALU.max, ALU.add))
            link(STT(gdn[:, :, :], gdn[:, :, :], -1.0, over_heads(eadn[:, :], TT), ALU.mult, ALU.mult))
            link(TS(beta[:, :, :], ebdn[:, :, :], 1.0, None, ALU.add))
            dve.reciprocal(beta[:, :, :], beta[:, :, :]).then_inc(sem("dn_gb"), 1)
            dve.wait_ge(sem("dn_gc"), 1)
            link(TS(ngc[:, :, :], ps[:, 4, 0:TT * DH].rearrange("p (t h) -> p t h", t=TT), -1.0, None, ALU.mult))
            TTO(ddk[:, :], ps[:, 4, 8:12], ngc[:, 0, :], ALU.add).then_inc(sem("dn_cols"), 1)
            dve.wait_ge(sem("dn_dke"), 2)
            dve.wait_ge(sem("dn_gb"), 1)
            link(TTO(bege[:, :], beta[:, 1, :], egc1[:, :], ALU.mult))
            for t in range(TT):
                dve.wait_ge(sem("dn_dec"), DH * (t + 1))
                dve.wait_ge(sem("dn_kk"), TT)
                hs = slice(t * DH, (t + 1) * DH)
                TTO(attnT[:, hs, :], four(ps[:, 6 + t, :]), decT[:, hs, :], ALU.mult)
                link(TTO(AT[:, hs, :], four(ps[:, 4 + t, :]), decT[:, hs, :], ALU.mult))
                TTO(AT[:, hs, :], AT[:, hs, :], four(ps[:, 2 + t, :]), ALU.mult).then_inc(sem("dn_A"), 1)
            dve.wait_ge(sem("dn_A"), TT)
            dve.wait_ge(sem("kv_turned"), 1)
            TTO(kdec[:, :, :], four(ps[:, 4, :]), bc(dke[:, :], P), ALU.mult)
            dve.wait_ge(sem("kv_turned"), 2)
            TTO(vb[:, 0:4, :], four(ps[:, 5, :]), bc(beta[:, 0, :], P), ALU.mult)
            dve.wait_ge(sem("kv_turned"), 3)
            TTO(kbe[:, :, :], four(ps[:, 6, :]), bc(bege[:, :], P), ALU.mult)
            dve.wait_ge(sem("kv_turned"), 4)
            TTO(vb[:, 4:8, :], four(ps[:, 7, :]), bc(beta[:, 1, :], P), ALU.mult).then_inc(sem("kv_scaled"), 1)
            def level(lv):
                if lv >= 2:
                    dve.wait_ge(sem("inv_P"), 2 * (lv - 1))
                mask = const[:, C_LVL + lv * P:C_LVL + (lv + 1) * P]
                for t in range(TT):
                    hs = slice(t * DH, (t + 1) * DH)
                    TTO(LT[:, lv % 2, hs, :], AT[:, hs, :], over_heads(mask, DH), ALU.mult).then_inc(sem("inv_L"), 1)

            am = const[:, C_AM:C_AM + 2 * P]

            def copy_qk(n):
                dve.wait_ge(sem("q_turned"), n + 1)
                if n < TT:
                    dve.tensor_copy(qT[:, :, n * P:(n + 1) * P], four(ps[:, 6 + n, :])).then_inc(sem("qT_copied"), 1)
                else:
                    dve.tensor_copy(kT[:, :], ps[:, 6, 0:SEQ]).then_inc(sem("qT_copied"), 1)

            def mask_scores(b):
                dve.wait_ge(sem("scores"), b + 1)
                bank = ps[:, 7 - b % 2, :]
                if b < 4:
                    ins = STT(s[:, 2 * b:2 * b + 2, 0:256], bank.rearrange("p (h k) -> p h k", h=2), AD ** -0.5,
                              over_heads(am, 2), ALU.mult, ALU.add)
                else:
                    ins = STT(s[:, 4 * (b - 4):4 * (b - 4) + 4, 256:384], four(bank), AD ** -0.5,
                              over_heads(am[:, P:2 * P], 4), ALU.mult, ALU.add)
                ins.then_inc(sem("scores_masked"), 1)

            def maximum():
                dve.wait_ge(sem("scores_masked"), 6)
                dve.tensor_reduce(mx[:, 1, :], s[:, :, 0:256], AX, ALU.max)
                link(dve.tensor_reduce(mx[:, 0, :], s[:, :, 256:384], AX, ALU.max))
                link(TTO(mx[:, :, :], mx[:, :, :], over_heads(sinks[:, :], 2), ALU.max))
                link(TS(nmx[:, :, :], mx[:, :, :], -1.0, None, ALU.mult))
                TTO(sdx[:, :, :], nmx[:, :, :], over_heads(sinks[:, :], 2), ALU.add).then_inc(sem("att_max"), 1)

            def divide(n):
                if n == 0:
                    dve.wait_ge(sem("att_exp"), 2 * AH + 1)
                    link(TTO(den[:, :, :], den[:, :, :], sdx[:, :, :], ALU.add))
                    link(dve.reciprocal(rden[:, :, :], den[:, :, :]))
                p_ = s[:, :, 256:384] if n == 0 else s[:, :, 0:256]
                TTO(p_, p_, bc(rden[:, n, :], 128 * (n + 1)), ALU.mult).then_inc(sem("p_ready"), 1)

            def copy_p(b):
                dve.wait_ge(sem("p_turned"), b + 1)
                dve.tensor_copy(pT[:, 4 * b:4 * b + 4, :], four(ps[:, 6, :])).then_inc(sem("pT_copied_dve"), 1)

            def attention(lv, half):
                at = (lv, half)
                if at == (0, 1):
                    copy_qk(0)
                    copy_qk(1)
                elif at == (1, 0):
                    copy_qk(2)
                elif at == (1, 1):
                    mask_scores(0)
                    mask_scores(1)
                elif at == (2, 0):
                    mask_scores(2)
                    mask_scores(3)
                elif at == (2, 1):
                    mask_scores(4)
                    mask_scores(5)
                    maximum()
                elif at == (4, 0):
                    divide(0)
                elif at == (4, 1):
                    divide(1)
                    copy_p(0)
                elif at == (5, 0):
                    copy_p(2)
                elif at == (5, 1):
                    copy_p(4)

            level(0)
            for lv in range(LEVELS):
                if lv == 1:
                    dve.wait_ge(sem("inv_X"), 2)
                if lv < LEVELS - 1:
                    level(lv + 1)
                attention(lv, 0)
                for t in range(TT):
                    hs = slice(t * DH, (t + 1) * DH)
                    if lv == 0:
                        dve.wait_ge(sem("inv_L"), t + 1)
                        TTO(XT[:, hs, :], over_heads(ident, DH), LT[:, 0, hs, :], ALU.subtract)
                        dve.wait_ge(sem("inv_P"), t + 1)
                        TTO(X[:, hs, :], over_heads(ident, DH), four(ps[:, t, :]), ALU.subtract).then_inc(sem("inv_X"), 1)
                    else:
                        dve.wait_ge(sem("inv_PX"), 2 * (lv - 1) + t + 1)
                        last = TTO(XT[:, hs, :], XT[:, hs, :], four(ps[:, 4 + t, :]), ALU.subtract)
                        if lv < LEVELS - 1:
                            last = TTO(X[:, hs, :], X[:, hs, :], four(ps[:, 2 + t, :]), ALU.subtract)
                        last.then_inc(sem("inv_X"), 1)
                attention(lv, 1)
            dve.wait_ge(sem("dn_u"), 1)
            dve.tensor_copy(u[:, 0:4, :], four(ps[:, 0, :])).then_inc(sem("dn_u_copied"), 1)
            dve.wait_ge(sem("dn_u"), 2)
            link(dve.tensor_copy(u[:, 4:8, :], four(ps[:, 1, :])))
            dve.wait_ge(sem("dn_o0"), 1)
            dve.tensor_copy(o[:, 0:4, :], four(ps[:, 3, :]))
            dve.wait_ge(sem("dn_wS"), 1)
            TTO(vnew[:, :, :], u[:, 4:8, :], four(ps[:, 5, :]), ALU.subtract).then_inc(sem("dn_vnew"), 1)
            dve.wait_ge(sem("dn_qS"), 1)
            link(TTO(o[:, 4:8, :], four(ps[:, 6, :]), bc(egc1[:, :], P), ALU.mult))
            dve.wait_ge(sem("dn_o1"), 1)
            link(TTO(o[:, 4:8, :], o[:, 4:8, :], four(ps[:, 7, :]), ALU.add))
            link(TTO(osq[:, :, :], o[:, :, :], o[:, :, :], ALU.mult))
            dve.tensor_reduce(oss[:, :], osq[:, :, :], AX, ALU.add).then_inc(sem("dn_oss"), 1)
            dve.wait_ge(sem("dn_orn"), 1)
            link(TTO(o[:, :, :], o[:, :, :], bc(orn[:, :], P), ALU.mult))
            link(TTO(o[:, :, :], o[:, :, :], over_heads(dn_nw[:, :], TT * DH), ALU.mult))
            dve.wait_ge(sem("gate_silu"), TT)
            TTO(o[:, :, :], o[:, :, :], gate[:, :, :].rearrange("p t (h d) -> p (t h) d", d=DD), ALU.mult).then_inc(sem("o_ready"), 1)
            dve.wait_ge(sem("o_turned"), 1)
            dve.tensor_copy(mixT[:, 4:8, 0:P], four(ps[:, 0, :])).then_inc(sem("mix_dn"), 1)
            layer_norm(0, [(sem("out_tile"), 1), (sem("out_proj"), 2)])
            if limit < 2:
                return
            for n in range(N0, N0 + 2):
                dense_low(n, n % RAW_D, n % CUT)
            turn_low(1)
            dense_low(N0 + 2, 2, 2)

            def ffn_h(b, step):
                dve.wait_ge(sem("ffn_silu"), step + 1)
                dve.wait_ge(d_piece_used, 3 * step + (CUT + N0 + 2))
                dve.wait_ge(sem("ffn_h"), step + FIRST)
                TTO(hT[:, :], sg[:, b, :], ps[:, 2 * b + 1, :], ALU.mult).then_inc(sem("ffn_h_full"), 1)
                dve.wait_ge(sem("ffn_h_full"), step + 1)
                dve.tensor_copy(hT_hi[:, :, :], hT[:, :].rearrange("p (k t) -> p k t", k=2)).then_inc(sem("ffn_h_hi"), 1)
                dve.wait_ge(sem("ffn_h_hi"), step + 1)
                TTO(hT_lo[:, :, :], hT[:, :].rearrange("p (k t) -> p k t", k=2), hT_hi[:, :, :].bitcast(F32), ALU.subtract
                    ).then_inc(sem("ffn_h"), 1)

            dve.sem_inc(sem("ffn_h"), FIRST)
            with dve.Fori(0, FSTEPS // 2) as i:
                dense_low(6 * i + (N0 + 3), 3, 0)
                ffn_h(0, 2 * i)
                dense_low(6 * i + (N0 + 4), 4, 1)
                dense_low(6 * i + (N0 + 5), 5, 2)
                dense_low(6 * i + (N0 + 6), 0, 0)
                ffn_h(1, 2 * i + 1)
                dense_low(6 * i + (N0 + 7), 1, 1)
                dense_low(6 * i + (N0 + 8), 2, 2)
            ffn_h(0, FSTEPS - 1)
            if limit >= 3:
                for n in range(N1, N1 + 2):
                    dense_low(n, n % RAW_D, n % CUT)
            layer_norm(1, [(sem("ffn_tile"), 1), (d_piece_used, CUT + N1)])
            if limit < 3:
                return
            turn_low(2)
            n = N1 + 2
            dense_low(n, n % RAW_D, n % CUT)

            for m, (kind, q) in enumerate(PROJ):
                if m == DT_AT + 1:
                    dve.wait_ge(sem("dt_proj"), 1)
                    link(TTO(sz[:, :, :], ps[:, 7, 0:TT * SH].rearrange("p (t h) -> p t h", t=TT), over_heads(ssm_dtb[:, :], TT), ALU.add))
                    STT(saz[:, :, :], sz[:, :, :], -1.0, sz[:, :, :], ALU.mult, ALU.max).then_inc(sem("ssm_z"), 1)
                n = N1 + m + CUT
                if n < N2:
                    dense_low(n, n % RAW_D, n % CUT)
                if kind == 0:
                    dve.wait_ge(d_piece_used, CUT + N1 + m + 1)
                    conv((2 * q, 2 * q + 1), lambda j: ps[:, (j // 2) % 4, (j % 2) * SEQ:(j % 2 + 1) * SEQ],
                         lambda j: xbcT[:, j, :], ssm_tap).then_inc(sem("ssm_conv"), 1)
            dve.wait_ge(sem("ssm_sp"), 2)
            link(STT(sdt[:, :, :], sz[:, :, :], 0.0, se2[:, :, :], ALU.max, ALU.add))
            STT(dA[:, :, :], sdt[:, :, :], -1.0, over_heads(sea[:, :], TT), ALU.mult, ALU.mult).then_inc(sem("dA_made"), 1)
            for t in range(TT):
                for q in range(4):
                    dve.wait_ge(sem("xs_turned"), 4 * t + q + 1)
                    TTO(xdt[:, t, 512 * q:512 * q + 512].rearrange("p (h d) -> p h d", d=SD),
                        ps[:, 4 * t + q, :].rearrange("p (h d) -> p h d", d=SD), bc(sdt[:, t, 8 * q:8 * q + 8], SD), ALU.mult
                        ).then_inc(sem("xdt_made"), 1)
            dve.wait_ge(sem("acs_made"), 1)
            link(TS(nacs[:, :, :], ps[:, 1, 0:TT * SH].rearrange("p (t h) -> p t h", t=TT), -1.0, None, ALU.mult))
            TTO(sdd[:, :], ps[:, 1, 64:96], nacs[:, 0, :], ALU.add).then_inc(sem("ssm_cols"), 1)
            dve.wait_ge(sem("ssm_dec"), 1)
            TTO(xdec[:, :].rearrange("p (h d) -> p h d", d=SD), xdt[:, 0, :].rearrange("p (h d) -> p h d", d=SD),
                bc(sdec[:, :], SD), ALU.mult).then_inc(sem("xdec_made"), 1)

            def y_diag(i):
                t, g = i // SG, i % SG
                dve.wait_ge(sem("y_made"), i + 1)
                for c in range(4):
                    j = 4 * g + c
                    yj = xbcT[:, j, t * P:(t + 1) * P]
                    last = STT(yj, yj, dcol[:, j:j + 1], ps[:, 4 + i % 2, c * P:(c + 1) * P], ALU.mult, ALU.add)
                last.then_inc(sem("y_added"), 1)

            for i in range(TT * SG):
                dve.wait_ge(sem("seg_made"), 8 * (i + 1))
                dve.wait_ge(sem("cb_copied"), TT)
                if i >= 2:
                    dve.wait_ge(sem("y_made"), i - 1)
                TTO(MT[:, i % 2], seg[:, i % 2], over_heads(cb[:, i, :], 8), ALU.mult).then_inc(sem("MT_made"), 1)
                if i:
                    y_diag(i - 1)
            y_diag(TT * SG - 1)
            dve.wait_ge(sem("y_added"), TT * SG)
            for q in range(4):
                dve.wait_ge(sem("er_made"), q + 1)
                link(TTO(yo[:, q % 2, :], er[:, q % 2, :], ps[:, 2 * (q % 2), :], ALU.mult))
                yq = xbcT[:, 4 * q:4 * q + 4, P:2 * P]
                TTO(yq, yq, four(yo[:, q % 2, :]), ALU.add).then_inc(sem("yoff_added"), 1)
            dve.wait_ge(sem("yoff_added"), 4)
            dve.wait_ge(sem("z_silu"), NX // 2)
            for g in range(SG):
                yg = xbcT[:, 4 * g:4 * g + 4, :]
                link(TTO(yg, yg, zT[:, 4 * g:4 * g + 4, :], ALU.mult))
                if g >= 2:
                    dve.wait_ge(sem("y_ss"), g - 1)
                TTO(ysq[:, g % 2, :].rearrange("p (k t) -> p k t", k=4), yg, yg, ALU.mult).then_inc(sem("ysq_made"), 1)
            dense_low(N2, N2 % RAW_D, N2 % CUT)
            for g in range(SG):
                dve.wait_ge(sem("y_rn"), g + 1)
                for j in range(4 * g, 4 * g + 4):
                    last = STT(xbcT[:, j, :], xbcT[:, j, :], ssm_nw(j), yrn[:, g, :], ALU.mult, ALU.mult)
                last.then_inc(sem("y_full"), 1)
            for g in range(SG):
                ks = slice(4 * g, 4 * g + 4)
                dve.wait_ge(sem("y_hi_made"), g + 1)
                TTO(y_lo(ks), xbcT[:, ks, :], y_hi[:, ks, :].bitcast(F32), ALU.subtract).then_inc(sem("y_ready"), 1)
                if g < CUT - 1:
                    n = N2 + g + 1
                    dense_low(n, n % RAW_D, n % CUT)
            for n in range(N2 + CUT, NPRE):
                dense_low(n, n % RAW_D, n % CUT)
            layer_norm(2, [(sem("out_tile"), 2), (d_piece_used, CUT + NPRE)])
            def cut_low(n, it):
                dve.wait_ge(sem("hi_made"), PPE * it + (n + 1))
                TTO(w_lo[:, n % CUT, :], raw[:, n % RAW, :], w_hi[:, n % CUT, :].bitcast(F32), ALU.subtract).then_inc(lo_made, 1)

            if limit >= 5:
                cut_low(0, 0)
            turn_copies(3)
            if limit < 5:
                return

            def select_rows(e, it, places):
                dve.wait_ge(sem("xg_made"), 2 * it + FIRST)
                for t in range(TT):
                    ins = TS(sel_rows[:, t, :], iota, places[:, t, bass.ds(e, 1)], None, ALU.is_equal)
                ins.then_inc(sem("sel_rows_made"), 1)

            def select_gates(e, places):
                for t in range(TT):
                    ins = TS(sel_gate[:, t, :], iota, places[:, t, bass.ds(e, 1)], comb[:, t, bass.ds(e, 1)], ALU.is_equal, ALU.mult)
                ins.then_inc(sem("sel_gate_made"), 1)

            cut_low(1, 0)
            dve.wait_ge(sem("logits"), TT)
            link(TTO(lg[:, :, :], ps[:, 4, 0:TT * E].rearrange("p (t e) -> p t e", t=TT), over_heads(brt[:, :], TT), ALU.add))
            for t in range(TT):
                link(dve.max(top8[:, t, :], lg[:, t, :]))
                link(dve.max_index(idx8[:, t, :].bitcast(U32), top8[:, t, :], lg[:, t, :]))
            TTO(dm[:, :, :], top8[:, :, 1:2], top8[:, :, 0:1], ALU.subtract).then_inc(sem("rt_dm"), 1)
            link(dve.tensor_copy(idxf[:, :, :], idx8[:, :, 0:2].bitcast(U32)))
            for t in range(TT):
                TS(oh1[:, t, :], iota8, idxf[:, t, 0:1], None, ALU.is_equal)
                link(TS(oh2[:, t, :], iota8, idxf[:, t, 1:2], None, ALU.is_equal))
            TTO(sel[:, :, :], oh1[:, :, :], oh2[:, :, :], ALU.add).then_inc(sem("sel_made"), 1)
            dve.wait_ge(sem("ranks"), 1)
            ps_rank = ps[:, 4, 32:32 + TT * E].rearrange("p (t e) -> p t e", t=TT)
            link(STT(rank[:, :, :], ps_rank, 1.0, sel[:, :, :], ALU.add, ALU.mult))
            link(TS(rank[:, :, :], rank[:, :, :], -1.0, None, ALU.add))
            select_rows(0, 0, rank)
            dve.wait_ge(sem("rt_e"), 1)
            link(TS(g2[:, :, :], g1[:, :, :], 1.0, None, ALU.add))
            link(dve.reciprocal(g2[:, :, :], g2[:, :, :]))
            link(TTO(g1[:, :, :], g1[:, :, :], g2[:, :, :], ALU.mult))
            for t in range(TT):
                link(TS(comb[:, t, :], oh1[:, t, :], g2[:, t, :], None, ALU.mult))
                link(STT(comb[:, t, :], oh2[:, t, :], g1[:, t, :], comb[:, t, :], ALU.mult, ALU.add))
            select_gates(0, rank)
            cut_low(2, 0)
            link(TS(rank2[:, :, :], rank[:, :, :], -float(P), None, ALU.add))
            link(dve.tensor_reduce(cnt[:, :], ps[:, 4, 64:64 + E], AX, ALU.max))
            link(TS(cnt[:, :], cnt[:, :], -float(P), 0.0, ALU.add, ALU.max))
            dve.tensor_copy(over[:, :].bitcast(I32), cnt[:, :]).then_inc(sem("overflow_known"), 1)
            for t in range(TT):
                last = TS(yacc[:, t, :], x_tok[:, t, :], ALPHA, None, ALU.mult)
            last.then_inc(sem("yacc_open"), 1)

            def gathered_low(it):
                for q in range(2):
                    dve.wait_ge(sem("xg_hi_made"), 2 * it + (q + 1))
                    hs = slice(4 * q, 4 * q + 4)
                    TTO(xg_lo[:, hs, :], four(ps[:, 2 + q, :]), xg_hi[:, hs, :].bitcast(F32), ALU.subtract).then_inc(sem("xg_lo_made"), 1)

            def expert_dve(it, following):
                def mult(j):
                    dve.wait_ge(sem("e_silu"), ESTEPS * it + (j + 1))
                    TTO(eh[:, j % 2, :], esg[:, j % 2, :], ps[:, 2 * (j % 2) + 1, :], ALU.mult).then_inc(sem("e_h"), 1)

                def turned(j):
                    dve.wait_ge(sem("ehT_hi_made"), ESTEPS * it + (j + 1))
                    TTO(ehT_lo[:, j % 2], four(ps[:, 4, :]), ehT_hi[:, j % 2].bitcast(F32), ALU.subtract).then_inc(sem("ehT_made"), 1)

                for n in range(CUT, PPE):
                    cut_low(n, it)
                    if n == G_AT:
                        dve.wait_ge(sem("G_turned"), it + 1)
                        dve.wait_ge(sem("e_scattered"), 4 * it + FIRST)
                        dve.tensor_copy(G[:, :, :], ps[:, 7, 0:TT * P].rearrange("p (t c) -> p t c", t=TT)).then_inc(sem("G_copied"), 1)
                    for j in range(ESTEPS):
                        if n == last_piece(j, 1) + 2:
                            mult(j)
                        if j and n == last_piece(j, 0) + 2:
                            turned(j - 1)
                    if n == last_piece(ESTEPS - 1, 0) and following is not None:
                        select_rows(following, following, rank)
                        select_gates(following, rank)
                    if n == PPE - 2 and following is not None:
                        gathered_low(following)
                turned(ESTEPS - 1)
                if following is not None:
                    cut_low(0, following)
                    cut_low(1, following)
                dve.wait_ge(piece_used, PPE * it + (CUT + PPE))
                dve.tensor_copy(oe[:, 0:512], ps[:, 5, :]).then_inc(sem("oe_copied_dve"), 1)
                dve.wait_ge(sem("e_added"), 4 * it + FIRST)
                for q in range(2 * TT):
                    dve.wait_ge(sem("e_scattered"), 4 * it + (q + 1) + FIRST)
                    yq = yacc[:, q // 2, 512 * (q % 2):512 * (q % 2) + 512]
                    TTO(yq, yq, ps[:, 7 if q % 2 == 0 else 4, :], ALU.add).then_inc(sem("e_added"), 1)
                if following is not None:
                    cut_low(2, following)

            dve.wait_ge(sem("yacc_open"), 1)
            dve.sem_inc(sem("e_h"), FIRST)
            dve.sem_inc(sem("e_added"), FIRST)
            dve.sem_inc(sem("ehT_made"), FIRST)
            gathered_low(0)
            with dve.Fori(0, E - 1) as e:
                expert_dve(e, e + 1)
            expert_dve(E - 1, None)
            more = dve.value_load(over[0:1, 0:1].bitcast(I32), min_val=0, max_val=SEQ)
            dve.wait_ge(sem("e_added"), 4 * E + FIRST)
            with dve.If(more > 0):
                with dve.Fori(0, E) as e:
                    select_rows(e, e + E, rank2)
                    select_gates(e, rank2)
                    for n in range(CUT):
                        cut_low(n, e + E)
                    gathered_low(e + E)
                    expert_dve(e + E, None)
                dve.wait_ge(sem("e_added"), 8 * E + FIRST)
            layer_norm(3, [(sem("e_added"), 4 * E + FIRST)] * TT, x=yacc, add=False)

        @block.tensor
        def _(pe):
            mm = pe.matmul

            def turn_tile(n, t):
                if n:
                    pe.wait_ge(sem("ln_done"), TT * (n - 1) + t + 1)
                for q in range(2):
                    for k in range(4):
                        c = 4 * q + k
                        last = pe.transpose(ps[:, 2 * t + q, k * P:(k + 1) * P], x_tok[:, t, c * P:(c + 1) * P], ident)
                    last.then_inc(sem("x_turned"), 1)

            def turn(n):
                for t in range(TT):
                    turn_tile(n, t)

            def token_major(out_ap, w, t):
                for k in range(KD):
                    last = mm(out_ap, xT[:, k, t * P:(t + 1) * P], w[:, k, :], start=k == 0, stop=k == KD - 1)
                return last

            def output_part(i, t):
                slot_ = out_units[i][1]
                pe.wait_ge(loaded[slot_], 32)
                w = slot(slot_)[:, :].rearrange("p (k n) -> p k n", n=D)
                for kk in range(4):
                    k = 4 * i + kk
                    for n in range(2):
                        last = mm(ps[:, 4 + 2 * t + n, :], mixT[:, k, t * P:(t + 1) * P], w[:, kk, 512 * n:512 * n + 512],
                                  start=k == 0, stop=k == KD - 1)
                return last

            def three_wx(out_ap, c, k, cs, first, last_):
                whi, wlo = [w[:, c, :].rearrange("p (k n) -> p k n", k=KD)[:, k, cs] for w in (w_hi, w_lo)]
                mm(out_ap, whi, xT_hi[:, k, :], start=first, stop=False)
                mm(out_ap, whi, xT_lo[:, k, :], start=False, stop=False)
                return mm(out_ap, wlo, xT_hi[:, k, :], start=False, stop=last_)

            def columns(n, c, bank):
                pe.wait_ge(d_lo_made, n + (RAW_D + 1))
                for j in range(2):
                    for k in range(KD):
                        last = three_wx(ps[:, bank, j * SEQ:(j + 1) * SEQ], c, k, slice(j * P, (j + 1) * P), k == 0, k == KD - 1)
                last.then_inc(d_piece_used, 1)

            def halves(n, width, place):
                for half in range(2):
                    c = (n + half) % CUT
                    pe.wait_ge(d_lo_made, RAW_D + n + half + 1)
                    whi, wlo = [w[:, c, 0:4 * width].rearrange("p (k n) -> p k n", k=4) for w in (w_hi, w_lo)]
                    for t in range(TT):
                        ts_ = slice(t * P, (t + 1) * P)
                        for kk in range(4):
                            k = 4 * half + kk
                            mm(place(t), xT_hi[:, k, ts_], whi[:, kk, :], start=k == 0, stop=False)
                            mm(place(t), xT_hi[:, k, ts_], wlo[:, kk, :], start=False, stop=False)
                            last = mm(place(t), xT_lo[:, k, ts_], whi[:, kk, :], start=False, stop=k == KD - 1)
                    last.then_inc(d_piece_used, 1)

            pe.wait_ge(sem("x_loaded"), 32)
            turn(0)
            pe.sem_inc(d_piece_used, CUT)
            pe.wait_ge(sem("xT_lo_made"), 4)
            columns(0, 0, 0)
            columns(1, 1, 1)
            pe.wait_ge(sem("taps_loaded"), 16 * 4)
            pe.transpose(ps[:, 7, 0:CONV * NXBC], prow_a[0:CONV * NXBC, :], ident[0:CONV * NXBC, 0:CONV * NXBC])
            pe.transpose(ps[:, 7, P:P + 88], prow_b[0:88, :], ident[0:88, 0:88]).then_inc(sem("params_turned"), 1)
            halves(N_GATE, 512, lambda t: ps[:, 4 + t, :])
            columns(N_DN[2], N_DN[2] % CUT, 2)
            columns(N_DN[3], N_DN[3] % CUT, 3)
            pe.wait_ge(sem("params_copied"), 1)
            halves(N_Q, 512, lambda t: ps[:, 6 + t, :])
            for q in (4, 5):
                pe.wait_ge(sem("dn_conv"), q - 3)
                columns(N_DN[q], N_DN[q] % CUT, q % 4)
            pe.wait_ge(sem("gate_silu"), TT)
            halves(N_KV, 256, lambda t: ps[:, 4 + t, 0:256])
            pe.wait_ge(sem("xT_joined"), 1)
            pe.wait_ge(sem("params_loaded"), 16 * 13)
            for t in range(TT):
                token_major(ps[:, 4 + t, 256:256 + 2 * DH], w_ba, t).then_inc(sem("kv_proj"), 1)
            pe.wait_ge(sem("pool_set"), 3)
            pe.wait_ge(sem("dn_conv"), NDN // 2)
            for b in range(4):
                pe.wait_ge(sem("dn_sq"), b + 1)
                mm(ps[:, b, :], ones[:, :], sq[:, 512 * b:512 * b + 512], start=True, stop=True).then_inc(sem("dn_ss"), 1)
            def kk_products(t):
                ts_ = slice(t * P, (t + 1) * P)
                for h in range(DH):
                    mm(ps[:, 4 + t, h * P:(h + 1) * P], dnT[:, 4 + h, ts_], dnT[:, 4 + h, ts_], start=True, stop=True)
                    last = mm(ps[:, 6 + t, h * P:(h + 1) * P], dnT[:, 4 + h, ts_], dnT[:, h, ts_], start=True, stop=True)
                last.then_inc(sem("dn_kk"), 1)

            pe.wait_ge(sem("dn_qk"), 2)
            pe.wait_ge(sem("dn_z"), 1)
            kk_products(1)
            pe.wait_ge(sem("dn_gb"), 1)
            g8 = gdn[:, :, :].rearrange("p t h -> p (t h)")
            mm(ps[:, 4, 0:8], tri, g8, start=True, stop=True)
            mm(ps[:, 4, 8:12], ones[:, :], gdn[:, 0, :], start=True, stop=True).then_inc(sem("dn_gc"), 1)
            pe.wait_ge(sem("dn_rn"), 4)
            for t in range(TT):
                mm(ps[:, t, :], identb[:, :], over_heads(maskb[:, :], 4), start=True, stop=False)
                for h in range(DH):
                    last = mm(ps[:, t, h * P:(h + 1) * P], gdn[:, t, h:h + 1].to_broadcast([P, P]), tri, start=False, stop=h == DH - 1)
                last.then_inc(sem("dn_gcrow"), 1)
                for h in range(DH):
                    mm(ps[:, 2 + t, h * P:(h + 1) * P], beta[:, t, h:h + 1].to_broadcast([P, P]), ident, start=True, stop=True)
            pe.wait_ge(sem("dn_cols"), 1)
            kk_products(0)
            pe.wait_ge(sem("dn_A"), TT)
            for t in range(TT):
                for w_ in range(2):
                    for h in range(DH):
                        last = pe.transpose(ps[:, 4 + 2 * t + w_, h * P:(h + 1) * P], dnT[:, 4 + 4 * w_ + h, t * P:(t + 1) * P], ident)
                    last.then_inc(sem("kv_turned"), 1)

            def turn_qk(n):
                if n == 0:
                    pe.wait_ge(sem("rope_done"), 1)
                    pe.wait_ge(sem("kv_scaled"), 1)
                if n < TT:
                    for c in range(4):
                        last = pe.transpose(ps[:, 6 + n, c * P:(c + 1) * P], qkv[:, n, c * P:(c + 1) * P], ident)
                else:
                    pe.wait_ge(sem("qT_copied"), 1)
                    for t in range(TT):
                        last = pe.transpose(ps[:, 6, t * P:(t + 1) * P], qkv[:, t, 512:640], ident)
                last.then_inc(sem("q_turned"), 1)

            def score_products(b):
                if b < 2:
                    pe.wait_ge(sem("qT_copied"), 3)
                else:
                    pe.wait_ge(sem("scores_masked"), b - 1)
                bank = ps[:, 7 - b % 2, :]
                if b < 4:
                    for h in (2 * b, 2 * b + 1):
                        r = slice(64 * (h // 4), 64 * (h // 4) + 64)
                        last = mm(bank[:, (h % 2) * 256:(h % 2) * 256 + 256], qT[r, h % 4, P:2 * P], kT[r, :], start=True, stop=True)
                else:
                    r = slice(64 * (b - 4), 64 * (b - 4) + 64)
                    for h in range(4):
                        last = mm(bank[:, h * P:(h + 1) * P], qT[r, h, 0:P], kT[r, 0:P], start=True, stop=True)
                last.then_inc(sem("scores"), 1)

            def turn_p(b):
                pe.wait_ge(sem("p_ready"), 1 if b < 2 else 2)
                if b < 2:
                    pe.wait_ge(sem("scores_masked"), 6)
                elif b % 2 == 0:
                    pe.wait_ge(sem("pT_copied_dve"), b // 2)
                else:
                    pe.wait_ge(sem("pT_copied_act"), b // 2)
                for i in range(4 * b, 4 * b + 4):
                    src = s[:, i, 256:384] if i < AH else s[:, (i - AH) // 2, ((i - AH) % 2) * P:((i - AH) % 2 + 1) * P]
                    last = pe.transpose(ps[:, 6 + b % 2, (i % 4) * P:(i % 4 + 1) * P], src, ident)
                last.then_inc(sem("p_turned"), 1)

            def weigh_v(b):
                pe.wait_ge(sem("pT_copied_dve"), 3)
                pe.wait_ge(sem("pT_copied_act"), 3)
                for h in range(4 * b, 4 * b + 4):
                    c, r = h // 2, 64 * (h % 2)
                    vcol = 640 + AD * (h // 4)
                    o_ = [ps[r:r + 64, 6 + b, (c % 2) * SEQ + t * P:(c % 2) * SEQ + (t + 1) * P] for t in range(TT)]
                    mm(o_[0], qkv[:, 0, vcol:vcol + AD], pT[:, h, :], start=True, stop=True)
                    mm(o_[1], qkv[:, 0, vcol:vcol + AD], pT[:, AH + 2 * h, :], start=True, stop=False)
                    last = mm(o_[1], qkv[:, 1, vcol:vcol + AD], pT[:, AH + 2 * h + 1, :], start=False, stop=True)
                last.then_inc(sem("att_out"), 1)

            def attention(lv, half):
                at = (lv, half)
                if at == (0, 1):
                    turn_qk(0)
                    turn_qk(1)
                elif at == (1, 0):
                    turn_qk(2)
                elif at == (1, 1):
                    score_products(0)
                    score_products(1)
                elif at == (2, 0):
                    score_products(2)
                    score_products(3)
                elif at == (2, 1):
                    score_products(4)
                    score_products(5)
                elif at == (4, 1):
                    turn_p(0)
                    turn_p(1)
                elif at == (5, 0):
                    turn_p(2)
                    turn_p(3)
                elif at == (5, 1):
                    turn_p(4)
                    turn_p(5)
                elif at == (6, 0):
                    weigh_v(0)
                elif at == (6, 1):
                    weigh_v(1)

            for lv in range(LEVELS):
                for t in range(TT):
                    pe.wait_ge(sem("inv_L"), 2 * lv + t + 1)
                    if lv:
                        pe.wait_ge(sem("inv_X"), 2 * (lv - 1) + t + 1)
                    for h in range(DH):
                        i = t * DH + h
                        last = mm(ps[:, t, h * P:(h + 1) * P], LT[:, lv % 2, i, :], X[:, i, :] if lv else ident, start=True, stop=True)
                    last.then_inc(sem("inv_P"), 1)
                attention(lv, 0)
                if lv == 1:
                    pe.wait_ge(sem("kv_scaled"), 1)
                for t in range(TT if lv else 0):
                    pe.wait_ge(sem("inv_P_copied"), 2 * (lv - 1) + t + 1)
                    for h in range(DH):
                        i = t * DH + h
                        if lv < LEVELS - 1:
                            mm(ps[:, 2 + t, h * P:(h + 1) * P], XT[:, i, :], Pm[:, i, :], start=True, stop=True)
                        last = mm(ps[:, 4 + t, h * P:(h + 1) * P], Pm[:, i, :], XT[:, i, :], start=True, stop=True)
                    last.then_inc(sem("inv_PX"), 1)
                attention(lv, 1)
            for t in range(TT):
                pe.wait_ge(sem("inv_X"), 2 * (LEVELS - 1) + t + 1)
                for h in range(DH):
                    i = t * DH + h
                    last = mm(ps[:, t, h * P:(h + 1) * P], XT[:, i, :], vb[:, i, :], start=True, stop=True)
                last.then_inc(sem("dn_u"), 1)
            for h in range(DH):
                last = mm(ps[:, 2, h * P:(h + 1) * P], kbe[:, h, :], XT[:, 4 + h, :], start=True, stop=True)
            last.then_inc(sem("dn_w"), 1)
            pe.wait_ge(sem("dn_u_copied"), 1)
            for h in range(DH):
                last = mm(ps[:, 4, h * P:(h + 1) * P], kdec[:, h, :], u[:, h, :], start=True, stop=True)
            last.then_inc(sem("dn_S"), 1)
            for h in range(DH):
                last = mm(ps[:, 3, h * P:(h + 1) * P], attnT[:, h, :], u[:, h, :], start=True, stop=True)
            last.then_inc(sem("dn_o0"), 1)
            pe.wait_ge(sem("dn_w_copied"), 1)
            pe.wait_ge(sem("dn_S_copied"), 1)
            for h in range(DH):
                last = mm(ps[:, 5, h * P:(h + 1) * P], wT[:, h, :], S1[:, h, :], start=True, stop=True)
            last.then_inc(sem("dn_wS"), 1)
            pe.wait_ge(sem("mix_att"), 2)
            for h in range(DH):
                last = mm(ps[:, 6, h * P:(h + 1) * P], dnT[:, h, P:2 * P], S1[:, h, :], start=True, stop=True)
            last.then_inc(sem("dn_qS"), 1)
            pe.wait_ge(sem("dn_vnew"), 1)
            for h in range(DH):
                last = mm(ps[:, 7, h * P:(h + 1) * P], attnT[:, 4 + h, :], vnew[:, h, :], start=True, stop=True)
            last.then_inc(sem("dn_o1"), 1)
            pe.wait_ge(sem("dn_oss"), 1)
            output_part(0, 0)
            pe.wait_ge(sem("o_ready"), 1)
            for t in range(TT):
                for h in range(DH):
                    last = pe.transpose(ps[:, t, h * P:(h + 1) * P], o[:, t * DH + h, :], ident)
                last.then_inc(sem("o_turned"), 1)

            output_part(0, 1).then_inc(sem("out_proj"), 1)
            pe.wait_ge(sem("mix_dn"), 2)
            output_part(1, 0).then_inc(sem("out_tile"), 1)
            output_part(1, 1).then_inc(sem("out_proj"), 1)
            turn(1)
            if limit < 2:
                return

            def open_banks():
                for b in range(4, 8):
                    mm(ps[:, b, :], identb[:, :], zerob[:, :], start=True, stop=False)

            def ffn_down(n, c, step, close):
                pe.wait_ge(d_lo_made, n + (RAW_D + 1))
                pe.wait_ge(sem("ffn_h"), step + (1 + FIRST))
                whi, wlo = [w[:, c, :].rearrange("p (k n) -> p k n", k=2) for w in (w_hi, w_lo)]
                for t in range(TT):
                    ts_ = slice(t * P, (t + 1) * P)
                    for h in range(2):
                        cs = slice(512 * h, 512 * h + 512)
                        for k in range(2):
                            out_ap = ps[:, 4 + 2 * t + h, :]
                            mm(out_ap, hT_hi[:, k, ts_], whi[:, k, cs], start=False, stop=False)
                            mm(out_ap, hT_hi[:, k, ts_], wlo[:, k, cs], start=False, stop=False)
                            last = mm(out_ap, hT_lo[:, k, ts_], whi[:, k, cs], start=False, stop=close and k == 1)
                    if close and t == 0:
                        last.then_inc(sem("ffn_tile"), 1)
                last.then_inc(d_piece_used, 1)

            open_banks()
            pe.wait_ge(sem("xT_lo_made"), 8)
            columns(N0, 0, 0)
            columns(N0 + 1, 1, 1)
            with pe.Fori(0, FSTEPS // 2) as i:
                columns(6 * i + (N0 + 2), 2, 2)
                columns(6 * i + (N0 + 3), 0, 3)
                ffn_down(6 * i + (N0 + 4), 1, 2 * i, False)
                columns(6 * i + (N0 + 5), 2, 0)
                columns(6 * i + (N0 + 6), 0, 1)
                ffn_down(6 * i + (N0 + 7), 1, 2 * i + 1, False)
            ffn_down(N1 - 1, (N1 - 1) % CUT, FSTEPS - 1, True)
            turn(2)
            if limit < 3:
                return

            pe.wait_ge(sem("xT_lo_made"), 12)
            for m, (kind, q) in enumerate(PROJ):
                n = N1 + m
                if kind == 0 and q >= 4:
                    pe.wait_ge(sem("ssm_conv"), q - 3)
                if m == DT_AT:
                    pe.wait_ge(sem("xT_joined"), 2)
                    for t in range(TT):
                        last = token_major(ps[:, 7, t * SH:(t + 1) * SH], w_dt, t)
                    last.then_inc(sem("dt_proj"), 1)
                if kind == 1 and q == 3:
                    pe.wait_ge(sem("ssm_z"), 1)
                if kind == 1 and q >= 4:
                    pe.wait_ge(sem("z_silu"), q - 3)
                columns(n, n % CUT, (0 if kind == 0 else 4) + q % 4)
            pe.wait_ge(sem("ssm_silu"), NXBC)
            for t in range(TT):
                for q in range(4):
                    if t == 1 and q == 0:
                        pe.wait_ge(sem("z_silu"), NX // 2)
                    for c in range(4):
                        j = 4 * q + c
                        last = pe.transpose(ps[:, 4 * t + q, c * P:(c + 1) * P], xbcT[:, j, t * P:(t + 1) * P], ident)
                    last.then_inc(sem("xs_turned"), 1)
            pe.wait_ge(sem("xdt_made"), 4)
            pe.wait_ge(sem("dA_made"), 1)
            mm(ps[:, 1, 0:64], tri, dA[:, :, :].rearrange("p t h -> p (t h)"), start=True, stop=True)
            mm(ps[:, 1, 64:96], ones[:, :], dA[:, 0, :], start=True, stop=True).then_inc(sem("acs_made"), 1)
            for g in range(SG):
                last = pe.transpose(ps[:, 0, g * P:(g + 1) * P], xbcT[:, NX + g, 0:P], ident)
            last.then_inc(sem("B_turned"), 1)
            for t in range(TT):
                for g in range(SG):
                    last = mm(ps[:, 2 + t, g * P:(g + 1) * P], xbcT[:, NX + g, t * P:(t + 1) * P],
                              xbcT[:, NX + SG + g, t * P:(t + 1) * P], start=True, stop=True)
                last.then_inc(sem("cb_made"), 1)
            pe.wait_ge(sem("B_copied"), 1)
            pe.wait_ge(sem("xdec_made"), 1)
            pe.wait_ge(sem("xdt_made"), 8)
            for g in range(SG):
                mm(ps[:, 4 + g, :], Btok[:, g * P:(g + 1) * P], xdec[:, 512 * g:512 * g + 512], start=True, stop=True
                   ).then_inc(sem("state_made"), 1)

            def acs_rows(i):
                t, g = i // SG, i % SG
                if i == 0:
                    pe.wait_ge(sem("ssm_cols"), 1)
                    pe.wait_ge(sem("B_copied"), 1)
                if i == 1:
                    pe.wait_ge(sem("cb_copied"), TT)
                if i >= 2:
                    pe.wait_ge(sem("seg_made"), 8 * (i - 1))
                for b in range(2):
                    bank = ps[:, 2 * (i % 2) + b, :]
                    mm(bank, identb[:, :], over_heads(maskb[:, :], 4), start=True, stop=False)
                    for r in range(4):
                        h = 8 * g + 4 * b + r
                        last = mm(bank[:, r * P:(r + 1) * P], dA[:, t, h:h + 1].to_broadcast([P, P]), tri, start=False, stop=r == 3)
                last.then_inc(sem("acs_rows"), 1)

            def y_products(i):
                t, g = i // SG, i % SG
                pe.wait_ge(sem("MT_made"), i + 1)
                if i == 0:
                    pe.wait_ge(sem("state_copied"), SG)
                if i >= 2:
                    pe.wait_ge(sem("y_added"), i - 1)
                for r in range(8):
                    h = 8 * g + r
                    last = mm(ps[64 * (r % 2):64 * (r % 2) + 64, 4 + i % 2, (r // 2) * P:(r // 2 + 1) * P],
                              xdt[:, t, SD * h:SD * (h + 1)], MT[:, i % 2, r, :], start=True, stop=True)
                last.then_inc(sem("y_made"), 1)

            acs_rows(0)
            for i in range(TT * SG):
                if i + 1 < TT * SG:
                    acs_rows(i + 1)
                y_products(i)
            pe.wait_ge(sem("seg_made"), 8 * TT * SG)
            for q in range(4):
                b = 2 * (q % 2)
                if q >= 2:
                    pe.wait_ge(sem("yoff_added"), q - 1)
                for c in range(4):
                    j = 4 * q + c
                    mm(ps[:, b, c * P:(c + 1) * P], state[:, j * P:(j + 1) * P], xbcT[:, NX + SG + q, P:2 * P], start=True, stop=True)
                    for r in range(2):
                        last = mm(ps[64 * r:64 * r + 64, b + 1, c * P:(c + 1) * P], dA[:, 1, 2 * j + r:2 * j + r + 1].to_broadcast([P, SD]),
                                  tri, start=True, stop=True)
                last.then_inc(sem("yoff_made"), 1)
            for g in range(SG):
                pe.wait_ge(sem("ysq_made"), g + 1)
                if g == 0:
                    pe.wait_ge(sem("y_added"), TT * SG)
                for c in range(4):
                    last = mm(ps[:, 4 + g, 0:SEQ], ones[:, :], ysq[:, g % 2, c * SEQ:(c + 1) * SEQ], start=c == 0, stop=c == 3)
                last.then_inc(sem("y_ss"), 1)

            pe.wait_ge(sem("y_rn"), SG)

            def y_out(i, t):
                n = N2 + i
                pe.wait_ge(sem("y_ready"), i // 2 + 1)
                pe.wait_ge(d_lo_made, RAW_D + n + 1)
                whi, wlo = [w[:, n % CUT, :].rearrange("p (k n) -> p k n", k=2) for w in (w_hi, w_lo)]
                ts_ = slice(t * P, (t + 1) * P)
                for h in range(2):
                    cs = slice(512 * h, 512 * h + 512)
                    out_ap = ps[:, 4 + 2 * t + h, :]
                    for kk in range(2):
                        k = 2 * i + kk
                        mm(out_ap, y_hi[:, k, ts_], whi[:, kk, cs], start=k == 0, stop=False)
                        mm(out_ap, y_hi[:, k, ts_], wlo[:, kk, cs], start=False, stop=False)
                        last = mm(out_ap, y_lo(k)[:, ts_], whi[:, kk, cs], start=False, stop=k == NX - 1)
                return last

            for i in range(N_OUT - CUT):
                y_out(i, 0)
                y_out(i, 1).then_inc(d_piece_used, 1)
            for i in range(N_OUT - CUT, N_OUT):
                last = y_out(i, 0)
            last.then_inc(sem("out_tile"), 1)
            for i in range(N_OUT - CUT, N_OUT):
                y_out(i, 1).then_inc(d_piece_used, 1)
            pe.sem_inc(piece_used, CUT)
            for t in range(TT):
                turn_tile(3, t)
                if limit < 5:
                    continue
                pe.wait_ge(sem("xT_copied"), 2 * t + 2)
                token_major(ps[:, 4, t * E:(t + 1) * E], w_rt, t).then_inc(sem("logits"), 1)
            if limit < 5:
                return
            pe.wait_ge(sem("sel_made"), 1)
            mm(ps[:, 4, 32:32 + E], tris, sel[:, 0, :], start=True, stop=True)
            mm(ps[:, 4, 40:40 + E], tris, sel[:, 1, :], start=True, stop=False)
            mm(ps[:, 4, 40:40 + E], ones[:, :], sel[:, 0, :], start=False, stop=True)
            mm(ps[:, 4, 64:64 + E], ones[:, :], sel[:, 0, :], start=True, stop=False)
            mm(ps[:, 4, 64:64 + E], ones[:, :], sel[:, 1, :], start=False, stop=True).then_inc(sem("ranks"), 1)

            def gather(it):
                pe.wait_ge(sem("sel_rows_made"), it + 1)
                for q in range(2):
                    for k in range(4):
                        c = 4 * q + k
                        for t in range(TT):
                            last = mm(ps[:, 2 + q, k * P:(k + 1) * P], x_tok[:, t, c * P:(c + 1) * P], sel_rows[:, t, :],
                                      start=t == 0, stop=t == TT - 1)
                    last.then_inc(sem("xg_made"), 1)

            def expert_pe(it, following):
                pe.wait_ge(sem("e_h"), ESTEPS * it + FIRST)
                pe.wait_ge(sem("xg_lo_made"), 2 * it + 2)

                def three(out_ap, hi, lo, whi, wlo, start, stop):
                    mm(out_ap, hi, whi, start=start, stop=False)
                    mm(out_ap, hi, wlo, start=False, stop=False)
                    return mm(out_ap, lo, whi, start=False, stop=stop)

                def pieces(n, k):
                    return [w[:, n % CUT, :].rearrange("p (k n) -> p k n", k=k) for w in (w_hi, w_lo)]

                def product(j, what):
                    for half in range(PPU):
                        n = PPU * ORDER.index((j, what)) + half
                        pe.wait_ge(lo_made, PPE * it + (RAW + n + 1))
                        whi, wlo = pieces(n, 4)
                        for kk in range(4):
                            k = 4 * half + kk
                            last = three(ps[:, 2 * (j % 2) + what, :], xg_hi[:, k, :], xg_lo[:, k, :], whi[:, kk, :], wlo[:, kk, :],
                                         k == 0, k == KD - 1)
                        last.then_inc(piece_used, 1)

                def turn_h(j):
                    pe.wait_ge(sem("e_h"), ESTEPS * it + (j + 1) + FIRST)
                    pe.wait_ge(sem("ehT_made"), ESTEPS * it + j + FIRST)
                    for c in range(4):
                        last = pe.transpose(ps[:, 4, c * P:(c + 1) * P], eh[:, j % 2, c * P:(c + 1) * P], ident)
                    last.then_inc(sem("eh_turned"), 1)

                def down(j):
                    pe.wait_ge(sem("ehT_made"), ESTEPS * it + (j + 1) + FIRST)
                    for half in range(PPU):
                        n = PPU * ORDER.index((j, 2)) + half
                        pe.wait_ge(lo_made, PPE * it + (RAW + n + 1))
                        whi, wlo = pieces(n, 2)
                        for cc in range(2):
                            c = 2 * half + cc
                            for h in range(2):
                                cs = slice(512 * h, 512 * h + 512)
                                last = three(ps[:, 5 + h, :], ehT_hi[:, j % 2, c, :], ehT_lo[:, j % 2, c, :], whi[:, cc, cs],
                                             wlo[:, cc, cs], j == 0 and c == 0, j == ESTEPS - 1 and c == 3)
                        last.then_inc(piece_used, 1)

                for j in range(ESTEPS):
                    if j >= 2:
                        pe.wait_ge(sem("e_h"), ESTEPS * it + (j - 1) + FIRST)
                    product(j, 0)
                    if j:
                        turn_h(j - 1)
                    else:
                        pe.wait_ge(sem("e_added"), 4 * it + FIRST)
                        pe.wait_ge(sem("sel_gate_made"), it + 1)
                        for t in range(TT):
                            last = pe.transpose(ps[:, 7, t * P:(t + 1) * P], sel_gate[:, t, :], ident)
                        last.then_inc(sem("G_turned"), 1)
                    product(j, 1)
                    if j == ESTEPS - 1 and following is not None:
                        pe.wait_ge(sem("e_h"), ESTEPS * it + j + FIRST)
                        gather(following)
                    if j:
                        down(j - 1)
                turn_h(ESTEPS - 1)
                down(ESTEPS - 1)
                pe.wait_ge(sem("G_copied"), it + 1)
                pe.wait_ge(sem("oe_copied_dve"), it + 1)
                pe.wait_ge(sem("oe_copied_act"), it + 1)
                for q in range(2 * TT):
                    if q >= 2:
                        pe.wait_ge(sem("e_added"), 4 * it + (q - 1) + FIRST)
                    mm(ps[:, 7 if q % 2 == 0 else 4, :], G[:, q // 2, :], oe[:, 512 * (q % 2):512 * (q % 2) + 512], start=True, stop=True
                       ).then_inc(sem("e_scattered"), 1)

            pe.sem_inc(sem("xg_made"), FIRST)
            pe.sem_inc(sem("e_scattered"), FIRST)
            gather(0)
            with pe.Fori(0, E - 1) as e:
                expert_pe(e, e + 1)
            expert_pe(E - 1, None)
            more = pe.value_load(over[0:1, 0:1].bitcast(I32), min_val=0, max_val=SEQ)
            with pe.If(more > 0):
                with pe.Fori(0, E) as e:
                    pe.wait_ge(sem("e_h"), ESTEPS * e + ESTEPS * E + FIRST)
                    gather(e + E)
                    expert_pe(e + E, None)


_INS = ["x", "ln_g", "ln_b", "even_w_in", "swa_sinks", "dn_conv_w", "dn_a_log", "dn_dt_bias", "dn_norm_w", "even_w_out",
        "ssm_w_in", "ssm_conv_w", "ssm_conv_b", "ssm_dt_bias", "ssm_a_log", "ssm_d", "ssm_norm_w", "ssm_w_out",
        "ffn_w_gate", "ffn_w_up", "ffn_w_down", "moe_w_router", "moe_b_router", "moe_w_gate", "moe_w_up", "moe_w_down"]


def kernel(**inputs):
    import ml_dtypes
    from concourse import bacc
    from concourse.bass_utils import run_bass_kernel_spmd

    nc = bacc.Bacc("TRN2", target_bir_lowering=False, num_devices=1)
    arrays = {name: np.ascontiguousarray(inputs[name]) for name in _INS}
    arrays["shape_consts"] = shape_constants()
    arrays["shape_consts_b"] = shape_constants_b(ml_dtypes.bfloat16)
    dram = {}
    for name, a in arrays.items():
        dram[name] = nc.dram_tensor(f"in_{name}", a.shape, mybir.dt.from_np(a.dtype), kind="ExternalInput").ap()
    out = nc.dram_tensor("out", (1, SEQ, D), F32, kind="ExternalOutput").ap()
    build(nc, dram, out)
    r = run_bass_kernel_spmd(nc, [{f"in_{name}": a for name, a in arrays.items()}], core_ids=[0])
    return r.results[0]["out"]
```
